# Optimizing a Trainium2 kernel written in Bass

```python
import jax, jax.numpy as jnp
from jax import lax
import numpy as np
import math

D_MODEL = 1024
BATCH = 1
SEQ = 256
DEPTH = 1

MLA_HEADS = 8
MLA_NOPE = 64
MLA_ROPE = 32
MLA_V = 64
MLA_QK = MLA_NOPE + MLA_ROPE
MLA_Q_RANK = 256
MLA_KV_RANK = 128
RET_HEADS = 4
RET_DK = 64
RET_DV = 128
CHUNK = 128
Q_BLOCK = 128
D_FF = 4 * D_MODEL
ROPE_BASE = 10000.0
EPS = 1e-5
MLA_WIDTH = MLA_HEADS * MLA_V
RET_WIDTH = RET_HEADS * RET_DV
MIX_WIDTH = MLA_WIDTH + RET_WIDTH
ALPHA = (2.0 * DEPTH) ** 0.25
BETA = (8.0 * DEPTH) ** -0.25
IN_SPLITS = (MLA_Q_RANK, MLA_KV_RANK, MLA_ROPE,
             RET_HEADS * RET_DK, RET_HEADS * RET_DK, RET_WIDTH, RET_WIDTH)
IN_WIDTH = sum(IN_SPLITS)
IN_OFFSETS = tuple(int(v) for v in np.cumsum(IN_SPLITS)[:-1])


def layer_norm(x, g, b):
    xf = x.astype(jnp.float32)
    mu = jnp.mean(xf, -1, keepdims=True)
    var = jnp.mean(jnp.square(xf - mu), -1, keepdims=True)
    return ((xf - mu) * lax.rsqrt(var + EPS) * g.astype(jnp.float32) + b.astype(jnp.float32)).astype(x.dtype)

def rms_norm(x, g):
    xf = x.astype(jnp.float32)
    ms = jnp.mean(jnp.square(xf), -1, keepdims=True)
    return (xf * lax.rsqrt(ms + EPS) * g.astype(jnp.float32)).astype(x.dtype)

def rotary(x, pos):
    half = x.shape[-1] // 2
    inv = ROPE_BASE ** (-jnp.arange(half, dtype=jnp.float32) / half)
    ang = pos.astype(jnp.float32)[..., None] * inv
    cos = jnp.cos(ang)[:, :, None, :]
    sin = jnp.sin(ang)[:, :, None, :]
    x1 = x[..., :half].astype(jnp.float32)
    x2 = x[..., half:].astype(jnp.float32)
    return jnp.concatenate([x1 * cos - x2 * sin, x2 * cos + x1 * sin], -1).astype(x.dtype)

def causal_block_attention(q, k, v):
    b, s, h, dq = q.shape
    dv = v.shape[-1]
    nb = s // Q_BLOCK
    scale = dq ** -0.5
    qb = q.reshape(b, nb, Q_BLOCK, h, dq).transpose(1, 0, 3, 2, 4)
    kt = k.transpose(0, 2, 1, 3)
    vt = v.transpose(0, 2, 1, 3)
    k_idx = jnp.arange(s)

    def one_block(args):
        q_blk, i = args
        sc = jnp.einsum('bhqd,bhkd->bhqk', q_blk, kt,
                        preferred_element_type=jnp.float32) * scale
        q_idx = i * Q_BLOCK + jnp.arange(Q_BLOCK)
        mask = k_idx[None, :] <= q_idx[:, None]
        p = jax.nn.softmax(jnp.where(mask, sc, -jnp.inf), axis=-1)
        return jnp.einsum('bhqk,bhkd->bhqd', p.astype(vt.dtype), vt)

    out = lax.map(one_block, (qb, jnp.arange(nb)))
    return out.transpose(1, 0, 3, 2, 4).reshape(b, s, h * dv)

def mla_mixer(q_c, kv_c, k_r, pos, g_q, w_uq, g_kv, w_ukv):
    b, s, _ = q_c.shape
    q = (rms_norm(q_c, g_q) @ w_uq).reshape(b, s, MLA_HEADS, MLA_QK)
    q = jnp.concatenate([q[..., :MLA_NOPE], rotary(q[..., MLA_NOPE:], pos)], -1)
    kv = (rms_norm(kv_c, g_kv) @ w_ukv).reshape(b, s, MLA_HEADS, MLA_NOPE + MLA_V)
    k_nope, v = kv[..., :MLA_NOPE], kv[..., MLA_NOPE:]
    k_rope = rotary(k_r[:, :, None, :], pos)
    k = jnp.concatenate([k_nope, jnp.broadcast_to(k_rope, (b, s, MLA_HEADS, MLA_ROPE))], -1)
    return causal_block_attention(q, k, v)

def retention_mixer(q, k, v, g, pos, gn_g, gn_b):
    b, s, _ = q.shape
    n = s // CHUNK
    q = rotary(q.reshape(b, s, RET_HEADS, RET_DK), pos)
    k = rotary(k.reshape(b, s, RET_HEADS, RET_DK), pos) * (RET_DK ** -0.5)
    v = v.reshape(b, s, RET_HEADS, RET_DV)
    qc = q.reshape(b, n, CHUNK, RET_HEADS, RET_DK).transpose(0, 3, 1, 2, 4)
    kc = k.reshape(b, n, CHUNK, RET_HEADS, RET_DK).transpose(0, 3, 1, 2, 4)
    vc = v.reshape(b, n, CHUNK, RET_HEADS, RET_DV).transpose(0, 3, 1, 2, 4)

    log_g = jnp.log(1.0 - 2.0 ** (-5.0 - jnp.arange(RET_HEADS, dtype=jnp.float32)))
    idx = jnp.arange(CHUNK, dtype=jnp.float32)
    diff = idx[:, None] - idx[None, :]
    decay = jnp.where(diff >= 0, jnp.exp(log_g[:, None, None] * jnp.maximum(diff, 0.0)), 0.0)
    zeta = jnp.exp(log_g[:, None] * (CHUNK - 1 - idx))
    xi = jnp.exp(log_g[:, None] * (idx + 1.0))

    scores = jnp.einsum('bhnid,bhnjd->bhnij', qc, kc) * decay[None, :, None]
    inner = jnp.einsum('bhnij,bhnjv->bhniv', scores, vc)
    chunk_kv = jnp.einsum('bhnjd,hj,bhnjv->bhndv', kc, zeta, vc)
    g_chunk = jnp.exp(log_g * CHUNK).astype(chunk_kv.dtype)[None, :, None, None]

    def step(state, kv_n):
        return state * g_chunk + kv_n, state

    init = jnp.zeros((b, RET_HEADS, RET_DK, RET_DV), chunk_kv.dtype)
    _, prev = lax.scan(step, init, chunk_kv.transpose(2, 0, 1, 3, 4))
    prev = prev.transpose(1, 2, 0, 3, 4)
    cross = jnp.einsum('bhnid,bhndv->bhniv', qc, prev) * xi[None, :, None, :, None]

    o = (inner + cross).transpose(0, 2, 3, 1, 4).reshape(b, s, RET_HEADS, RET_DV)
    of = o.astype(jnp.float32)
    mu = jnp.mean(of, -1, keepdims=True)
    var = jnp.mean(jnp.square(of - mu), -1, keepdims=True)
    on = ((of - mu) * lax.rsqrt(var + EPS)).reshape(b, s, RET_WIDTH)
    on = on * gn_g.astype(jnp.float32) + gn_b.astype(jnp.float32)
    return (on * jax.nn.silu(g.astype(jnp.float32))).astype(g.dtype)

def first_inputs(seed: int = 0) -> dict:
    key = jax.random.key(seed)
    ks = jax.random.split(key, 24)
    f32 = jnp.float32
    nrm = lambda k, shape, fan: jax.random.normal(k, shape, f32) * (fan ** -0.5)
    gain = lambda k, shape: 1.0 + 0.05 * jax.random.normal(k, shape, f32)
    bias = lambda k, shape: 0.02 * jax.random.normal(k, shape, f32)

    x = jax.random.normal(ks[0], (BATCH, SEQ, D_MODEL), f32)
    c = jax.random.normal(ks[1], (BATCH, D_MODEL), f32)
    offset = jax.random.randint(ks[2], (BATCH, 1), 0, 1024, dtype=jnp.int32)
    positions = (offset + jnp.arange(SEQ, dtype=jnp.int32)[None, :]).astype(jnp.int32)

    in_col_scale = jnp.concatenate([
        jnp.ones((IN_WIDTH - 2 * RET_WIDTH,), f32),
        jnp.full((RET_WIDTH,), BETA, f32),
        jnp.ones((RET_WIDTH,), f32)])
    ukv_col_scale = jnp.tile(jnp.concatenate([jnp.ones((MLA_NOPE,), f32),
                                              jnp.full((MLA_V,), BETA, f32)]), MLA_HEADS)
    return {
        "x": x,
        "c": c,
        "positions": positions,
        "ln_in_g": gain(ks[3], (D_MODEL,)),
        "ln_in_b": bias(ks[4], (D_MODEL,)),
        "w_ada": nrm(ks[5], (DEPTH, D_MODEL, 6 * D_MODEL), D_MODEL) * 0.5,
        "b_ada": bias(ks[6], (DEPTH, 6 * D_MODEL)),
        "w_in": nrm(ks[7], (DEPTH, D_MODEL, IN_WIDTH), D_MODEL) * in_col_scale,
        "mla_q_norm": gain(ks[8], (DEPTH, MLA_Q_RANK)),
        "w_uq": nrm(ks[9], (DEPTH, MLA_Q_RANK, MLA_HEADS * MLA_QK), MLA_Q_RANK),
        "mla_kv_norm": gain(ks[10], (DEPTH, MLA_KV_RANK)),
        "w_ukv": nrm(ks[11], (DEPTH, MLA_KV_RANK, MLA_HEADS * (MLA_NOPE + MLA_V)), MLA_KV_RANK) * ukv_col_scale,
        "ret_gn_g": gain(ks[12], (DEPTH, RET_WIDTH)),
        "ret_gn_b": bias(ks[13], (DEPTH, RET_WIDTH)),
        "w_out": nrm(ks[14], (DEPTH, MIX_WIDTH, D_MODEL), MIX_WIDTH) * BETA,
        "ln1_g": gain(ks[15], (DEPTH, D_MODEL)),
        "ln1_b": bias(ks[16], (DEPTH, D_MODEL)),
        "w_ff1": nrm(ks[17], (DEPTH, D_MODEL, D_FF), D_MODEL) * BETA,
        "w_ff2": nrm(ks[18], (DEPTH, D_FF, D_MODEL), D_FF) * BETA,
        "ln2_g": gain(ks[19], (DEPTH, D_MODEL)),
        "ln2_b": bias(ks[20], (DEPTH, D_MODEL)),
    }

def first_block(x, c, positions, ln_in_g, ln_in_b, w_ada, b_ada, w_in, mla_q_norm, w_uq,
              mla_kv_norm, w_ukv, ret_gn_g, ret_gn_b, w_out, ln1_g, ln1_b,
              w_ff1, w_ff2, ln2_g, ln2_b):
    x = layer_norm(x, ln_in_g, ln_in_b)
    c_act = jax.nn.silu(c)
    for l in range(DEPTH):
        mod = c_act @ w_ada[l] + b_ada[l]
        sh1, sc1, gt1, sh2, sc2, gt2 = [m[:, None, :] for m in jnp.split(mod, 6, axis=-1)]

        h = x * (1.0 + sc1) + sh1
        proj = h @ w_in[l]
        q_c, kv_c, k_r, r_q, r_k, r_v, r_g = jnp.split(proj, IN_OFFSETS, axis=-1)
        a = mla_mixer(q_c, kv_c, k_r, positions, mla_q_norm[l], w_uq[l], mla_kv_norm[l], w_ukv[l])
        r = retention_mixer(r_q, r_k, r_v, r_g, positions, ret_gn_g[l], ret_gn_b[l])
        y = jnp.concatenate([a, r], axis=-1) @ w_out[l]
        x = layer_norm(ALPHA * x + gt1 * y, ln1_g[l], ln1_b[l])

        h = x * (1.0 + sc2) + sh2
        f = jnp.square(jax.nn.relu(h @ w_ff1[l])) @ w_ff2[l]
        x = layer_norm(ALPHA * x + gt2 * f, ln2_g[l], ln2_b[l])
    return x


N_META = 16
DN_HEADS = 4
DN_HEAD_DIM = 128
DN_WIDTH = DN_HEADS * DN_HEAD_DIM
DN_CONV = 4
DN_CHUNK = 64
SB_HEADS = 8
SB_HEAD_DIM = 64
SB_WIDTH = SB_HEADS * SB_HEAD_DIM
SB_BLOCK = 128
N_BRANCH = 2
IN_COLS = 4 * DN_WIDTH + 2 * DN_HEADS + 3 * SB_WIDTH + N_BRANCH * D_MODEL
SPLIT_POINTS = [3 * DN_WIDTH, 4 * DN_WIDTH, 4 * DN_WIDTH + DN_HEADS, 4 * DN_WIDTH + 2 * DN_HEADS,
                4 * DN_WIDTH + 2 * DN_HEADS + 3 * SB_WIDTH]
COL_DN_V0 = 2 * DN_WIDTH
COL_SB_V0 = 4 * DN_WIDTH + 2 * DN_HEADS + 2 * SB_WIDTH
N_GROUPS = 4
EXPERTS_PER_GROUP = 8
TOP_K_IN_GROUP = 2
EXPERT_FF = 256
DEEPNORM_ALPHA = (2.0 * DEPTH) ** 0.25
DEEPNORM_BETA = (8.0 * DEPTH) ** -0.25
LN_EPS = 1e-5
RMS_EPS = 1e-6


def layer_norm_2(x, g, b):
    xf = x.astype(jnp.float32)
    mu = jnp.mean(xf, -1, keepdims=True)
    var = jnp.mean(jnp.square(xf - mu), -1, keepdims=True)
    return ((xf - mu) * lax.rsqrt(var + LN_EPS) * g.astype(jnp.float32) + b.astype(jnp.float32)).astype(x.dtype)

def rms_norm_2(x, g):
    xf = x.astype(jnp.float32)
    return xf * lax.rsqrt(jnp.mean(xf * xf, -1, keepdims=True) + RMS_EPS) * g.astype(jnp.float32)

def l2_normalize(x):
    xf = x.astype(jnp.float32)
    return xf * lax.rsqrt(jnp.sum(xf * xf, -1, keepdims=True) + RMS_EPS)

def split_heads(t, n):
    b, l, _ = t.shape
    return t.reshape(b, l, n, -1).transpose(0, 2, 1, 3)

def merge_heads(t):
    b, h, l, d = t.shape
    return t.transpose(0, 2, 1, 3).reshape(b, l, h * d)

def causal_depthwise_conv(x, w):
    c = x.shape[-1]
    return lax.conv_general_dilated(x, w[:, None, :], window_strides=(1,), padding=[(w.shape[0] - 1, 0)],
                                    dimension_numbers=("NWC", "WIO", "NWC"), feature_group_count=c)

def gated_delta_rule_chunked(q, k, v, beta, g):
    b, h, l, dk = q.shape
    dv = v.shape[-1]
    c = DN_CHUNK
    n = l // c
    q = q.reshape(b, h, n, c, dk)
    k = k.reshape(b, h, n, c, dk)
    v = v.reshape(b, h, n, c, dv)
    beta = beta.reshape(b, h, n, c)
    decay = jnp.cumsum(g.reshape(b, h, n, c), axis=-1)
    idx = jnp.arange(c)
    causal = idx[:, None] >= idx[None, :]
    strict = idx[:, None] > idx[None, :]
    diff = decay[..., :, None] - decay[..., None, :]
    lmask = jnp.where(causal, jnp.exp(jnp.where(causal, diff, 0.0)), 0.0)
    k_beta = k * beta[..., None]
    v_beta = v * beta[..., None]
    a = jnp.where(strict, jnp.einsum("bhnid,bhnjd->bhnij", k_beta, k) * lmask, 0.0)
    m = a + jnp.eye(c, dtype=a.dtype)
    u = lax.linalg.triangular_solve(m, v_beta, left_side=True, lower=True, unit_diagonal=True)
    w = lax.linalg.triangular_solve(m, k_beta * jnp.exp(decay)[..., None], left_side=True, lower=True,
                                    unit_diagonal=True)
    qk = jnp.where(causal, jnp.einsum("bhnid,bhnjd->bhnij", q, k) * lmask, 0.0)
    q_dec = q * jnp.exp(decay)[..., None]
    k_dec = k * jnp.exp(decay[..., -1:] - decay)[..., None]
    chunk_decay = jnp.exp(decay[..., -1])
    xs = tuple(jnp.moveaxis(t, 2, 0) for t in (q_dec, k_dec, u, w, qk, chunk_decay))

    def step(state, inp):
        qd, kd, uc, wc, qkc, cd = inp
        v_new = uc - jnp.einsum("bhcd,bhde->bhce", wc, state)
        o = jnp.einsum("bhcd,bhde->bhce", qd, state) + jnp.einsum("bhij,bhje->bhie", qkc, v_new)
        state = state * cd[..., None, None] + jnp.einsum("bhcd,bhce->bhde", kd, v_new)
        return state, o

    s0 = jnp.zeros((b, h, dk, dv), jnp.float32)
    _, o = lax.scan(step, s0, xs)
    return jnp.moveaxis(o, 0, 2).reshape(b, h, l, dv)

def stick_breaking_attention(q, k, v):
    l = q.shape[2]
    scale = q.shape[-1] ** -0.5
    bounds = [0] + list(range(N_META, l, SB_BLOCK)) + [l]
    outs = []
    for s0, s1 in zip(bounds[:-1], bounds[1:]):
        z = jnp.einsum("bhqd,bhkd->bhqk", q[:, :, s0:s1], k[:, :, :s1]).astype(jnp.float32) * scale
        mask = jnp.arange(s1)[None, :] < jnp.arange(s0, s1)[:, None]
        log_keep = jnp.where(mask, jax.nn.log_sigmoid(-z), 0.0)
        later = lax.cumsum(log_keep, axis=3, reverse=True) - log_keep
        weights = jnp.where(mask, jnp.exp(jax.nn.log_sigmoid(z) + later), 0.0)
        outs.append(jnp.einsum("bhqk,bhkd->bhqd", weights.astype(v.dtype), v[:, :, :s1]))
    return jnp.concatenate(outs, axis=2)

def hybrid_mixer(x, w_in, b_gate, dn_conv_w, dn_a_log, dn_dt_bias, dn_norm_g, w_branch_dn, w_branch_sb, w_out):
    b, l, d = x.shape
    proj = x @ w_in
    dn_qkv, dn_z, dn_b, dn_a, sb_qkv, gates = jnp.split(proj, SPLIT_POINTS, axis=-1)
    dn_qkv = jax.nn.silu(causal_depthwise_conv(dn_qkv, dn_conv_w))
    q, k, v = jnp.split(dn_qkv, 3, axis=-1)
    q = l2_normalize(split_heads(q, DN_HEADS)) * (DN_HEAD_DIM ** -0.5)
    k = l2_normalize(split_heads(k, DN_HEADS))
    v = split_heads(v, DN_HEADS).astype(jnp.float32)
    beta = jax.nn.sigmoid(dn_b.astype(jnp.float32)).transpose(0, 2, 1)
    g = (-jnp.exp(dn_a_log.astype(jnp.float32))
         * jax.nn.softplus(dn_a.astype(jnp.float32) + dn_dt_bias.astype(jnp.float32))).transpose(0, 2, 1)
    pad = (DN_CHUNK - N_META % DN_CHUNK) % DN_CHUNK
    front = lambda t: jnp.pad(t, [(0, 0), (0, 0), (pad, 0)] + [(0, 0)] * (t.ndim - 3))
    o_dn = gated_delta_rule_chunked(front(q), front(k), front(v), front(beta), front(g))[:, :, pad:]
    o_dn = merge_heads(rms_norm_2(o_dn, dn_norm_g)) * jax.nn.silu(dn_z.astype(jnp.float32))
    sq, sk, sv = (split_heads(t, SB_HEADS) for t in jnp.split(sb_qkv, 3, axis=-1))
    o_sb = merge_heads(stick_breaking_attention(sq, sk, sv))
    gate = jax.nn.sigmoid(gates.reshape(b, l, N_BRANCH, d) + b_gate)
    merged = (gate[:, :, 0] * (o_dn.astype(x.dtype) @ w_branch_dn)
              + gate[:, :, 1] * (o_sb.astype(x.dtype) @ w_branch_sb))
    return merged @ w_out

def hierarchical_moe(h, router_group_w, router_group_b, router_expert_w, router_expert_b,
                     expert_w_gate, expert_w_up, expert_w_down):
    b, l, d = h.shape
    t = h.reshape(b * l, d)
    group_probs = jax.nn.softmax((t @ router_group_w).astype(jnp.float32) + router_group_b, axis=-1)
    g_idx = jnp.argmax(group_probs, axis=-1)
    g_prob = jnp.max(group_probs, axis=-1)
    exp_logits = jnp.einsum("td,gde->tge", t, router_expert_w).astype(jnp.float32) + router_expert_b
    sel_logits = jnp.take_along_axis(exp_logits, g_idx[:, None, None], axis=1)[:, 0]
    top_logit, top_idx = lax.top_k(sel_logits, TOP_K_IN_GROUP)
    top_w = jax.nn.softmax(top_logit, axis=-1) * g_prob[:, None]
    combine_e = jnp.sum(jax.nn.one_hot(top_idx, EXPERTS_PER_GROUP) * top_w[..., None], axis=1)
    combine = jax.nn.one_hot(g_idx, N_GROUPS)[:, :, None] * combine_e[:, None, :]
    y = jnp.zeros_like(t)
    for gi in range(N_GROUPS):
        hid = (jax.nn.silu(jnp.einsum("td,edf->tef", t, expert_w_gate[gi]))
               * jnp.einsum("td,edf->tef", t, expert_w_up[gi]))
        hid = hid * combine[:, gi, :, None].astype(hid.dtype)
        y = y + jnp.einsum("tef,efd->td", hid, expert_w_down[gi])
    return y.reshape(b, l, d)

def second_inputs(seed: int = 0) -> dict:
    key = jax.random.key(seed)
    ks = jax.random.split(key, 24)
    f32 = jnp.float32
    nrm = lambda k, shape, scale: jax.random.normal(k, shape, f32) * scale
    col_scale = np.ones((IN_COLS,), np.float32)
    col_scale[COL_DN_V0:COL_DN_V0 + DN_WIDTH] = DEEPNORM_BETA
    col_scale[COL_SB_V0:COL_SB_V0 + SB_WIDTH] = DEEPNORM_BETA
    dt = jnp.exp(jax.random.uniform(ks[6], (DEPTH, DN_HEADS), f32, math.log(1e-3), math.log(1e-1)))
    return {
        "x": nrm(ks[0], (BATCH, SEQ, D_MODEL), 1.0),
        "meta_tokens": nrm(ks[1], (N_META, D_MODEL), 1.0),
        "ln_emb_g": 1.0 + nrm(ks[2], (D_MODEL,), 0.05),
        "ln_emb_b": nrm(ks[3], (D_MODEL,), 0.02),
        "w_in": nrm(ks[4], (DEPTH, D_MODEL, IN_COLS), D_MODEL ** -0.5) * jnp.asarray(col_scale),
        "b_gate": nrm(ks[5], (DEPTH, N_BRANCH, D_MODEL), 0.02),
        "dn_conv_w": nrm(ks[7], (DEPTH, DN_CONV, 3 * DN_WIDTH), DN_CONV ** -0.5),
        "dn_a_log": jnp.log(jax.random.uniform(ks[8], (DEPTH, DN_HEADS), f32, 1.0, 16.0)),
        "dn_dt_bias": jnp.log(jnp.expm1(dt)),
        "dn_norm_g": 1.0 + nrm(ks[9], (DEPTH, DN_HEAD_DIM), 0.05),
        "w_branch_dn": nrm(ks[10], (DEPTH, DN_WIDTH, D_MODEL), DEEPNORM_BETA * DN_WIDTH ** -0.5),
        "w_branch_sb": nrm(ks[11], (DEPTH, SB_WIDTH, D_MODEL), DEEPNORM_BETA * SB_WIDTH ** -0.5),
        "w_out": nrm(ks[12], (DEPTH, D_MODEL, D_MODEL), DEEPNORM_BETA * D_MODEL ** -0.5),
        "ln1_g": 1.0 + nrm(ks[13], (DEPTH, D_MODEL), 0.05),
        "ln1_b": nrm(ks[14], (DEPTH, D_MODEL), 0.02),
        "router_group_w": nrm(ks[15], (DEPTH, D_MODEL, N_GROUPS), D_MODEL ** -0.5),
        "router_group_b": nrm(ks[16], (DEPTH, N_GROUPS), 0.01),
        "router_expert_w": nrm(ks[17], (DEPTH, N_GROUPS, D_MODEL, EXPERTS_PER_GROUP), D_MODEL ** -0.5),
        "router_expert_b": nrm(ks[18], (DEPTH, N_GROUPS, EXPERTS_PER_GROUP), 0.01),
        "expert_w_gate": nrm(ks[19], (DEPTH, N_GROUPS, EXPERTS_PER_GROUP, D_MODEL, EXPERT_FF), D_MODEL ** -0.5),
        "expert_w_up": nrm(ks[20], (DEPTH, N_GROUPS, EXPERTS_PER_GROUP, D_MODEL, EXPERT_FF),
                           DEEPNORM_BETA * D_MODEL ** -0.5),
        "expert_w_down": nrm(ks[21], (DEPTH, N_GROUPS, EXPERTS_PER_GROUP, EXPERT_FF, D_MODEL),
                             DEEPNORM_BETA * EXPERT_FF ** -0.5),
        "ln2_g": 1.0 + nrm(ks[22], (DEPTH, D_MODEL), 0.05),
        "ln2_b": nrm(ks[23], (DEPTH, D_MODEL), 0.02),
    }

def second_block(x, meta_tokens, ln_emb_g, ln_emb_b, w_in, b_gate, dn_conv_w, dn_a_log, dn_dt_bias, dn_norm_g,
              w_branch_dn, w_branch_sb, w_out, ln1_g, ln1_b, router_group_w, router_group_b, router_expert_w,
              router_expert_b, expert_w_gate, expert_w_up, expert_w_down, ln2_g, ln2_b):
    b = x.shape[0]
    meta = jnp.broadcast_to(meta_tokens[None].astype(x.dtype), (b, N_META, x.shape[-1]))
    h = layer_norm_2(jnp.concatenate([meta, x], axis=1), ln_emb_g, ln_emb_b)
    for i in range(DEPTH):
        mix = hybrid_mixer(h, w_in[i], b_gate[i], dn_conv_w[i], dn_a_log[i], dn_dt_bias[i], dn_norm_g[i],
                           w_branch_dn[i], w_branch_sb[i], w_out[i])
        h = layer_norm_2(DEEPNORM_ALPHA * h + mix, ln1_g[i], ln1_b[i])
        ffn = hierarchical_moe(h, router_group_w[i], router_group_b[i], router_expert_w[i], router_expert_b[i],
                               expert_w_gate[i], expert_w_up[i], expert_w_down[i])
        h = layer_norm_2(DEEPNORM_ALPHA * h + ffn, ln2_g[i], ln2_b[i])
    return h[:, N_META:]


def setup_inputs(seed=0):
    out = dict(first_inputs(seed))
    for name, value in second_inputs(seed + 1).items():
        if name != "x":
            out[name + "_2"] = value
    return out


def reference(
    x, c, positions, ln_in_g, ln_in_b, w_ada, b_ada, w_in, mla_q_norm, w_uq, mla_kv_norm, w_ukv,
    ret_gn_g, ret_gn_b, w_out, ln1_g, ln1_b, w_ff1, w_ff2, ln2_g, ln2_b, meta_tokens_2,
    ln_emb_g_2, ln_emb_b_2, w_in_2, b_gate_2, dn_conv_w_2, dn_a_log_2, dn_dt_bias_2,
    dn_norm_g_2, w_branch_dn_2, w_branch_sb_2, w_out_2, ln1_g_2, ln1_b_2, router_group_w_2,
    router_group_b_2, router_expert_w_2, router_expert_b_2, expert_w_gate_2, expert_w_up_2,
    expert_w_down_2, ln2_g_2, ln2_b_2,
):
    x = first_block(
        x, c, positions, ln_in_g, ln_in_b, w_ada, b_ada, w_in, mla_q_norm, w_uq, mla_kv_norm,
        w_ukv, ret_gn_g, ret_gn_b, w_out, ln1_g, ln1_b, w_ff1, w_ff2, ln2_g, ln2_b,
    )
    return second_block(
        x, meta_tokens_2, ln_emb_g_2, ln_emb_b_2, w_in_2, b_gate_2, dn_conv_w_2, dn_a_log_2,
        dn_dt_bias_2, dn_norm_g_2, w_branch_dn_2, w_branch_sb_2, w_out_2, ln1_g_2, ln1_b_2,
        router_group_w_2, router_group_b_2, router_expert_w_2, router_expert_b_2,
        expert_w_gate_2, expert_w_up_2, expert_w_down_2, ln2_g_2, ln2_b_2,
    )


_drawn_inputs = setup_inputs


def setup_inputs(seed=0):
    import zlib

    import numpy as np

    out = dict(_drawn_inputs(seed))
    spreads = {}
    factors = {'b_ada': 5.507,
     'mla_q_norm': 8.0,
     'w_uq': 5.159,
     'mla_kv_norm': 8.0,
     'ret_gn_g': 8.0,
     'ret_gn_b': 33.669,
     'ln2_b': 2.765,
     'meta_tokens_2': 4.302,
     'b_gate_2': 8.0,
     'dn_a_log_2': 4.862,
     'dn_norm_g_2': 8.0,
     'ln1_b_2': 2.687,
     'router_group_b_2': 28.537,
     'router_expert_b_2': 32.023,
     'ln2_b_2': 2.852}
    for name, (base, spread) in spreads.items():
        noise = np.random.default_rng([zlib.crc32(name.encode()), seed]).standard_normal(out[name].shape)
        drawn = base * np.exp(spread * noise) if base else spread * noise
        out[name] = __import__('jax').numpy.asarray(drawn.astype(out[name].dtype))
    for name, factor in factors.items():
        out[name] = (out[name] * factor).astype(out[name].dtype)
    return out
```

```python
from collections import namedtuple
from contextlib import ExitStack

import numpy as np
import concourse.bass as bass
from concourse import mybir

ALU = mybir.AluOpType
ACT = mybir.ActivationFunctionType
AX = mybir.AxisListType.X
F32 = mybir.dt.float32
I32 = mybir.dt.int32

P = 128
DM = 1024
KD = DM // P
T = 2
NT = T * P
EPS = 1e-5
ALPHA = 2.0 ** 0.25
NEG = -1.0e30

QR, KVR, ROPE = 256, 128, 32
MH, NOPE, MV = 8, 64, 64
QK = NOPE + ROPE
RH, RDK, RDV = 4, 64, 128
FF = 4096
FT = FF // P

CH = 4096
RING = 5

META = 16
L2 = META + NT
DH, DD = 4, 128
SH, SD = 8, 64
NE, EF = 32, 256
CAP = 64
RMS_EPS = 1e-6


def chunk_plan():
    at, n = {}, 0
    for name, k in (("ada_h1", 4), ("w_in", 4), ("ada_rest", 8), ("w_out", 2), ("ffn", 16),
                    ("dn_qkv", 3), ("sb_qkv", 3), ("dn_z", 1), ("gates", 4), ("branch", 2), ("w_out2", 2),
                    ("experts", NE * 3 // 2)):
        at[name] = n
        n += k
    at["end"] = n
    return at


AT = chunk_plan()


def gate_chunk(e):
    return AT["experts"] + 3 * (e // 2) + e % 2


def down_chunk(e):
    return AT["experts"] + 3 * (e // 2) + 2


def ada_chunk(c):
    return AT["ada_h1"] + c if c < 4 else AT["ada_rest"] + c - 4


COLS = {}


def _cols():
    n = 0
    for name, k in (("g0", 8), ("b0", 8), ("g1", 8), ("b1", 8), ("ge", 8), ("be", 8), ("g3", 8), ("b3", 8),
                    ("b_ada", 48), ("qg", 2), ("kvg", 1), ("conv", 48), ("b_gate", 16), ("c", 8)):
        COLS[name] = (n, k)
        n += k
    COLS["end"] = (n, 0)


_cols()

CONST = {}


def _consts():
    n = 0
    for name, k in (("ident", P), ("ones", P), ("causal", P), ("decay", RH * P), ("xi", 2 * P), ("zeta", RH),
                    ("inv", RDK // 2), ("ucum", P), ("strict", P), ("m16", P), ("off16", P), ("causT", P),
                    ("sbmul", P), ("sbadd", P), ("tri", P), ("tie", 8), ("iota", CAP), ("eye32", 32)):
        CONST[name] = (n, k)
        n += k
    CONST["end"] = (n, 0)


_consts()

LN_ROWS = ("ln0", "ln1", "ln2", "emb", "ln3", "ln4")


def const_array():
    c = np.zeros((P, CONST["end"][0]), np.float32)
    p = np.arange(P)[:, None]
    f = np.arange(P)[None, :]

    def put(name, a):
        o, k = CONST[name]
        c[:, o:o + k] = a

    put("ident", p == f)
    put("ones", 1.0)
    put("causal", np.where(f <= p, 0.0, NEG))
    lg = np.log(1.0 - 2.0 ** (-5.0 - np.arange(RH)))
    sc = RDK ** -0.5
    put("decay", np.concatenate([np.where(f >= p, np.exp(lg[h] * np.maximum(f - p, 0)), 0.0) * sc
                                 for h in (0, 2, 1, 3)], 1))
    put("xi", np.concatenate([np.exp(lg[2 * a + p // 64] * (f + 1.0)) for a in range(2)], 1))
    put("zeta", np.exp(lg[None, :] * (P - 1 - p)) * sc)
    put("inv", 10000.0 ** (-np.arange(RDK // 2)[None, :] / (RDK // 2)) * np.ones((P, 1)))
    same = (p // 64) == (f // 64)
    same16 = (p // 16) == (f // 16)
    put("ucum", (p <= f) & same)
    put("strict", (f < p) & same)
    put("m16", np.where((f < p) & same16, -1.0, 0.0))
    put("off16", (f < p) & same & ~same16)
    put("causT", (f >= p) & same)
    put("sbmul", p < f)
    put("sbadd", np.where(p < f, 0.0, NEG))
    put("tri", p >= f)
    put("tie", np.arange(8, 0, -1)[None, :])
    put("eye32", p % 32 == np.arange(32)[None, :])
    put("iota", np.arange(CAP)[None, :])
    return c


def build(nc, IN, out):
    ctx = ExitStack()
    with ctx:
        def sb(name, shape, dt=F32):
            return ctx.enter_context(nc.sbuf_tensor(name, shape, dt))

        names = """
            landed0 landed1 landed2 landed3 landed4 used in_x in_cst in_col in_row0 in_row1 in_pos
            in_uq in_ukv in_gn silu_c xn xn_tr affine hT mod1 mod2 pj_mm pj_ev_a pj_ev_v rms_sq qn
            qn_tr qnT uq_mm rot rot_tr rotT_a rotT_v knope kn_ev sc0 sc1 sm0 sm1 ex0 ex1 nm0 nm1
            p_tr p_ev pv_mm mix_ev trig_r trig rqk_tr rqkT rs_mm sT kz kv_mm rS qx ro_mm ro_n rg_s
            gated g_tr g_ev dg gt_mm gtB ff_mm ff_rl ff_sq y2_mm out_done dve act pool ln_s ln_v
            in_meta meta_v meta_s meta_n meta_tr meta_h in_ba in_dn g2_mm g2_ev conv cvs ba_mm ba_ev
            sq nsq nr nrmd gates_ev br_mm mg mgd z1 zc ze zl zk zm za zw zo zov lg_mm cmb cT cTv
            cB_mm cB_ev eg eu hid d_mm rt_e rt_x in_rt be_e ug R_mm E01 ex01 knt vnt kv_ev gram ab
            n1t rd_mm rd_v rd_a u_mm uv wv s_mm sv vn_mm vn_v o_mm o_v os orv z_ev on on_tr mod_ev
            flag sel xg xgv sct yv
            """.split()
        S = namedtuple("Semaphores", names)(*[ctx.enter_context(nc.semaphore("s_" + n)) for n in names])
        landed = [S.landed0, S.landed1, S.landed2, S.landed3, S.landed4]

        psum = ctx.enter_context(nc.psum_tensor("psum", [P, 8, 512], F32))

        ring = sb("ring", [P, RING, CH])
        cst = sb("cst", [P, CONST["end"][0]])
        col = sb("col", [P, COLS["end"][0]])
        rowB = sb("rowB", [P, 2, 2, DM])
        gnB = sb("gnB", [P, 2, RH * RDV])
        X = sb("X", [P, T, DM])
        hT = sb("hT", [P, KD, L2])
        small = sb("small", [P, 336])
        modc = sb("modc", [P, 48])
        SCR = 19456
        scr = sb("scr", [P, SCR])

        def C(name, a=0, b=None):
            o, k = CONST[name]
            return cst[:, o + a:o + (k if b is None else b)]

        def V(name, a=0, b=None):
            o, k = COLS[name]
            return col[:, o + a:o + (k if b is None else b)]

        def arena(off, *shape):
            n = int(np.prod(shape))
            assert off + n <= SCR, (off, n)
            a = scr[:, off:off + n]
            if len(shape) == 2:
                return a.rearrange("p (a b) -> p a b", b=shape[1])
            if len(shape) == 3:
                return a.rearrange("p (a b c) -> p a b c", b=shape[1], c=shape[2])
            return a

        stat = small[:, 0:24].rearrange("p (t n s) -> p t n s", t=2, s=6)
        mv = small[:, 24:28].rearrange("p (t s) -> p t s", s=2)
        rstd = small[:, 28:30]
        sd = small[:, 30:32]
        csil = small[:, 32:40]
        epsc = small[:, 40:41]
        ssq = small[:, 42:46]
        rq = small[:, 46:50]
        posf = small[:, 52:54]
        diag = small[:, 208:336].rearrange("p (m j) -> p m j", m=4)
        A1 = small[:, 56:64]
        B1 = small[:, 64:72]
        nmax = small[:, 80:96]
        rsum = small[:, 96:112]
        rinv = small[:, 112:128]
        gst = small[:, 128:128 + 48].rearrange("p (n s) -> p n s", s=6)
        gmv = small[:, 176:192].rearrange("p (n s) -> p n s", s=2)
        grs = small[:, 192:200]
        gsd = small[:, 200:208]
        posi = sb("posi", [P, T], I32)

        pj = arena(0, T, 416)
        rqk = arena(832, T, 512)
        rv = arena(1856, T, 512)
        rg = arena(2880, T, 512)
        qnat = arena(3904, T * 9, QK)
        qnat4 = scr[:, 3904:3904 + T * 9 * QK].rearrange("p (t h d) -> p t h d", t=T, d=QK)
        qT = arena(5632, MH, NT)
        kT = arena(7680, MH, NT)
        vN = arena(9728, T, 512)
        mixT = arena(10752, KD, NT)
        Sb = arena(12800, MH, NT)
        S0 = arena(14848, MH, P)
        PT = scr[:, 15872:15872 + 3072].rearrange("p (k h q) -> p k h q", k=3, h=MH)
        qcn = arena(12800, T, 384)
        qnT = arena(13568, 2, NT)
        kvnT = arena(14080, NT)
        wuq = arena(15872, 2, 768)
        wukv = arena(17408, 1024)
        trig = arena(18944, 4, 64)
        cosT = trig[:, 0, :].rearrange("p (t f) -> p t f", t=T)
        sinT = trig[:, 1, :].rearrange("p (t f) -> p t f", t=T)
        rtmp = scr[:, 14848:15872].rearrange("p (n t w) -> p n t w", n=2, t=T)
        rqT = arena(5632, 4, NT)
        rsT = arena(6656, 8, P)
        rqx = arena(7680, 2, P)
        rkz = arena(7936, RH, RDK)
        rSt = arena(8192, 2, P)
        ro = arena(832, T, 512)
        dgt = arena(12800, KD, P)
        dgt2 = arena(16000, KD, P)
        gtB = arena(0, 2, DM)
        fTr = arena(2048, 8, NT)
        frl = arena(4096, 4, NT)
        metaX = scr[0:META, 12800:12800 + DM]

        raw = arena(0, 12, 3 + L2)
        cv = arena(3300, 12, L2)
        sbT = arena(6564, 8, L2)
        sbv = arena(8740, 3, 512)
        M = [arena(10276 + 1088 * n, 1088) for n in range(7)]
        vb = arena(0, 3, 512)
        kdec = arena(1536, 3, 512)
        kbe = arena(17892, 3, 512)
        sqr = arena(0, 8, L2)
        nrm = arena(10276, 8, L2)
        sm2 = sb("sm2", [P, 400])
        ba = sm2[:, 0:24].rearrange("p (t n) -> p t n", t=3)
        wba = sm2[:, 24:88].rearrange("p (k n) -> p k n", k=KD)
        beta = sm2[:, 88:100].rearrange("p (t n) -> p t n", t=3)
        gdn = sm2[:, 100:112].rearrange("p (t n) -> p t n", t=3)
        dN = sm2[:, 112:124].rearrange("p (t n) -> p t n", t=3)
        edN = sm2[:, 124:136].rearrange("p (t n) -> p t n", t=3)
        bed = sm2[:, 136:148].rearrange("p (t n) -> p t n", t=3)
        kdN = sm2[:, 148:160].rearrange("p (t n) -> p t n", t=3)
        alog = sm2[:, 160:164]
        dtb = sm2[:, 164:168]
        ealog = sm2[:, 168:172]
        t1, t2, t3, t4 = (sm2[:, 172 + 12 * n:184 + 12 * n].rearrange("p (t n) -> p t n", t=3) for n in range(4))
        cdc = sm2[:, 220:236].rearrange("p (n c) -> p n c", c=2)
        oss = sm2[:, 236:244]
        orn = sm2[:, 244:252]
        dnG = sm2[:, 252:380]
        epsq, epsk = sm2[:, 380:381], sm2[:, 381:382]

        b_ = lambda n: psum[:, n, :]
        block = ctx.enter_context(nc.Block())

        GROUPS = [(AT["dn_qkv"] + m // 4, m % 4, "T") for m in range(12)]
        GROUPS += [(AT["sb_qkv"] + m // 4, m % 4, "T") for m in range(8)]
        GROUPS += [(AT["sb_qkv"] + 2, 0, t) for t in range(3)]

        def ends_chunk(g):
            return g + 1 == len(GROUPS) or GROUPS[g + 1][0] != GROUPS[g][0]

        def group_wait(eng, g):
            if ends_chunk(g):
                eng.wait_ge(S.used, GROUPS[g][0] + 1)
            else:
                eng.wait_ge(S.g2_mm, sum(not ends_chunk(n) for n in range(g + 1)))

        def tok(t):
            return slice(0, META) if t == 2 else slice(META + t * P, META + (t + 1) * P)

        def prob(m, p):
            return m[:, p * P:(p + 1) * P] if p < 8 else m[0:META, 1024 + (p - 8) * META:1024 + (p - 7) * META]

        def bank_prob(b, p, mb, mo=0):
            if p < 8:
                return psum[:, b + p // 4, (p % 4) * P:(p % 4 + 1) * P]
            return psum[0:META, mb, mo + (p - 8) * META:mo + (p - 7) * META]

        x8 = lambda m: m[:, 0:1024].rearrange("p (n w) -> p n w", w=P)
        m4 = lambda m: m[0:META, 1024:1088].rearrange("p (n w) -> p n w", w=META)
        two = lambda b: psum[:, b:b + 2, :].rearrange("p b (n w) -> p (b n) w", w=P)
        mt4 = lambda b, o=0: psum[0:META, b, o:o + 64].rearrange("p (n w) -> p n w", w=META)
        mask8 = lambda c: C(c).unsqueeze(1).broadcast_to([P, 8, P])
        mask4 = lambda c: C(c)[0:META, 0:META].unsqueeze(1).broadcast_to([META, 4, META])
        M0, M1, M2, M3, M4, M5, M6 = M
        St = [M5[:, 0:512], M5[:, 512:1024]]
        zN = arena(17892, T, 512)
        oT = arena(10276, 4, NT)
        lk = [arena(12452, 640), arena(13092, 640)]
        ez = [arena(13732, 640), arena(14372, 640)]
        osT = arena(10276 + 5 * 1088, 4, NT)
        gat = arena(0, 16, NT)
        mrg = arena(6564, 8, NT)
        mtmp = arena(12452, 2, NT)

        def pe_second(pe, mm, transposes):
            tr = nc.tensor.transpose
            pe.wait_ge(S.hT, 3)
            pe.wait_ge(S.in_ba, 16)
            for t in range(3):
                for k in range(KD):
                    last = mm(psum[0:(META if t == 2 else P), 4, 8 * t:8 * t + 8], hT[:, k, tok(t)], wba[:, k, :],
                              start=(k == 0), stop=(k == KD - 1))
            last.then_inc(S.ba_mm, 1)
            for g, (n, m, form) in enumerate(GROUPS):
                if g == 0 or ends_chunk(g - 1):
                    landed_wait(pe, n)
                if g >= 4:
                    pe.wait_ge(S.g2_ev, g - 3)
                w = ring_at(n).rearrange("p (k n) -> p k n", k=KD)
                for k in range(KD):
                    if form == "T":
                        last = mm(psum[:, g % 4, 0:L2], w[:, k, m * P:(m + 1) * P], hT[:, k, :],
                                  start=(k == 0), stop=(k == KD - 1))
                    else:
                        last = mm(psum[0:(META if form == 2 else P), g % 4, :], hT[:, k, tok(form)], w[:, k, :],
                                  start=(k == 0), stop=(k == KD - 1))
                last.then_inc(S.used if ends_chunk(g) else S.g2_mm, 1)

            pe.wait_ge(S.sq, 1)
            pe.wait_ge(S.ba_ev, 1)
            for i in range(8):
                if i >= 4:
                    pe.wait_ge(S.nr, i - 3)
                mm(psum[:, 4 + i % 4, 0:L2], C("ones"), sqr[:, i, :], start=True, stop=True).then_inc(S.nsq, 1)
            pe.wait_ge(S.ug, 1)
            pe.wait_ge(S.nr, 8)
            for b in range(2):
                mm(b_(4 + b), C("ones"), M2[:, 512 * b:512 * b + 512], start=True, stop=True)
            mm(psum[:, 6, 0:64], C("ones")[0:META, :], M2[0:META, 1024:1088], start=True, stop=True)\
                .then_inc(S.R_mm, 1)
            pe.wait_ge(S.nrmd, 1)
            pe.wait_ge(S.cvs, 12)
            pe.wait_ge(S.g2_ev, len(GROUPS))
            for t in range(3):
                for h in range(DH):
                    last = tr(psum[0:(META if t == 2 else P), t, h * P:(h + 1) * P], cv[:, 4 + h, tok(t)], C("ident"))
            last.then_inc(S.knt, 1)
            for t, b in enumerate((3, 7, 4)):
                if t == 2:
                    pe.wait_ge(S.ex01, 1)
                for h in range(DH):
                    last = tr(psum[0:(META if t == 2 else P), b, h * P:(h + 1) * P], cv[:, 8 + h, tok(t)], C("ident"))
            last.then_inc(S.vnt, 1)
            pe.wait_ge(S.kv_ev, 1)
            for p in range(12):
                t, h = p // 4, p % 4
                kT_ = cv[:, 4 + h, tok(t)]
                mm(bank_prob(0, p, 2), kT_, kT_, start=True, stop=True)
                if p < 8:
                    last = mm(bank_prob(4, p, 6), kT_, cv[:, h, tok(t)], start=True, stop=True)
            mm(bank_prob(0, 11, 2), kT_, kT_, start=True, stop=True).then_inc(S.gram, 1)
            pe.wait_ge(S.ab, 1)
            for p in range(12):
                last = tr(bank_prob(0, p, 2), prob(M2, p), C("ident") if p < 8 else C("ident")[0:META, 0:META])
            last.then_inc(S.n1t, 1)

            rounds = [
                (12, [(0, 2, 0, M4, M2), (3, 5, 0, M2, M4)]),
                (12, [(0, 2, 0, M1, M6), (3, 5, 0, M5, M1), (6, 5, 64, M1, M5)]),
                (12, [(0, 2, 0, M2, M6), (3, 5, 0, M4, M2)]),
                (12, [(0, 2, 0, M1, M6)]),
                (8, [(0, 2, 0, M3, M6), (3, 5, 0, M6, None), (6, 5, 64, M6, M3)]),
                (8, [(3, 5, 0, M2, M1)]),
                (8, [(0, 2, 0, M3, M4)]),
                (8, [(0, 2, 0, M5, M4)]),
            ]
            for r, (count, products) in enumerate(rounds):
                pe.wait_ge(S.rd_v, DVE_ROUNDS[r])
                pe.wait_ge(S.rd_a, ACT_ROUNDS[r])
                for b, mb, mo, lhsT, rhs in products:
                    for p in range(count):
                        o = bank_prob(b, p, mb, mo)
                        if rhs is None:
                            last = tr(o, prob(lhsT, p), C("ident"))
                        else:
                            last = mm(o, prob(lhsT, p), prob(rhs, p), start=True, stop=True)
                last.then_inc(S.rd_mm, 1)
            pe.wait_ge(S.rd_v, 8)
            for p in range(12):
                t, h = p // 4, p % 4
                rows_ = slice(0, META) if t == 2 else slice(0, P)
                o = psum[0:META, 5, h * P:(h + 1) * P] if t == 2 else bank_prob(0, p, 2)
                last = mm(o, prob(M6, p), vb[rows_, t, h * P:(h + 1) * P], start=True, stop=True)
                if p < 8:
                    mm(bank_prob(3, p, 5), kbe[:, t, h * P:(h + 1) * P], prob(M6, p), start=True, stop=True)
            last.then_inc(S.u_mm, 1)
            pe.wait_ge(S.uv, 1)
            for h in range(DH):
                last = mm(psum[:, 6, h * P:(h + 1) * P], kdec[0:META, 2, h * P:(h + 1) * P],
                          M2[0:META, h * P:(h + 1) * P], start=True, stop=True)
            last.then_inc(S.s_mm, 1)
            pe.wait_ge(S.wv, 1)
            for i in range(4):
                t, c = i // 2, i % 2
                r = slice(64 * c, 64 * c + 64)
                pe.wait_ge(S.sv, i + 1)
                for h in range(DH):
                    p = 4 * t + h
                    last = mm(psum[r, i % 2, h * P:(h + 1) * P], M3[:, p * P + 64 * c:p * P + 64 * c + 64],
                              St[i % 2][:, h * P:(h + 1) * P], start=True, stop=True)
                last.then_inc(S.vn_mm, 1)
                pe.wait_ge(S.vn_v, i + 1)
                vnew = M4[:, 512 * t:512 * t + 512]
                if i < 3:
                    for h in range(DH):
                        last = mm(psum[:, 7 - i % 2, h * P:(h + 1) * P], kdec[r, t, h * P:(h + 1) * P],
                                  vnew[r, h * P:(h + 1) * P], start=True, stop=True)
                    last.then_inc(S.s_mm, 1)
                for h in range(DH):
                    p = 4 * t + h
                    o = psum[r, 3 + t, h * P:(h + 1) * P]
                    mm(o, cv[:, h, META + i * 64:META + i * 64 + 64], St[i % 2][:, h * P:(h + 1) * P],
                       start=True, stop=False)
                    last = mm(o, M0[r, p * P + 64 * c:p * P + 64 * c + 64], vnew[r, h * P:(h + 1) * P],
                              start=False, stop=True)
                last.then_inc(S.o_mm, 1)
            n = AT["dn_z"]
            landed_wait(pe, n)
            pe.wait_ge(S.vn_v, 4)
            w = ring_at(n).rearrange("p (k n) -> p k n", k=KD)
            for t in range(T):
                for k in range(KD):
                    last = mm(b_(t), hT[:, k, tok(t)], w[:, k, :], start=(k == 0), stop=(k == KD - 1))
            last.then_inc(S.used, 1)
            pe.wait_ge(S.on, 1)
            for h in range(DH):
                for t in range(T):
                    last = tr(psum[:, 5 + h // 2, (h % 2) * NT + t * P:(h % 2) * NT + (t + 1) * P],
                              M1[:, 512 * t + h * P:512 * t + (h + 1) * P], C("ident"))
            last.then_inc(S.on_tr, 1)

            def z_scores(h):
                b = h % 2
                if h >= 2:
                    pe.wait_ge(S.zw, h - 1)
                r = slice(64 * b, 64 * b + 64)
                q = sbT[r, h // 2, META:L2]
                k = sbT[r, 4 + h // 2, :]
                mm(psum[:, 2 * b, 0:NT], k[:, tok(0)], q, start=True, stop=False, skip_group_check=True)
                mm(psum[:, 2 * b, NT:2 * NT], k[:, 0:P], q, start=False, stop=False, skip_group_check=True)
                mm(psum[:, 2 * b + 1, 0:P], k[:, tok(1)], q[:, P:NT], start=True, stop=False,
                   skip_group_check=True).then_inc(S.z1, 1)

            def z_sums(h):
                b = h % 2
                pe.wait_ge(S.zm, h + 1)
                l0, l1 = lk[b][:, 0:NT], lk[b][:, 512:640]
                k0, me, k1 = psum[:, 2 * b, 0:NT], psum[:, 2 * b, NT:512], psum[:, 2 * b + 1, 0:P]
                mm(k0, C("tri"), l0, start=False, stop=False, skip_group_check=True)
                mm(k0[:, P:NT], C("ones"), l1, start=False, stop=True, skip_group_check=True)
                mm(me[0:META], C("tri")[0:META, 0:META], lk[b][0:META, NT:512], start=False, stop=False,
                   skip_group_check=True)
                mm(me[0:META], C("ones")[:, 0:META], l0, start=False, stop=False, skip_group_check=True)
                mm(me[0:META, P:NT], C("ones")[:, 0:META], l1, start=False, stop=True, skip_group_check=True)
                mm(k1, C("tri"), l1, start=False, stop=True, skip_group_check=True).then_inc(S.za, 1)

            def z_out(h):
                b = h % 2
                pe.wait_ge(S.zw, h + 1)
                if h % 4 == 0 and h:
                    pe.wait_ge(S.zov, h // 4)
                r = slice(64 * b, 64 * b + 64)
                o = psum[r, 4, (h // 2 % 2) * NT:(h // 2 % 2 + 1) * NT]
                f = slice(64 * h, 64 * h + 64)
                mm(o, sbv[:, 0, f], ez[b][:, 0:NT], start=True, stop=False)
                mm(o, sbv[0:META, 2, f], ez[b][0:META, NT:512], start=False, stop=False)
                mm(o[:, P:NT], sbv[:, 1, f], ez[b][:, 512:640], start=False, stop=True).then_inc(S.zo, 1)

            pe.wait_ge(S.z_ev, 2)
            pe.wait_ge(S.orv, 1)
            z_scores(0)
            for h in range(SH):
                if h + 1 < SH:
                    z_scores(h + 1)
                z_sums(h)
                if h:
                    z_out(h - 1)
            z_out(SH - 1)
            pe.wait_ge(S.zw, SH)
            for g in range(16):
                n = AT["gates"] + g // 4
                if g % 4 == 0:
                    landed_wait(pe, n)
                if g >= 4:
                    pe.wait_ge(S.gates_ev, g - 3)
                w = ring_at(n).rearrange("p (k n) -> p k n", k=KD)
                for k in range(KD):
                    last = mm(psum[:, g % 4, 0:NT], w[:, k, (g % 4) * P:(g % 4 + 1) * P], hT[:, k, META:L2],
                              start=(k == 0), stop=(k == KD - 1))
                last.then_inc(S.used if g % 4 == 3 else S.g2_mm, 1)
            pe.wait_ge(S.gates_ev, 16)
            pe.wait_ge(S.zov, 2)
            for i in range(2):
                landed_wait(pe, AT["branch"] + i)
            for m in range(KD):
                if m >= 2:
                    pe.wait_ge(S.mg, m - 1)
                for i, src in ((0, oT), (1, osT)):
                    w = ring_at(AT["branch"] + i).rearrange("p (k n) -> p k n", k=4)
                    for k in range(4):
                        last = mm(psum[:, 2 * (m % 2) + i, 0:NT], w[:, k, m * P:(m + 1) * P], src[:, k, :],
                                  start=(k == 0), stop=(k == 3))
                    last.then_inc(S.br_mm if m < KD - 1 else S.used, 1)
            pe.wait_ge(S.mgd, KD)
            for half in range(2):
                n = AT["w_out2"] + half
                landed_wait(pe, n)
                w = ring_at(n).rearrange("p (k n) -> p k n", k=KD)
                for t in range(T):
                    for k in range(KD):
                        last = mm(b_(4 + 2 * t + half), mrg[:, k, t * P:(t + 1) * P], w[:, k, :],
                                  start=(k == 0), stop=(k == KD - 1))
                last.then_inc(S.used, 1)
            transposes(5)
            pe_experts(pe, mm)

        DVE_ROUNDS = [1, 2, 3, 4, 5, 6, 6, 7]
        ACT_ROUNDS = [0, 1, 2, 3, 3, 4, 5, 5]

        def act_second(act, link, ln_sqrt):
            sc = nc.scalar
            act.wait_ge(S.in_dn, 32)
            act.wait_ge(S.ba_ev, 1)
            sc.activation(ealog, alog, ACT.Exp)
            sc.activation(t1, ba[:, :, 0:4], ACT.Exp, scale=-1.0)
            sc.activation(t2, t4, ACT.Exp, scale=-1.0).then_inc(S.be_e, 1)

            def evac(g):
                group_wait(act, g)
                b = psum[:, g % 4, :]
                if g < 12:
                    ins = sc.copy(raw[:, g, 3:3 + L2], b[:, 0:L2])
                elif g < 20:
                    ins = sc.activation(sbT[:, g - 12, :], b[:, 0:L2], ACT.Copy, scale=SD ** -0.5 if g < 16 else 1.0)
                elif g < 22:
                    ins = sc.copy(sbv[:, g - 20, :], b)
                else:
                    ins = sc.copy(sbv[0:META, 2, :], b[0:META])
                ins.then_inc(S.g2_ev, 1)

            for g in range(len(GROUPS)):
                evac(g)
                if g >= 3 and g - 3 < 12:
                    act.wait_ge(S.conv, g - 2)
                    sc.activation(cv[:, g - 3, :], cv[:, g - 3, :], ACT.Silu).then_inc(S.cvs, 1)
            act.wait_ge(S.cvs, 8)
            act.wait_ge(S.conv, 12)
            sc.activation(sqr[:, :, :], cv[:, 0:8, :], ACT.Square).then_inc(S.sq, 1)
            for i in range(8):
                act.wait_ge(S.nsq, i + 1)
                q = i < 4
                sc.activation(nrm[:, i, :], psum[:, 4 + i % 4, 0:L2], ACT.Sqrt, bias=epsq if q else epsk,
                              scale=float(DD) if q else 1.0).then_inc(S.nr, 1)
            act.wait_ge(S.E01, 1)
            sc.activation(M0[:, 0:1024], M0[:, 0:1024], ACT.Exp)
            sc.activation(M0[0:META, 1024:1088], M0[0:META, 1024:1088], ACT.Exp)
            sc.activation(M1[:, 0:1024], M1[:, 0:1024], ACT.Exp, scale=-1.0)
            sc.activation(M1[0:META, 1024:1088], M1[0:META, 1024:1088], ACT.Exp, scale=-1.0)
            sc.activation(M5[:, 0:1024], psum[:, 4:6, :].rearrange("p a b -> p (a b)"), ACT.Exp)
            sc.activation(edN, dN, ACT.Exp)
            sc.activation(kdN, kdN, ACT.Exp).then_inc(S.ex01, 1)

            def evac2(r, pairs):
                act.wait_ge(S.rd_mm, r + 1)
                for dst, b, mo, meta in pairs:
                    last = sc.copy(dst[:, 0:1024], psum[:, b:b + 2, :].rearrange("p a b -> p (a b)"))
                    if meta:
                        last = sc.copy(dst[0:META, 1024:1088], psum[0:META, 5, mo:mo + 64])
                last.then_inc(S.rd_a, 1)

            evac2(0, [(M5, 3, 0, True)])
            evac2(1, [(M2, 3, 0, True), (M4, 6, 64, True)])
            evac2(2, [(M1, 3, 0, True)])
            evac2(4, [(M5, 3, 0, False), (M1, 6, 0, False)])
            evac2(5, [(M3, 3, 0, False)])
            act.wait_ge(S.u_mm, 1)
            sc.copy(M3[:, 0:1024], psum[:, 3:5, :].rearrange("p a b -> p (a b)")).then_inc(S.wv, 1)
            act.wait_ge(S.o_v, 2)
            for i in range(8):
                last = sc.activation(M2[:, i * P:(i + 1) * P], M1[:, i * P:(i + 1) * P], ACT.Square,
                                     accum_out=oss[:, i:i + 1])
            link(last)
            sc.activation(orn, oss, ACT.Sqrt, bias=epsk, scale=1.0 / DD).then_inc(S.os, 1)
            act.wait_ge(S.used, AT["dn_z"] + 1)
            for t in range(T):
                sc.activation(zN[:, t, :], b_(t), ACT.Silu).then_inc(S.z_ev, 1)
            for h in range(SH + 1):
                if h < SH:
                    b = h % 2
                    act.wait_ge(S.zc, h + 1)
                    sc.activation(lk[b][:, :], lk[b][:, :], ACT.Exp).then_inc(S.ze, 1)
                    act.wait_ge(S.ze, h + 1)
                    sc.activation(lk[b][:, :], lk[b][:, :], ACT.Ln, bias=1.0).then_inc(S.zl, 1)
                if h:
                    b = (h - 1) % 2
                    act.wait_ge(S.zk, h)
                    if h >= 3:
                        act.wait_ge(S.zo, h - 2)
                    sc.activation(ez[b][:, :], psum[:, 2 * b:2 * b + 2, :].rearrange("p a b -> p (a b)")[:, 0:640],
                                  ACT.Exp).then_inc(S.zw, 1)
            for g in range(16):
                c = 4 * (g // 4) + g % 4
                if g % 4 == 3:
                    act.wait_ge(S.used, AT["gates"] + g // 4 + 1)
                else:
                    act.wait_ge(S.g2_mm, sum(not ends_chunk(n) for n in range(len(GROUPS))) + 3 * (g // 4) + g % 4 + 1)
                sc.activation(gat[:, g, :], psum[:, g % 4, 0:NT], ACT.Sigmoid,
                              bias=V("b_gate", g, g + 1)).then_inc(S.gates_ev, 1)
            ln_sqrt(6)
            act_experts(act, link, ln_sqrt)

        def dve_second(dve, v, link, residual, layer_norm, to_hT):
            for a in (ba, dN, kdN):
                v.memset(a, 0.0)
            v.memset(epsq, DD * RMS_EPS)
            v.memset(epsk, RMS_EPS)
            link(v.memset(raw[:, :, 0:3], 0.0))
            dve.wait_ge(S.ba_mm, 1)
            v.tensor_copy(ba[:, 0:2, :], psum[:, 4, 0:16].rearrange("p (t n) -> p t n", t=2))
            link(v.tensor_copy(ba[0:META, 2, :], psum[0:META, 4, 16:24]))
            dve.wait_ge(S.in_dn, 32)
            link(v.tensor_tensor(t3, ba[:, :, 4:8], dtb.unsqueeze(1).broadcast_to([P, 3, 4]), ALU.add))
            v.scalar_tensor_tensor(t4, t3, -1.0, t3, ALU.mult, ALU.max).then_inc(S.ba_ev, 1)
            dve.wait_ge(S.be_e, 1)
            link(v.tensor_scalar(t1, t1, 1.0, None, ALU.add))
            link(v.reciprocal(beta, t1))
            link(v.tensor_scalar(t4, t2, 2.0, None, ALU.add))
            link(v.reciprocal(t4, t4))
            link(v.tensor_tensor(t4, t4, t2, ALU.mult))
            link(v.tensor_tensor(t1, t4, t4, ALU.mult))
            link(v.tensor_scalar(t2, t1, 1.0 / 15, None, ALU.mult))
            for n in (13, 11, 9, 7, 5, 3):
                link(v.scalar_tensor_tensor(t2, t2, 1.0 / n, t1, ALU.add, ALU.mult))
            link(v.scalar_tensor_tensor(t2, t2, 1.0, t4, ALU.add, ALU.mult))
            link(v.tensor_scalar(t3, t3, 0.0, 0.5, ALU.max, ALU.mult))
            link(v.tensor_tensor(t3, t3, t2, ALU.add))
            link(v.scalar_tensor_tensor(gdn, t3, -2.0, ealog.unsqueeze(1).broadcast_to([P, 3, 4]), ALU.mult, ALU.mult))
            for i in range(12):
                dve.wait_ge(S.g2_ev, i + 1)
                link(v.tensor_scalar(cv[:, i, :], raw[:, i, 0:L2], V("conv", 4 * i, 4 * i + 1), None, ALU.mult))
                for j in range(1, 4):
                    ins = v.scalar_tensor_tensor(cv[:, i, :], raw[:, i, j:j + L2], V("conv", 4 * i + j, 4 * i + j + 1),
                                                 cv[:, i, :], ALU.mult, ALU.add)
                    if j < 3:
                        link(ins)
                ins.then_inc(S.conv, 1)
            for p in range(12):
                t, h = p // 4, p % 4
                r = slice(0, META) if t == 2 else slice(0, P)
                last = v.tensor_scalar(prob(M2, p), C("ucum")[r, 0:(META if t == 2 else P)], gdn[r, t, h:h + 1], None,
                                       ALU.mult)
            last.then_inc(S.ug, 1)
            dve.wait_ge(S.nr, 8)
            link(v.reciprocal(nrm[:, :, :], nrm[:, :, :]))
            v.tensor_tensor(cv[:, 0:8, :], cv[:, 0:8, :], nrm[:, :, :], ALU.mult).then_inc(S.nrmd, 1)
            dve.wait_ge(S.nrmd, 1)
            dve.wait_ge(S.R_mm, 1)
            for p in range(12):
                t, h = p // 4, p % 4
                r = slice(0, META) if t == 2 else slice(0, P)
                last = v.tensor_tensor_reduce(prob(M3, p), bank_prob(4, p, 6)[r], C("ident")[r, 0:(META if t == 2 else P)],
                                              1.0, 0.0, ALU.mult, ALU.add, dN[r, t, h:h + 1])
            link(last)
            for t in range(T):
                d = dN[:, t, :].unsqueeze(2).broadcast_to([P, 4, P])
                v.tensor_tensor(M4[:, 512 * t:512 * t + 512].rearrange("p (n w) -> p n w", w=P),
                                b_(4 + t).rearrange("p (n w) -> p n w", w=P), d, ALU.subtract)
            link(v.tensor_tensor(m4(M4), psum[0:META, 6, 0:64].rearrange("p (n w) -> p n w", w=META),
                                 dN[0:META, 2, :].unsqueeze(2).broadcast_to([META, 4, META]), ALU.subtract))
            for r, a, b in ((slice(0, P), 0, 1024), (slice(0, META), 1024, 1088)):
                v.tensor_scalar(M0[r, a:b], M4[r, a:b], 0.0, None, ALU.min)
                v.tensor_scalar(M1[r, a:b], M4[r, a:b], 0.0, None, ALU.max)
            flat = psum[:, 4:6, :].rearrange("p a b -> p (a b)")
            for c in range(2):
                r = slice(64 * c, 64 * c + 64)
                v.tensor_tensor(kdN[r, 0:2, :], flat[r, 64 * c + 63:1024:P].rearrange("p (t h) -> p t h", t=2),
                                dN[r, 0:2, :], ALU.subtract)
            v.tensor_tensor(kdN[0:META, 2, :], psum[0:META, 6, META - 1:64:META], dN[0:META, 2, :],
                            ALU.subtract).then_inc(S.E01, 1)
            dve.wait_ge(S.ex01, 1)
            v.tensor_tensor(x8(M0), x8(M0), mask8("causT"), ALU.mult)
            v.tensor_copy(cdc[:, :, :].rearrange("p n c -> p (n c)"), M5[:, 63:1024:64])
            link(v.tensor_tensor(bed, beta, edN, ALU.mult))
            dve.wait_ge(S.knt, 1)
            for t in range(3):
                r = slice(0, META) if t == 2 else slice(0, P)
                n = META if t == 2 else P
                src = psum[r, t, :].rearrange("p (h d) -> p h d", d=P)
                for dst, f in ((kbe, bed), (kdec, kdN)):
                    v.tensor_tensor(dst[r, t, :].rearrange("p (h d) -> p h d", d=P), src,
                                    f[r, t, :].unsqueeze(2).broadcast_to([n, 4, P]), ALU.mult)
            dve.wait_ge(S.vnt, 1)
            for t, b in enumerate((3, 7, 4)):
                r = slice(0, META) if t == 2 else slice(0, P)
                n = META if t == 2 else P
                last = v.tensor_tensor(vb[r, t, :].rearrange("p (h d) -> p h d", d=P),
                                       psum[r, b, :].rearrange("p (h d) -> p h d", d=P),
                                       beta[r, t, :].unsqueeze(2).broadcast_to([n, 4, P]), ALU.mult)
            last.then_inc(S.kv_ev, 1)
            dve.wait_ge(S.gram, 1)
            for p in range(12):
                t, h = p // 4, p % 4
                r = slice(0, META) if t == 2 else slice(0, P)
                last = v.scalar_tensor_tensor(prob(M1, p), bank_prob(0, p, 2), beta[r, t, h:h + 1], prob(M1, p),
                                              ALU.mult, ALU.mult)
            link(last)
            for t in range(T):
                c = slice(512 * t, 512 * t + 512)
                v.tensor_tensor(M0[:, c], M0[:, c], b_(4 + t), ALU.mult)
            v.tensor_tensor(x8(M3), x8(M1), mask8("off16"), ALU.mult)
            v.tensor_tensor(x8(M2), x8(M1), mask8("m16"), ALU.mult)
            v.tensor_tensor(m4(M2), m4(M1), mask4("m16"), ALU.mult).then_inc(S.ab, 1)
            for h in range(DH):
                last = v.tensor_tensor(cv[:, h, META:L2].rearrange("p (t w) -> p t w", t=T),
                                       cv[:, h, META:L2].rearrange("p (t w) -> p t w", t=T),
                                       M5[:, 0:1024].rearrange("p (t n w) -> p t n w", t=T, w=P)[:, :, h, :], ALU.mult)
            link(last)
            dve.wait_ge(S.n1t, 1)
            v.tensor_copy(M4[:, 0:1024], psum[:, 0:2, :].rearrange("p a b -> p (a b)"))
            v.tensor_copy(M4[0:META, 1024:1088], psum[0:META, 2, 0:64])
            v.tensor_tensor(x8(M6), two(0), mask8("ident"), ALU.add)
            v.tensor_tensor(m4(M6), mt4(2), mask4("ident"), ALU.add).then_inc(S.rd_v, 1)
            dve.wait_ge(S.rd_mm, 1)
            v.tensor_copy(M1[:, 0:1024], psum[:, 0:2, :].rearrange("p a b -> p (a b)"))
            v.tensor_copy(M1[0:META, 1024:1088], psum[0:META, 2, 0:64]).then_inc(S.rd_v, 1)
            for r in (1, 2, 3):
                dve.wait_ge(S.rd_mm, r + 1)
                v.tensor_tensor(x8(M6), two(0), x8(M6), ALU.add)
                v.tensor_tensor(m4(M6), mt4(2), m4(M6), ALU.add).then_inc(S.rd_v, 1)
            dve.wait_ge(S.rd_mm, 5)
            v.tensor_copy(M2[:, 0:1024], psum[:, 0:2, :].rearrange("p a b -> p (a b)"))
            v.scalar_tensor_tensor(x8(M4), two(0), -1.0, mask8("ident"), ALU.mult, ALU.add).then_inc(S.rd_v, 1)
            dve.wait_ge(S.rd_mm, 7)
            v.tensor_tensor(x8(M4), two(0), x8(M4), ALU.add).then_inc(S.rd_v, 1)
            dve.wait_ge(S.rd_mm, 8)
            v.tensor_copy(x8(M6), two(0)).then_inc(S.rd_v, 1)
            dve.wait_ge(S.u_mm, 1)
            v.tensor_copy(M1[:, 0:1024], psum[:, 0:2, :].rearrange("p a b -> p (a b)"))
            v.tensor_copy(M2[0:META, 0:512], psum[0:META, 5, :]).then_inc(S.uv, 1)
            dve.wait_ge(S.s_mm, 1)
            v.tensor_copy(St[0], b_(6)).then_inc(S.sv, 1)
            for i in range(4):
                t, c = i // 2, i % 2
                r = slice(64 * c, 64 * c + 64)
                f = slice(512 * t, 512 * t + 512)
                dve.wait_ge(S.vn_mm, i + 1)
                v.tensor_tensor(M4[r, f], M1[r, f], psum[r, i % 2, :], ALU.subtract).then_inc(S.vn_v, 1)
                if i < 3:
                    if i >= 1:
                        dve.wait_ge(S.o_mm, i)
                    dve.wait_ge(S.sv, i + 1)
                    dve.wait_ge(S.s_mm, i + 2)
                    for h in range(DH):
                        d = slice(h * P, (h + 1) * P)
                        last = v.scalar_tensor_tensor(St[(i + 1) % 2][:, d], St[i % 2][:, d],
                                                      cdc[:, 4 * t + h, c:c + 1], psum[:, 7 - i % 2, d],
                                                      ALU.mult, ALU.add)
                    last.then_inc(S.sv, 1)
                if c == 1:
                    dve.wait_ge(S.o_mm, i + 1)
                    v.tensor_copy(M1[:, f], b_(3 + t)).then_inc(S.o_v, 1)
            dve.wait_ge(S.os, 1)
            dve.wait_ge(S.o_v, 2)
            link(v.reciprocal(orn, orn))
            link(v.tensor_tensor(x8(M1), x8(M1), orn.unsqueeze(2).broadcast_to([P, 8, P]), ALU.mult))
            link(v.tensor_tensor(x8(M1), x8(M1), dnG.unsqueeze(1).broadcast_to([P, 8, P]), ALU.mult))
            dve.wait_ge(S.z_ev, 2)
            v.tensor_tensor(M1[:, 0:1024], M1[:, 0:1024], zN[:, :, :].rearrange("p t w -> p (t w)"),
                            ALU.mult).then_inc(S.on, 1)
            dve.wait_ge(S.on_tr, 1)
            v.tensor_copy(oT[:, :, :], psum[:, 5:7, :].rearrange("p a (b c) -> p (a b) c", c=NT)).then_inc(S.orv, 1)

            diag = lambda a: a.rearrange("p (n w) -> p n w", w=P)[:, 0:5:4, :]
            mul2 = C("sbmul").unsqueeze(1).broadcast_to([P, 2, P])
            add2 = C("sbadd").unsqueeze(1).broadcast_to([P, 2, P])
            for h in range(SH + 1):
                if h < SH:
                    b = h % 2
                    z = psum[:, 2 * b:2 * b + 2, :].rearrange("p a b -> p (a b)")[:, 0:640]
                    dve.wait_ge(S.z1, h + 1)
                    if h >= 2:
                        dve.wait_ge(S.za, h - 1)
                    v.tensor_scalar(lk[b][:, :], z, 80.0, None, ALU.min).then_inc(S.zc, 1)
                    dve.wait_ge(S.zl, h + 1)
                    link(v.tensor_tensor(lk[b][:, :], lk[b][:, :], z, ALU.max))
                    link(v.tensor_scalar(lk[b][:, :], lk[b][:, :], -1.0, None, ALU.mult))
                    v.tensor_tensor(diag(lk[b]), diag(lk[b]), mul2, ALU.mult).then_inc(S.zm, 1)
                if h:
                    b = (h - 1) % 2
                    z = psum[:, 2 * b:2 * b + 2, :].rearrange("p a b -> p (a b)")[:, 0:640]
                    dve.wait_ge(S.za, h)
                    v.tensor_tensor(diag(z), diag(z), add2, ALU.add).then_inc(S.zk, 1)
                    if h % 4 == 0:
                        dve.wait_ge(S.zo, h)
                        v.tensor_copy(osT[:, h // 2 - 2:h // 2, :], b_(4).rearrange("p (a b) -> p a b", a=2))\
                            .then_inc(S.zov, 1)
            for m in range(KD):
                if m < KD - 1:
                    dve.wait_ge(S.br_mm, 2 * m + 2)
                else:
                    dve.wait_ge(S.used, AT["branch"] + 2)
                dve.wait_ge(S.gates_ev, 16)
                v.tensor_tensor(mtmp[:, 0, :], psum[:, 2 * (m % 2), 0:NT], gat[:, m, :], ALU.mult)
                v.tensor_tensor(mtmp[:, 1, :], psum[:, 2 * (m % 2) + 1, 0:NT], gat[:, 8 + m, :], ALU.mult)\
                    .then_inc(S.mg, 1)
                dve.wait_ge(S.mg, m + 1)
                v.tensor_tensor(mrg[:, m, :], mtmp[:, 0, :], mtmp[:, 1, :], ALU.add).then_inc(S.mgd, 1)
                dve.wait_ge(S.mgd, m + 1)
            dve.wait_ge(S.used, AT["w_out2"] + 2)
            residual(None, 4)
            layer_norm(5, 6)
            to_hT(4, V("g3"), V("b3"))
            dve_experts(dve, v, link, residual, layer_norm)

        def pool_tail(pool, link, affine):
            affine(4, S.xn_tr, 4)
            pool_experts(pool, link, affine)

        lay = gnB[:, :, :].rearrange("p a b -> p (a b)")
        Rw = lay[:, 0:288].rearrange("p (k n) -> p k n", k=KD)
        rb = lay[:, 288:324]
        NG, EG = 4, NE // 4

        def rt(off, *shape):
            return arena(off, T, *shape)

        lg = rt(0, 36)
        gmx, ohg, gex, gsum = rt(80, 1), rt(84, NG), rt(92, NG), rt(100, 1)
        stmp = arena(104, T * NG, EG)
        sel, oh1, oh2 = rt(168, EG), rt(184, EG), rt(200, EG)
        m1, m2, dl, ed = rt(216, 1), rt(218, 1), rt(220, 1), rt(222, 1)
        a1, a2, tq = rt(224, 1), rt(226, 1), rt(228, 1)
        comb = arena(240, T, NE)
        cT = arena(320, NT)[0:NE]
        mem = rt(600, NE)
        slot = rt(664, NE)
        cmx = arena(728, 1)
        flag = sb("flag", [P, 1], I32)
        sel2 = [arena(1000 + 256 * n, T, 2 * CAP) for n in range(2)]
        selw = [arena(1512 + 256 * n, T, 2 * CAP) for n in range(2)]
        xg = [arena(2536 + 1024 * n, KD, 2 * CAP) for n in range(2)]
        yg = [arena(4584 + 1024 * n, DM) for n in range(2)]
        pg = [arena(6632 + 256 * n, 256) for n in range(2)]
        hp = [arena(7144 + 256 * n, 256) for n in range(2)]
        turned = [arena(7656 + 512 * n, 512) for n in range(2)]
        NP = NE // 2
        cB = arena(1000, NE, NT)
        eg_s = arena(9192, 2, 512)
        eh_s = arena(10216, 2, 512)
        hid = arena(11240, 2, 512)

        def pe_experts(pe, mm):
            pe.wait_ge(S.hT, 4)
            pe.wait_ge(S.in_rt, 32)
            for t in range(T):
                for k in range(KD):
                    last = mm(psum[:, 4, 36 * t:36 * t + 36], hT[:, k, tok(t)], Rw[:, k, :],
                              start=(k == 0), stop=(k == KD - 1))
            last.then_inc(S.lg_mm, 1)
            pe.wait_ge(S.cmb, 1)
            mm(psum[:, 5, 0:NE], C("sbmul"), mem[:, 0, :], start=True, stop=True)
            mm(psum[:, 5, NE:2 * NE], C("ones"), mem[:, 0, :], start=True, stop=False)
            mm(psum[:, 5, NE:2 * NE], C("sbmul"), mem[:, 1, :], start=False, stop=True)
            mm(psum[:, 5, 2 * NE:3 * NE], C("ones"), mem[:, 0, :], start=True, stop=False)
            mm(psum[:, 5, 2 * NE:3 * NE], C("ones"), mem[:, 1, :], start=False, stop=True).then_inc(S.lg_mm, 1)
            pe.wait_ge(S.flag, 1)
            crowded = pe.value_load(flag[0:1, 0:1], min_val=0, max_val=1)
            with pe.If(crowded == 0):
                pe_gathered(pe, mm)
            with pe.Else():
                pe_dense(pe, mm)

        def pe_gathered(pe, mm):
            def gather(p):
                pe.wait_ge(S.sel, 2 * p + 1)
                if p >= 2:
                    pe.wait_ge(S.yv, 2 * (p - 1))
                for k in range(KD):
                    for t in range(T):
                        last = mm(psum[:, k // 4, (k % 4) * P:(k % 4 + 1) * P], X[:, t, k * P:(k + 1) * P],
                                  sel2[p % 2][:, t, :], start=(t == 0), stop=(t == T - 1))
                last.then_inc(S.xg, 1)

            def gate_up(p):
                for e in range(2):
                    landed_wait(pe, gate_chunk(2 * p + e))
                pe.wait_ge(S.xgv, 2 * (p + 1))
                if p:
                    pe.wait_ge(S.eu, p)
                for k in range(KD):
                    for e in range(2):
                        w = ring_at(gate_chunk(2 * p + e)).rearrange("p (k n) -> p k n", k=KD)
                        last = mm(psum[e * CAP:(e + 1) * CAP, 2, :], xg[p % 2][:, k, e * CAP:(e + 1) * CAP],
                                  w[:, k, :], start=(k == 0), stop=(k == KD - 1))
                        if k == KD - 1:
                            last.then_inc(S.used, 1)

            def turn(p):
                pe.wait_ge(S.sel, 2 * p + 2)
                pe.wait_ge(S.eu, p + 1)
                if p:
                    pe.wait_ge(S.cTv, p)
                for i in range(2):
                    nc.tensor.transpose(psum[:, 3, i * P:(i + 1) * P], hp[p % 2][:, i * P:(i + 1) * P], C("ident"))
                for t in range(T):
                    last = nc.tensor.transpose(psum[:, 3, 256 + t * P:256 + (t + 1) * P], selw[p % 2][:, t, :],
                                               C("ident"))
                last.then_inc(S.cT, 1)

            def scatter(p):
                pe.wait_ge(S.yv, 2 * (p + 1))
                for t in range(T):
                    for half in range(2):
                        last = mm(b_(4 + 2 * t + half), turned[p % 2][:, 256 + t * P:256 + (t + 1) * P],
                                  yg[p % 2][:, half * 512:(half + 1) * 512], start=(p == 0), stop=(p == NP - 1))
                last.then_inc(S.sct, 1)

            def down(p):
                n = down_chunk(2 * p)
                landed_wait(pe, n)
                pe.wait_ge(S.cTv, p + 1)
                if p < NP - 1:
                    pe.wait_ge(S.xgv, 2 * (p + 2))
                w = ring_at(n).rearrange("p (e f n) -> p e f n", e=2, f=2)
                for half in range(2):
                    for f in range(2):
                        for e in range(2):
                            c = f * P + e * CAP
                            last = mm(psum[e * CAP:(e + 1) * CAP, half, :], turned[p % 2][:, c:c + CAP],
                                      w[:, e, f, half * 512:(half + 1) * 512], start=(f == 0), stop=(f == 1))
                last.then_inc(S.used, 1)

            pe.wait_ge(S.affine, 5)
            gather(0)
            for p in range(NP):
                gate_up(p)
                if p < NP - 1:
                    gather(p + 1)
                turn(p)
                if p:
                    scatter(p - 1)
                down(p)
            scatter(NP - 1)

        def pe_dense(pe, mm):
            pe.wait_ge(S.cmb, 2)
            for t in range(T):
                last = nc.tensor.transpose(psum[0:NE, 5, t * P:(t + 1) * P], comb[:, t, :], C("ident"))
            last.then_inc(S.cT, 1)
            pe.wait_ge(S.cTv, 1)
            for e in range(NE):
                if e >= 4:
                    pe.wait_ge(S.cB_ev, e - 3)
                mm(psum[:, e % 4, 0:NT], C("ident")[0:NE, e:e + 1].broadcast_to([NE, P]), cT, start=True, stop=True)\
                    .then_inc(S.cB_mm, 1)
            pe.wait_ge(S.cB_ev, NE)

            def down(e):
                n = down_chunk(e)
                landed_wait(pe, n)
                pe.wait_ge(S.hid, e + 1)
                w = ring_at(n).rearrange("p (e f n) -> p e f n", e=2, f=2)
                for f in range(2):
                    for t in range(T):
                        for half in range(2):
                            last = mm(b_(4 + 2 * t + half), hid[:, e % 2, f * NT + t * P:f * NT + (t + 1) * P],
                                      w[:, e % 2, f, half * 512:(half + 1) * 512],
                                      start=(e == 0 and f == 0), stop=(e == NE - 1 and f == 1))
                last.then_inc(S.used if e % 2 else S.d_mm, 1)

            for e in range(NE):
                n = gate_chunk(e)
                landed_wait(pe, n)
                if e >= 2:
                    pe.wait_ge(S.eu, e - 1)
                w = ring_at(n).rearrange("p (k w n) -> p k w n", w=2, k=KD)
                for i in range(2):
                    for f in range(2):
                        for k in range(KD):
                            last = mm(psum[:, 2 * (e % 2) + i, f * NT:(f + 1) * NT],
                                      w[:, k, i, f * P:(f + 1) * P], hT[:, k, META:L2],
                                      start=(k == 0), stop=(k == KD - 1))
                last.then_inc(S.used, 1)
                if e % 2:
                    down(e - 1)
                    down(e)

        def act_experts(act, link, ln_sqrt):
            act.wait_ge(S.rt_x, 1)
            nc.scalar.activation(gex[:, :, :], gex[:, :, :], ACT.Exp)
            nc.scalar.activation(ed[:, :, :], dl[:, :, :], ACT.Exp).then_inc(S.rt_e, 1)
            act.wait_ge(S.flag, 1)
            crowded = act.value_load(flag[0:1, 0:1], min_val=0, max_val=1)
            with act.If(crowded == 0):
                act_gathered(act)
            with act.Else():
                act_dense(act)
            ln_sqrt(7)

        def act_gathered(act):
            def gathered(p):
                act.wait_ge(S.xg, p + 1)
                nc.scalar.copy(xg[p % 2][:, 0:4, :].rearrange("p k n -> p (k n)"), b_(0)).then_inc(S.xgv, 1)

            gathered(0)
            for p in range(NP):
                act.wait_ge(S.used, gate_chunk(2 * p + 1) + 1)
                if p >= 2:
                    act.wait_ge(S.eu, p - 1)
                nc.scalar.activation(pg[p % 2], psum[:, 2, 0:256], ACT.Silu).then_inc(S.eg, 1)
                if p < NP - 1:
                    gathered(p + 1)
                act.wait_ge(S.used, down_chunk(2 * p) + 1)
                if p >= 2:
                    act.wait_ge(S.sct, p - 1)
                nc.scalar.copy(yg[p % 2][:, 0:512], b_(0)).then_inc(S.yv, 1)

        def act_dense(act):
            for e in range(NE):
                act.wait_ge(S.cB_mm, e + 1)
                nc.scalar.copy(cB[:, e, :], psum[:, e % 4, 0:NT]).then_inc(S.cB_ev, 1)
            for e in range(NE):
                act.wait_ge(S.used, gate_chunk(e) + 1)
                if e >= 2:
                    act.wait_ge(S.eu, e - 1)
                nc.scalar.activation(eg_s[:, e % 2, :], b_(2 * (e % 2)), ACT.Silu).then_inc(S.eg, 1)

        def dve_experts(dve, v, link, residual, layer_norm):
            dve.wait_ge(S.lg_mm, 1)
            dve.wait_ge(S.in_rt, 32)
            link(v.tensor_tensor(lg[:, :, :], psum[:, 4, 0:72].rearrange("p (t n) -> p t n", t=T),
                                 rb.unsqueeze(1).broadcast_to([P, T, 36]), ALU.add))
            gl, el = lg[:, :, 0:NG], lg[:, :, NG:36]

            def first_max(x, n, mx, oh):
                link(v.tensor_reduce(mx, x, AX, ALU.max))
                link(v.tensor_tensor(oh, x, mx.broadcast_to([P, T, n]), ALU.is_equal))
                link(v.tensor_tensor(oh, oh, C("tie", 0, n).unsqueeze(1).broadcast_to([P, T, n]), ALU.mult))
                link(v.tensor_reduce(tq, oh, AX, ALU.max))
                link(v.tensor_tensor(oh, oh, tq.broadcast_to([P, T, n]), ALU.is_equal))

            first_max(gl, NG, gmx, ohg)
            link(v.tensor_tensor(gex, gl, gmx.broadcast_to([P, T, NG]), ALU.subtract))
            for t in range(T):
                last = v.tensor_tensor(stmp[:, t * NG:(t + 1) * NG, :], el[:, t, :].rearrange("p (g e) -> p g e", g=NG),
                                       ohg[:, t, :].unsqueeze(2).broadcast_to([P, NG, EG]), ALU.mult)
            link(last)
            for t in range(T):
                last = v.tensor_reduce(sel[:, t, :], stmp[:, t * NG:(t + 1) * NG, :].rearrange("p g e -> p e g"), AX,
                                       ALU.add)
            link(last)
            first_max(sel, EG, m1, oh1)
            link(v.scalar_tensor_tensor(sel, oh1, NEG, sel, ALU.mult, ALU.add))
            first_max(sel, EG, m2, oh2)
            v.tensor_tensor(dl, m2, m1, ALU.subtract).then_inc(S.rt_x, 1)
            link(v.tensor_tensor(sel, oh1, oh2, ALU.add))
            for t in range(T):
                last = v.tensor_tensor(mem[:, t, :].rearrange("p (g e) -> p g e", g=NG),
                                       sel[:, t:t + 1, :].broadcast_to([P, NG, EG]),
                                       ohg[:, t, :].unsqueeze(2).broadcast_to([P, NG, EG]), ALU.mult)
            last.then_inc(S.cmb, 1)
            dve.wait_ge(S.rt_e, 1)
            link(v.tensor_reduce(gsum, gex, AX, ALU.add))
            link(v.tensor_scalar(a1, ed, 1.0, None, ALU.add))
            link(v.tensor_tensor(a1, a1, gsum, ALU.mult))
            link(v.reciprocal(a1, a1))
            link(v.tensor_tensor(a2, a1, ed, ALU.mult))
            link(v.tensor_tensor(oh1, oh1, a1.broadcast_to([P, T, EG]), ALU.mult))
            link(v.tensor_tensor(oh2, oh2, a2.broadcast_to([P, T, EG]), ALU.mult))
            link(v.tensor_tensor(oh1, oh1, oh2, ALU.add))
            for t in range(T):
                last = v.tensor_tensor(comb[:, t, :].rearrange("p (g e) -> p g e", g=NG),
                                       oh1[:, t:t + 1, :].broadcast_to([P, NG, EG]),
                                       ohg[:, t, :].unsqueeze(2).broadcast_to([P, NG, EG]), ALU.mult)
            last.then_inc(S.cmb, 1)
            dve.wait_ge(S.lg_mm, 2)
            dve.wait_ge(S.cmb, 2)
            link(v.scalar_tensor_tensor(slot, psum[:, 5, 0:2 * NE].rearrange("p (t n) -> p t n", t=T), 1.0, mem,
                                        ALU.add, ALU.mult))
            link(v.tensor_scalar(slot, slot, -1.0, None, ALU.add))
            link(v.tensor_reduce(cmx, psum[:, 5, 2 * NE:3 * NE], AX, ALU.max))
            v.tensor_scalar(flag[:, :], cmx, float(CAP), None, ALU.is_gt).then_inc(S.flag, 1)
            dve.wait_ge(S.flag, 1)
            crowded = dve.value_load(flag[0:1, 0:1], min_val=0, max_val=1)
            with dve.If(crowded == 0):
                dve_gathered(dve, v)
            with dve.Else():
                dve_dense(dve, v)
            residual(None, 5)
            layer_norm(6, 7)

        def dve_gathered(dve, v):
            def select(p):
                if p >= 2:
                    dve.wait_ge(S.xg, p - 1)
                v.tensor_tensor(sel2[p % 2][:, :, :].rearrange("p t (e n) -> p t e n", e=2),
                                C("iota").unsqueeze(1).unsqueeze(1).broadcast_to([P, T, 2, CAP]),
                                slot[:, :, 2 * p:2 * p + 2].unsqueeze(3).broadcast_to([P, T, 2, CAP]),
                                ALU.is_equal).then_inc(S.sel, 1)
                dve.wait_ge(S.sel, 2 * p + 1)
                if p >= 2:
                    dve.wait_ge(S.cT, p - 1)
                v.tensor_tensor(selw[p % 2][:, :, :].rearrange("p t (e n) -> p t e n", e=2),
                                sel2[p % 2][:, :, :].rearrange("p t (e n) -> p t e n", e=2),
                                comb[:, :, 2 * p:2 * p + 2].unsqueeze(3).broadcast_to([P, T, 2, CAP]),
                                ALU.mult).then_inc(S.sel, 1)

            def gathered(p):
                dve.wait_ge(S.xg, p + 1)
                v.tensor_copy(xg[p % 2][:, 4:8, :].rearrange("p k n -> p (k n)"), b_(1)).then_inc(S.xgv, 1)

            select(0)
            select(1)
            gathered(0)
            for p in range(NP):
                dve.wait_ge(S.eg, p + 1)
                if p >= 2:
                    dve.wait_ge(S.cT, p - 1)
                v.tensor_tensor(hp[p % 2], psum[:, 2, 256:512], pg[p % 2], ALU.mult).then_inc(S.eu, 1)
                if p < NP - 1:
                    gathered(p + 1)
                dve.wait_ge(S.cT, p + 1)
                if p >= 2:
                    dve.wait_ge(S.sct, p - 1)
                v.tensor_copy(turned[p % 2], b_(3)).then_inc(S.cTv, 1)
                if p + 2 < NP:
                    select(p + 2)
                dve.wait_ge(S.used, down_chunk(2 * p) + 1)
                v.tensor_copy(yg[p % 2][:, 512:1024], b_(1)).then_inc(S.yv, 1)
            dve.wait_ge(S.sct, NP)

        def dve_dense(dve, v):
            dve.wait_ge(S.cT, 1)
            v.tensor_copy(cT, psum[0:NE, 5, 0:NT]).then_inc(S.cTv, 1)
            for e in range(NE):
                dve.wait_ge(S.eg, e + 1)
                if e >= 2:
                    dve.wait_ge(S.hid, e - 1)
                v.tensor_tensor(eh_s[:, e % 2, :], b_(2 * (e % 2) + 1), eg_s[:, e % 2, :], ALU.mult).then_inc(S.eu, 1)
            dve.wait_ge(S.used, AT["end"])

        def pool_experts(pool, link, affine):
            pool.wait_ge(S.flag, 1)
            crowded = pool.value_load(flag[0:1, 0:1], min_val=0, max_val=1)
            with pool.If(crowded == 1):
                pool_dense(pool)
            affine(5, S.xn, 6)

        def pool_dense(pool):
            for e in range(NE):
                pool.wait_ge(S.eu, e + 1)
                pool.wait_ge(S.cB_ev, NE)
                if e >= 2:
                    if e % 2:
                        pool.wait_ge(S.used, down_chunk(e - 2) + 1)
                    else:
                        pool.wait_ge(S.d_mm, (e - 2) // 2 + 1)
                nc.gpsimd.tensor_tensor(hid[:, e % 2, :].rearrange("p (f t) -> p f t", f=2),
                                        eh_s[:, e % 2, :].rearrange("p (f t) -> p f t", f=2),
                                        cB[:, e:e + 1, :].broadcast_to([P, 2, NT]), ALU.mult).then_inc(S.hid, 1)


        def ring_at(n):
            return ring[:, n % RING, :]

        def landed_wait(eng, n):
            eng.wait_ge(landed[n % RING], 16 * (n // RING + 1))

        n_chunks = AT["end"]

        @block.sync
        def _(sp):
            sp.dma_start(X[:, :, :], IN["x"].rearrange("(t p) d -> p t d", p=P)).then_inc(S.in_x, 16)
            sp.dma_start(col[:, :], IN["cols"]).then_inc(S.in_col, 16)
            sp.dma_start(metaX, IN["meta"]).then_inc(S.in_meta, 16)
            for n in range(min(RING, n_chunks)):
                sp.dma_start(ring_at(n), IN["stream"][n]).then_inc(landed[n % RING], 16)
            for n in range(RING, n_chunks):
                sp.wait_ge(S.used, n - RING + 1)
                sp.dma_start(ring_at(n), IN["stream"][n]).then_inc(landed[n % RING], 16)
            sp.wait_ge(S.affine, 6)
            sp.dma_start(out.rearrange("(t p) d -> p t d", p=P), X[:, :, :]).then_inc(S.out_done, 16)
            sp.wait_ge(S.out_done, 16)

        @block.gpsimd
        def _(pool):
            chain = [0]

            def link(ins):
                chain[0] += 1
                ins.then_inc(S.pool, 1)
                pool.wait_ge(S.pool, chain[0])

            def rows(i, buf, sem):
                pool.dma_start(rowB[:, buf, :, :], IN["rows"][i].partition_broadcast(P)).then_inc(sem, 16)

            pool.dma_start(cst[:, :], IN["consts"]).then_inc(S.in_cst, 16)
            pool.dma_start(posi[:, :], IN["pos"]).then_inc(S.in_pos, 16)
            rows(0, 0, S.in_row0)
            rows(1, 1, S.in_row1)
            pool.dma_start(wuq[:, :, :], IN["w_uq"]).then_inc(S.in_uq, 16)
            pool.dma_start(wukv[:, :], IN["w_ukv"]).then_inc(S.in_ukv, 16)
            pool.dma_start(gnB[:, :, :], IN["gn"].partition_broadcast(P)).then_inc(S.in_gn, 16)

            def affine(i, sem, count):
                buf = i % 2
                pool.wait_ge((S.in_row0, S.in_row1)[buf], 16 * (i // 2 + 1))
                pool.wait_ge(sem, count)
                g = rowB[:, buf, 0:1, :].broadcast_to([P, T, DM])
                b = rowB[:, buf, 1:2, :].broadcast_to([P, T, DM])
                link(nc.gpsimd.tensor_tensor(X[:, :, :], X[:, :, :], g, ALU.mult))
                nc.gpsimd.tensor_tensor(X[:, :, :], X[:, :, :], b, ALU.add).then_inc(S.affine, 1)

            pool.dma_start(wba[:, :, :], IN["w_ba"]).then_inc(S.in_ba, 16)
            pool.dma_start(sm2[:, 160:168], IN["dn_rows"].partition_broadcast(P)).then_inc(S.in_dn, 16)
            pool.dma_start(dnG, IN["dn_g"].partition_broadcast(P)).then_inc(S.in_dn, 16)
            affine(0, S.xn_tr, 1)
            pool.wait_ge(S.affine, 1)
            rows(2, 0, S.in_row0)
            pool.wait_ge(S.in_gn, 16)
            pool.wait_ge(S.ro_n, 1)
            g = gnB[:, 0:1, :].broadcast_to([P, T, 512])
            b = gnB[:, 1:2, :].broadcast_to([P, T, 512])
            link(nc.gpsimd.tensor_tensor(ro[:, :, :], ro[:, :, :], g, ALU.mult))
            link(nc.gpsimd.tensor_tensor(ro[:, :, :], ro[:, :, :], b, ALU.add))
            pool.wait_ge(S.rg_s, 2)
            nc.gpsimd.tensor_tensor(ro[:, :, :], ro[:, :, :], rg[:, :, :], ALU.mult).then_inc(S.gated, 1)
            pool.wait_ge(S.gated, 1)
            pool.dma_start(gnB[:, :, :].rearrange("p a b -> p (a b)")[:, 0:288], IN["router_w"]).then_inc(S.in_rt, 16)
            pool.dma_start(gnB[:, :, :].rearrange("p a b -> p (a b)")[:, 288:324], IN["router_b"].partition_broadcast(P)).then_inc(S.in_rt, 16)
            affine(1, S.xn_tr, 2)
            pool.wait_ge(S.affine, 2)
            rows(3, 1, S.in_row1)
            for f in range(FT):
                pool.wait_ge(S.ff_rl, f + 1)
                if f >= 8:
                    pool.wait_ge(S.y2_mm, f - 7)
                nc.gpsimd.tensor_tensor(fTr[:, f % 8, :], frl[:, f % 4, :], frl[:, f % 4, :], ALU.mult)\
                    .then_inc(S.ff_sq, 1)
            affine(2, S.xn, 3)
            pool.wait_ge(S.affine, 3)
            rows(4, 0, S.in_row0)
            affine(3, S.xn_tr, 3)
            pool.wait_ge(S.affine, 4)
            rows(5, 1, S.in_row1)
            pool_tail(pool, link, affine)

        @block.tensor
        def _(pe):
            mm = nc.tensor.matmul

            def transposes(count):
                pe.wait_ge(S.xn, count)
                for k in range(KD):
                    for t in range(T):
                        last = nc.tensor.transpose(
                            psum[:, k // 2, (k % 2) * NT + t * P:(k % 2) * NT + (t + 1) * P],
                            X[:, t, k * P:(k + 1) * P], C("ident"))
                last.then_inc(S.xn_tr, 1)

            def ada(c):
                n = ada_chunk(c)
                landed_wait(pe, n)
                if c:
                    pe.wait_ge(S.mod_ev, c)
                w = ring_at(n).rearrange("p (k m q j) -> p k q m j", k=KD, m=4, q=4)
                for k in range(KD):
                    for q in range(4):
                        last = mm(psum[32 * q:32 * q + 32, 7, 0:P].rearrange("p (m j) -> p m j", m=4),
                                  csil[:, k:k + 1].broadcast_to([P, 32]), w[:, k, q],
                                  start=(k == 0), stop=(k == KD - 1))
                last.then_inc(S.used, 1)

            pe.wait_ge(S.in_cst, 16)
            transposes(1)
            pe.wait_ge(S.meta_n, 1)
            for k in range(KD):
                last = nc.tensor.transpose(psum[:, 5, k * META:(k + 1) * META], metaX[:, k * P:(k + 1) * P],
                                           C("ident")[0:META, 0:META])
            last.then_inc(S.meta_tr, 1)
            pe.wait_ge(S.silu_c, 1)
            for c in range(4):
                ada(c)

            g = 0
            pe.wait_ge(S.hT, 1)
            pe.wait_ge(S.meta_h, 1)
            for c in range(4):
                n = AT["w_in"] + c
                landed_wait(pe, n)
                w = ring_at(n).rearrange("p (k n) -> p k n", k=KD)
                wd = 416 if c == 0 else 512
                for t in range(T):
                    if g >= 6:
                        pe.wait_ge(S.pj_ev_a if g % 2 else S.pj_ev_v, (g - 6) // 2 + 1)
                    for k in range(KD):
                        last = mm(psum[:, g % 6, 0:wd], hT[:, k, META + t * P:META + (t + 1) * P], w[:, k, 0:wd],
                                  start=(k == 0), stop=(k == KD - 1))
                    if t == 0:
                        last.then_inc(S.pj_mm, 1)
                    g += 1
                last.then_inc(S.used, 1)

            ada(4)
            pe.wait_ge(S.rot, 1)
            pe.wait_ge(S.pj_ev_a, 4)
            pe.wait_ge(S.pj_ev_v, 4)
            for a in range(4):
                for t in range(T):
                    last = nc.tensor.transpose(psum[:, a // 2, (a % 2) * NT + t * P:(a % 2) * NT + (t + 1) * P],
                                               rqk[:, t, a * P:(a + 1) * P], C("ident"))
            last.then_inc(S.rqk_tr, 1)
            ada(5)
            pe.wait_ge(S.rqkT, 2)
            for t in range(T):
                for h in range(RH):
                    r = slice(64 * (h % 2), 64 * (h % 2) + 64)
                    c = (2 * t + h // 2) * P
                    last = mm(psum[:, 2 + h % 2, c:c + P], rqT[r, 2 + h // 2, t * P:(t + 1) * P],
                              rqT[r, h // 2, t * P:(t + 1) * P], start=True, stop=True)
            last.then_inc(S.rs_mm, 1)
            pe.wait_ge(S.kz, 1)
            for h in range(RH):
                r = slice(64 * (h % 2), 64 * (h % 2) + 64)
                last = mm(psum[r, 4, (h // 2) * P:(h // 2 + 1) * P], rkz[:, h, :],
                          rv[:, 0, h * P:(h + 1) * P], start=True, stop=True)
            last.then_inc(S.kv_mm, 1)
            ada(6)
            pe.wait_ge(S.sT, 2)
            pe.wait_ge(S.rS, 1)
            pe.wait_ge(S.qx, 1)
            for par in range(2):
                r = slice(64 * par, 64 * par + 64)
                for t in range(T):
                    for a in range(2):
                        h = 2 * a + par
                        o = psum[:, 5 + par, (2 * t + a) * P:(2 * t + a + 1) * P]
                        last = mm(o, rsT[:, 4 * par + 2 * t + a, :], rv[:, t, h * P:(h + 1) * P],
                                  start=True, stop=(t == 0))
                        if t == 1:
                            last = mm(o, rqx[r, a, :], rSt[r, a, :], start=False, stop=True)
                last.then_inc(S.ro_mm, 1)
            ada(7)

            pe.wait_ge(S.qn, 1)
            for a in range(3):
                for t in range(T):
                    last = nc.tensor.transpose(psum[:, a // 2, (a % 2) * NT + t * P:(a % 2) * NT + (t + 1) * P],
                                               qcn[:, t, a * P:(a + 1) * P], C("ident"))
            last.then_inc(S.qn_tr, 1)
            pe.wait_ge(S.qnT, 1)
            pe.wait_ge(S.in_uq, 16)
            for i, (t, half) in enumerate(((0, 0), (0, 1), (1, 0), (1, 1))):
                bank = (2, 3, 4, 0)[i]
                for k in range(2):
                    last = mm(psum[:, bank, 0:384], qnT[:, k, t * P:(t + 1) * P],
                              wuq[:, k, half * 384:(half + 1) * 384], start=(k == 0), stop=(k == 1))
                last.then_inc(S.uq_mm, 1)
            pe.wait_ge(S.in_ukv, 16)
            pe.wait_ge(S.ro_n, 1)
            for i in range(4):
                if i >= 2:
                    pe.wait_ge(S.kn_ev, i - 1)
                if i == 1:
                    pe.wait_ge(S.mod_ev, 8)
                bank = (1, 7)[i % 2]
                for hh in range(2):
                    h = 2 * i + hh
                    last = mm(psum[0:64, bank, hh * NT:(hh + 1) * NT], wukv[:, h * 64:(h + 1) * 64], kvnT,
                              start=True, stop=True)
                last.then_inc(S.knope, 1)
            for t in range(T):
                last = mm(b_(5 + t), kvnT[:, t * P:(t + 1) * P], wukv[:, 512:1024], start=True, stop=True)
                last.then_inc(S.knope, 1)
            pe.wait_ge(S.kn_ev, 4)
            ada(8)
            pe.wait_ge(S.rot, 2)
            pe.wait_ge(S.kn_ev, 6)
            for h in range(9):
                for t in range(T):
                    last = nc.tensor.transpose(psum[0:QK, h // 2, (h % 2) * NT + t * P:(h % 2) * NT + (t + 1) * P],
                                               qnat4[:, t, h, :], C("ident"))
            last.then_inc(S.rot_tr, 1)
            ada(9)
            pe.wait_ge(S.rotT_v, 1)
            pe.wait_ge(S.rotT_a, 1)
            for h in range(MH):
                last = mm(psum[:, 5 + h // 4, (h % 4) * P:(h % 4 + 1) * P], qT[0:QK, h, 0:P], kT[0:QK, h, 0:P],
                          start=True, stop=True)
            last.then_inc(S.sc0, 1)
            for h in range(MH):
                last = mm(psum[:, h // 2, (h % 2) * NT:(h % 2 + 1) * NT], qT[0:QK, h, P:NT], kT[0:QK, h, :],
                          start=True, stop=True)
            last.then_inc(S.sc1, 1)
            ada(10)
            pe.wait_ge(S.sm0, 1)
            for h in range(MH):
                last = nc.tensor.transpose(psum[:, 4 + h // 4, (h % 4) * P:(h % 4 + 1) * P], S0[:, h, :], C("ident"))
            last.then_inc(S.p_tr, 1)
            ada(11)
            pe.wait_ge(S.sm1, 1)
            for k in range(2):
                for h in range(MH):
                    last = nc.tensor.transpose(psum[:, 2 * k + h // 4, (h % 4) * P:(h % 4 + 1) * P],
                                               Sb[:, h, k * P:(k + 1) * P], C("ident"))
            last.then_inc(S.p_tr, 1)
            pe.wait_ge(S.p_ev, 3)
            for h in range(MH):
                r = slice(64 * (h % 2), 64 * (h % 2) + 64)
                i = h // 2
                o = psum[r, (6, 4)[i // 2], (i % 2) * NT:(i % 2 + 1) * NT]
                mm(o[:, 0:P], vN[:, 0, h * 64:(h + 1) * 64], PT[:, 0, h, :], start=True, stop=True)
                mm(o[:, P:NT], vN[:, 0, h * 64:(h + 1) * 64], PT[:, 1, h, :], start=True, stop=False)
                last = mm(o[:, P:NT], vN[:, 1, h * 64:(h + 1) * 64], PT[:, 2, h, :], start=False, stop=True)
            last.then_inc(S.pv_mm, 1)
            pe.wait_ge(S.gated, 1)
            for a in range(4):
                for t in range(T):
                    last = nc.tensor.transpose(psum[:, a // 2, (a % 2) * NT + t * P:(a % 2) * NT + (t + 1) * P],
                                               ro[:, t, a * P:(a + 1) * P], C("ident"))
            last.then_inc(S.g_tr, 1)

            def gate_rows(i):
                pe.wait_ge(S.dg, i + 1)
                for half in range(2):
                    last = mm(b_(2 * i + half), C("ones"), (dgt, dgt2)[i][:, 4 * half:4 * half + 4, :],
                              start=True, stop=True)
                last.then_inc(S.gt_mm, 1)

            pe.wait_ge(S.g_ev, 1)
            gate_rows(0)
            gate_rows(1)
            pe.wait_ge(S.mix_ev, 1)
            pe.wait_ge(S.mod2, 1)
            for half in range(2):
                n = AT["w_out"] + half
                landed_wait(pe, n)
                w = ring_at(n).rearrange("p (k n) -> p k n", k=KD)
                for t in range(T):
                    for k in range(KD):
                        last = mm(b_(4 + 2 * t + half), mixT[:, k, t * P:(t + 1) * P], w[:, k, :],
                                  start=(k == 0), stop=(k == KD - 1))
                last.then_inc(S.used, 1)
            pe.wait_ge(S.gtB, 2)
            transposes(2)
            pe.wait_ge(S.hT, 2)

            def ff1(c):
                n = AT["ffn"] + (0 if c == 0 else 2 * c - 1)
                landed_wait(pe, n)
                w = ring_at(n).rearrange("p (k n) -> p k n", k=KD)
                for m in range(4):
                    f = 4 * c + m
                    if f >= 4:
                        pe.wait_ge(S.ff_rl, f - 3)
                    for k in range(KD):
                        last = mm(psum[:, f % 4, 0:NT], w[:, k, m * P:(m + 1) * P], hT[:, k, META:L2],
                                  start=(k == 0), stop=(k == KD - 1))
                    if m < 3:
                        last.then_inc(S.ff_mm, 1)
                last.then_inc(S.used, 1)

            def ff2(c):
                n = AT["ffn"] + (15 if c == 7 else 2 * c + 2)
                landed_wait(pe, n)
                w = ring_at(n).rearrange("p (m n) -> p m n", m=4)
                for m in range(4):
                    f = 4 * c + m
                    pe.wait_ge(S.ff_sq, f + 1)
                    for t in range(T):
                        for half in range(2):
                            last = mm(b_(4 + 2 * t + half), fTr[:, f % 8, t * P:(t + 1) * P],
                                      w[:, m, half * 512:(half + 1) * 512], start=(f == 0), stop=(f == FT - 1))
                    if m < 3:
                        last.then_inc(S.y2_mm, 1)
                last.then_inc(S.used, 1)

            ff1(0)
            for c in range(1, 8):
                ff1(c)
                ff2(c - 1)
            ff2(7)
            transposes(4)
            pe_second(pe, mm, transposes)

        @block.scalar
        def _(act):
            chain = [0]

            def link(ins):
                chain[0] += 1
                ins.then_inc(S.act, 1)
                act.wait_ge(S.act, chain[0])

            def ln_sqrt(i):
                act.wait_ge(S.ln_v, i)
                nc.scalar.activation(sd, mv[:, :, 1], ACT.Sqrt, bias=epsc).then_inc(S.ln_s, 1)

            act.wait_ge(S.in_col, 16)
            nc.scalar.activation(csil, V("c"), ACT.Silu).then_inc(S.silu_c, 1)
            ln_sqrt(1)
            act.wait_ge(S.meta_v, 1)
            nc.scalar.activation(sd[0:META, 0:1], mv[0:META, 0, 1:2], ACT.Sqrt, bias=epsc[0:META]).then_inc(S.meta_s, 1)
            act.wait_ge(S.trig_r, 1)
            nc.scalar.activation(trig[:, 0:2, :], trig[:, 2:4, :], ACT.Sin).then_inc(S.trig, 1)

            dst = [pj, rqk, rv, rg]
            for c in range(4):
                act.wait_ge(S.used, AT["w_in"] + c + 1)
                wd = 416 if c == 0 else 512
                if c < 3:
                    nc.scalar.copy(dst[c][:, 1, :], psum[:, (2 * c + 1) % 6, 0:wd]).then_inc(S.pj_ev_a, 1)
                else:
                    nc.scalar.activation(rg[:, 1, :], psum[:, 1, :], ACT.Silu).then_inc(S.pj_ev_a, 1)
            act.wait_ge(S.pj_ev_v, 4)
            nc.scalar.activation(rg[:, 0, :], rg[:, 0, :], ACT.Silu).then_inc(S.rg_s, 2)
            act.wait_ge(S.pj_ev_a, 1)
            for t in range(T):
                nc.scalar.activation(Sb[:, 2 * t, :], pj[:, t, 0:QR], ACT.Square, accum_out=ssq[:, t:t + 1])
                ins = nc.scalar.activation(Sb[:, 2 * t + 1, 0:KVR], pj[:, t, QR:QR + KVR], ACT.Square,
                                           accum_out=ssq[:, 2 + t:3 + t])
                link(ins)
            link(nc.scalar.activation(rq[:, 0:2], ssq[:, 0:2], ACT.Sqrt, bias=epsc, scale=1.0 / QR))
            nc.scalar.activation(rq[:, 2:4], ssq[:, 2:4], ACT.Sqrt, bias=epsc, scale=1.0 / KVR).then_inc(S.rms_sq, 1)
            act.wait_ge(S.rqk_tr, 1)
            nc.scalar.copy(rqT[:, 2:4, :], b_(1)).then_inc(S.rqkT, 1)
            act.wait_ge(S.kv_mm, 1)
            nc.scalar.copy(rSt[:, :, :], psum[:, 4, 0:256]).then_inc(S.rS, 1)
            act.wait_ge(S.ln_v, 2)
            nc.scalar.activation(gsd, gmv[:, :, 1], ACT.Sqrt, bias=epsc).then_inc(S.ln_s, 1)
            for i in range(4):
                act.wait_ge(S.knope, i + 1)
                nc.scalar.copy(kT[0:64, 2 * i:2 * i + 2, :], psum[0:64, (1, 7)[i % 2], :]).then_inc(S.kn_ev, 1)
            for t in range(T):
                act.wait_ge(S.knope, 5 + t)
                nc.scalar.copy(vN[:, t, :], b_(5 + t)).then_inc(S.kn_ev, 1)
            act.wait_ge(S.rot_tr, 1)
            nc.scalar.copy(kT[64:QK, :, :], psum[64:QK, 4:5, 0:NT].broadcast_to([32, MH, NT])).then_inc(S.rotT_a, 1)
            for t, (buf, w) in enumerate(((S0, P), (Sb, NT))):
                act.wait_ge(S.nm0 if t == 0 else S.nm1, 1)
                for h in range(MH):
                    last = nc.scalar.activation(buf[:, h, :], buf[:, h, :], ACT.Exp,
                                                bias=nmax[:, 8 * t + h:8 * t + h + 1],
                                                accum_out=rsum[:, 8 * t + h:8 * t + h + 1])
                last.then_inc(S.ex0 if t == 0 else S.ex1, 1)
            act.wait_ge(S.p_tr, 2)
            nc.scalar.copy(PT[:, 1, :, :], psum[:, 0:2, :].rearrange("p a b -> p (a b)")).then_inc(S.p_ev, 1)
            act.wait_ge(S.pv_mm, 1)
            nc.scalar.copy(mixT[:, 0:2, :], b_(6)).then_inc(S.mix_ev, 1)
            for i in range(2):
                act.wait_ge(S.gt_mm, i + 1)
                nc.scalar.copy(gtB[:, i, :], psum[:, 2 * i:2 * i + 2, :].rearrange("p a b -> p (a b)"))\
                    .then_inc(S.gtB, 1)
            ln_sqrt(3)
            for f in range(FT):
                if f % 4 < 3:
                    act.wait_ge(S.ff_mm, 3 * (f // 4) + f % 4 + 1)
                else:
                    c = f // 4
                    act.wait_ge(S.used, AT["ffn"] + (0 if c == 0 else 2 * c - 1) + 1)
                if f >= 4:
                    act.wait_ge(S.ff_sq, f - 3)
                nc.scalar.activation(frl[:, f % 4, :], psum[:, f % 4, 0:NT], ACT.Relu).then_inc(S.ff_rl, 1)
            ln_sqrt(4)
            ln_sqrt(5)
            act_second(act, link, ln_sqrt)

        @block.vector
        def _(dve):
            chain = [0]

            def link(ins):
                chain[0] += 1
                ins.then_inc(S.dve, 1)
                dve.wait_ge(S.dve, chain[0])

            v = nc.vector

            def layer_norm(count, sem_count):
                for t in range(T):
                    for n in range(2):
                        last = v.bn_stats(stat[:, t, n, :], X[:, t, n * 512:(n + 1) * 512])
                link(last)
                for t in range(T):
                    last = v.bn_aggr(mv[:, t, :], stat[:, t, :, :].rearrange("p n s -> p (n s)"))
                last.then_inc(S.ln_v, 1)
                dve.wait_ge(S.ln_s, sem_count)
                link(v.reciprocal(rstd, sd))
                for t in range(T):
                    last = v.tensor_scalar(X[:, t, :], X[:, t, :], mv[:, t, 0:1], rstd[:, t:t + 1],
                                           ALU.subtract, ALU.mult)
                last.then_inc(S.xn, 1)

            def to_hT(tr_count, A1=A1, B1=B1):
                dve.wait_ge(S.xn_tr, tr_count)
                for k in range(KD):
                    last = v.tensor_scalar(hT[:, k, META:L2], psum[:, k // 2, (k % 2) * NT:(k % 2 + 1) * NT],
                                           A1[:, k:k + 1], B1[:, k:k + 1], ALU.mult, ALU.add)
                last.then_inc(S.hT, 1)

            link(v.memset(epsc, EPS))
            dve.wait_ge(S.in_x, 16)
            layer_norm(1, 1)
            dve.wait_ge(S.in_meta, 16)
            dve.wait_ge(S.xn, 1)
            for n in range(2):
                last = v.bn_stats(stat[0:META, 0, n, :], metaX[:, n * 512:(n + 1) * 512])
            link(last)
            v.bn_aggr(mv[0:META, 0, :], stat[0:META, 0, :, :].rearrange("p n s -> p (n s)")).then_inc(S.meta_v, 1)
            dve.wait_ge(S.meta_s, 1)
            link(v.reciprocal(rstd[0:META, 0:1], sd[0:META, 0:1]))
            v.tensor_scalar(metaX, metaX, mv[0:META, 0, 0:1], rstd[0:META, 0:1],
                            ALU.subtract, ALU.mult).then_inc(S.meta_n, 1)
            dve.wait_ge(S.in_pos, 16)
            dve.wait_ge(S.in_cst, 16)
            link(v.tensor_copy(posf, posi[:, :]))
            ang, kk, red = scr[:, 0:64], scr[:, 64:192].rearrange("p (a b) -> p a b", a=2), trig[:, 2:4, :]
            for t in range(T):
                last = v.tensor_scalar(ang[:, t * 32:(t + 1) * 32], C("inv"), posf[:, t:t + 1], None, ALU.mult)
            link(last)
            R = 12582912.0
            for a, turn in ((0, 0.25), (1, 0.0)):
                link(v.tensor_scalar(kk[:, a, :], ang, float(1.0 / (2 * np.pi)), turn, ALU.mult, ALU.add))
                link(v.tensor_scalar(kk[:, a, :], kk[:, a, :], R, None, ALU.add))
                link(v.tensor_scalar(kk[:, a, :], kk[:, a, :], R, None, ALU.subtract))
                c1 = 6.28125
                c2 = float((np.float32(2 * np.pi - c1).view(np.uint32) & np.uint32(0xFFFFF000)).view(np.float32))
                c3 = float(2 * np.pi - c1 - c2)
                link(v.scalar_tensor_tensor(red[:, a, :], kk[:, a, :], -c1, ang, ALU.mult, ALU.add))
                link(v.scalar_tensor_tensor(red[:, a, :], kk[:, a, :], -c2, red[:, a, :], ALU.mult, ALU.add))
                link(v.scalar_tensor_tensor(red[:, a, :], kk[:, a, :], -c3, red[:, a, :], ALU.mult, ALU.add))
                if a == 0:
                    link(v.tensor_scalar(red[:, a, :], red[:, a, :], float(np.pi / 2), None, ALU.add))
            pi = 3.1415925
            v.tensor_scalar(red, red, pi, -pi, ALU.min, ALU.max).then_inc(S.trig_r, 1)
            dve.wait_ge(S.in_col, 16)
            dve.wait_ge(S.meta_tr, 1)
            for k in range(KD):
                last = v.tensor_scalar(hT[:, k, 0:META], psum[:, 5, k * META:(k + 1) * META], V("ge", k, k + 1),
                                       V("be", k, k + 1), ALU.mult, ALU.add)
            last.then_inc(S.meta_h, 1)

            def take(c):
                dve.wait_ge(S.used, ada_chunk(c) + 1)
                link(v.tensor_tensor(diag, psum[:, 7, 0:P].rearrange("p (m j) -> p m j", m=4),
                                     C("eye32").unsqueeze(1).broadcast_to([P, 4, 32]), ALU.mult))
                last = v.tensor_reduce(modc[:, 4 * c:4 * c + 4], diag, AX, ALU.add)
                last.then_inc(S.mod_ev, 1)

            for c in range(4):
                take(c)
            dve.wait_ge(S.mod_ev, 4)
            link(v.tensor_tensor(modc[:, 0:16], modc[:, 0:16], V("b_ada", 0, 16), ALU.add))
            link(v.tensor_scalar(modc[:, 8:16], modc[:, 8:16], 1.0, None, ALU.add))
            link(v.tensor_tensor(A1, modc[:, 8:16], V("g0"), ALU.mult))
            link(v.tensor_tensor(B1, modc[:, 8:16], V("b0"), ALU.mult))
            v.tensor_tensor(B1, B1, modc[:, 0:8], ALU.add).then_inc(S.mod1, 1)
            dve.wait_ge(S.mod1, 1)
            to_hT(1)
            dst = [pj, rqk, rv, rg]
            for c in range(4):
                dve.wait_ge(S.pj_mm, c + 1)
                wd = 416 if c == 0 else 512
                v.tensor_copy(dst[c][:, 0, :], psum[:, (2 * c) % 6, 0:wd]).then_inc(S.pj_ev_v, 1)

            def rotary(x, heads, half, step, tmp_a, tmp_b):
                x1, x2 = x[:, :, :, 0:half], x[:, :, :, half:2 * half]
                for t in range(T):
                    cb = cosT[:, t:t + 1, 0:32:step].broadcast_to([P, heads, half])
                    sb_ = sinT[:, t:t + 1, 0:32:step].broadcast_to([P, heads, half])
                    a = tmp_a[:, 0:heads * half].rearrange("p (h d) -> p h d", d=half)
                    b = tmp_a[:, heads * half:2 * heads * half].rearrange("p (h d) -> p h d", d=half)
                    c = tmp_b[:, 0:heads * half].rearrange("p (h d) -> p h d", d=half)
                    d = tmp_b[:, heads * half:2 * heads * half].rearrange("p (h d) -> p h d", d=half)
                    v.tensor_tensor(a, x1[:, t], cb, ALU.mult)
                    v.tensor_tensor(b, x2[:, t], sb_, ALU.mult)
                    v.tensor_tensor(c, x2[:, t], cb, ALU.mult)
                    link(v.tensor_tensor(d, x1[:, t], sb_, ALU.mult))
                    v.tensor_tensor(x1[:, t], a, b, ALU.subtract)
                    last = v.tensor_tensor(x2[:, t], c, d, ALU.add)
                    if t == 0:
                        link(last)
                return last

            dve.wait_ge(S.trig, 1)
            dve.wait_ge(S.pj_ev_a, 2)
            dve.wait_ge(S.pj_ev_v, 2)
            tA, tB = rtmp[:, 0].rearrange("p t w -> p (t w)"), rtmp[:, 1].rearrange("p t w -> p (t w)")
            rotary(rqk[:, :, :].rearrange("p t (h d) -> p t h d", d=64), 8, 32, 1, tA, tB).then_inc(S.rot, 1)
            take(4)
            dve.wait_ge(S.rot, 1)
            v.tensor_tensor(rkz[:, :, :], rqk[:, 0, 256:512].rearrange("p (h d) -> p h d", d=64),
                            C("zeta").unsqueeze(2).broadcast_to([P, RH, RDK]), ALU.mult).then_inc(S.kz, 1)
            dve.wait_ge(S.rqk_tr, 1)
            v.tensor_copy(rqT[:, 0:2, :], b_(0).rearrange("p (a b) -> p a b", a=2)).then_inc(S.rqkT, 1)
            take(5)
            dve.wait_ge(S.rqkT, 2)
            v.tensor_tensor(rqx[:, :, :], rqT[:, 0:2, P:NT], C("xi").rearrange("p (a b) -> p a b", a=2),
                            ALU.mult).then_inc(S.qx, 1)
            dve.wait_ge(S.rs_mm, 1)
            for t in range(T):
                v.tensor_tensor(rsT[:, 4 * t:4 * t + 4, :].rearrange("p (t a) b -> p t (a b)", t=T),
                                b_(2 + t).rearrange("p (t w) -> p t w", t=T),
                                C("decay", 256 * t, 256 * t + 256).unsqueeze(1).broadcast_to([P, T, 256]),
                                ALU.mult).then_inc(S.sT, 1)
            take(6)
            dve.wait_ge(S.rms_sq, 1)
            link(v.reciprocal(rq, rq))
            for t in range(T):
                v.tensor_scalar(qcn[:, t, 0:QR], pj[:, t, 0:QR], rq[:, t:t + 1], None, ALU.mult)
                last = v.tensor_scalar(qcn[:, t, QR:384], pj[:, t, QR:384], rq[:, 2 + t:3 + t], None, ALU.mult)
            last.then_inc(S.qn, 1)
            for par in range(2):
                dve.wait_ge(S.ro_mm, par + 1)
                for n in range(4):
                    last = v.bn_stats(gst[:, 4 * par + n, :], psum[:, 5 + par, n * P:(n + 1) * P])
            link(last)
            for i in range(8):
                last = v.bn_aggr(gmv[:, i, :], gst[:, i, :])
            last.then_inc(S.ln_v, 1)
            dve.wait_ge(S.ln_s, 2)
            link(v.reciprocal(grs, gsd))
            for i in range(8):
                par, t, a = i // 4, i // 2 % 2, i % 2
                h = 2 * a + par
                last = v.tensor_scalar(ro[:, t, h * P:(h + 1) * P], psum[:, 5 + par, (i % 4) * P:(i % 4 + 1) * P],
                                       gmv[:, i, 0:1], grs[:, i:i + 1], ALU.subtract, ALU.mult)
            last.then_inc(S.ro_n, 1)
            take(7)
            dve.wait_ge(S.qn_tr, 1)
            for k in range(2):
                v.tensor_scalar(qnT[:, k, :], psum[:, 0, k * NT:(k + 1) * NT], V("qg", k, k + 1), None, ALU.mult)
            v.tensor_scalar(kvnT, psum[:, 1, 0:NT], V("kvg"), None, ALU.mult).then_inc(S.qnT, 1)
            link(v.memset(qnat4[:, :, 8, 0:64], 0.0))
            link(v.tensor_copy(qnat4[:, :, 8, 64:QK], pj[:, :, 384:416]))
            for i, (t, half) in enumerate(((0, 0), (0, 1), (1, 0), (1, 1))):
                bank = (2, 3, 4, 0)[i]
                dve.wait_ge(S.uq_mm, i + 1)
                last = v.tensor_copy(qnat4[:, t, 4 * half:4 * half + 4, :],
                                     psum[:, bank, 0:384].rearrange("p (h d) -> p h d", d=QK))
            link(last)
            rotary(qnat4[:, :, :, 64:QK], 9, 16, 2, tA, tB).then_inc(S.rot, 1)
            take(8)
            dve.wait_ge(S.rot_tr, 1)
            for i in range(4):
                last = v.tensor_copy(qT[0:QK, 2 * i:2 * i + 2, :],
                                     psum[0:QK, i, :].rearrange("p (a b) -> p a b", a=2))
            last.then_inc(S.rotT_v, 1)
            take(9)
            scale = QK ** -0.5
            mask = C("causal").unsqueeze(1).broadcast_to([P, 4, P])
            dve.wait_ge(S.sc0, 1)
            for a in range(2):
                last = v.scalar_tensor_tensor(S0[:, 4 * a:4 * a + 4, :], b_(5 + a).rearrange("p (h k) -> p h k", k=P),
                                              scale, mask, ALU.mult, ALU.add)
            link(last)
            link(v.tensor_reduce(nmax[:, 0:8], S0[:, :, :], AX, ALU.max))
            v.tensor_scalar(nmax[:, 0:8], nmax[:, 0:8], -1.0, None, ALU.mult).then_inc(S.nm0, 1)
            dve.wait_ge(S.sc1, 1)
            mask2 = C("causal").unsqueeze(1).broadcast_to([P, 2, P])
            for a in range(4):
                src = b_(a).rearrange("p (h k) -> p h k", k=NT)
                v.tensor_scalar(Sb[:, 2 * a:2 * a + 2, 0:P], src[:, :, 0:P], scale, None, ALU.mult)
                last = v.scalar_tensor_tensor(Sb[:, 2 * a:2 * a + 2, P:NT], src[:, :, P:NT], scale, mask2,
                                              ALU.mult, ALU.add)
            link(last)
            link(v.tensor_reduce(nmax[:, 8:16], Sb[:, :, :], AX, ALU.max))
            v.tensor_scalar(nmax[:, 8:16], nmax[:, 8:16], -1.0, None, ALU.mult).then_inc(S.nm1, 1)
            take(10)
            for t, (buf, w) in enumerate(((S0, P), (Sb, NT))):
                dve.wait_ge(S.ex0 if t == 0 else S.ex1, 1)
                link(v.reciprocal(rinv[:, 8 * t:8 * t + 8], rsum[:, 8 * t:8 * t + 8]))
                v.tensor_tensor(buf[:, :, :], buf[:, :, :],
                                rinv[:, 8 * t:8 * t + 8].unsqueeze(2).broadcast_to([P, MH, w]),
                                ALU.mult).then_inc(S.sm0 if t == 0 else S.sm1, 1)
            dve.wait_ge(S.p_tr, 1)
            v.tensor_copy(PT[:, 0, :, :], psum[:, 4:6, :].rearrange("p a (b c) -> p (a b) c", c=P)).then_inc(S.p_ev, 1)
            dve.wait_ge(S.p_tr, 2)
            v.tensor_copy(PT[:, 2, :, :], psum[:, 2:4, :].rearrange("p a (b c) -> p (a b) c", c=P)).then_inc(S.p_ev, 1)
            take(11)
            dve.wait_ge(S.pv_mm, 1)
            v.tensor_copy(mixT[:, 2:4, :], b_(4).rearrange("p (a b) -> p a b", a=2))
            dve.wait_ge(S.g_tr, 1)
            v.tensor_copy(mixT[:, 4:8, :], psum[:, 0:2, :].rearrange("p a (b c) -> p (a b) c", c=NT)).then_inc(S.g_ev, 1)
            dve.wait_ge(S.mod_ev, 12)
            v.tensor_tensor(modc[:, 16:48], modc[:, 16:48], V("b_ada", 16, 48), ALU.add).then_inc(S.mod2, 1)
            dve.wait_ge(S.mod2, 1)

            def gate_diag(first, dgt):
                for k in range(KD):
                    last = v.tensor_scalar(dgt[:, k, :], C("ident"), modc[:, first + k:first + k + 1], None, ALU.mult)
                last.then_inc(S.dg, 1)

            gate_diag(16, dgt)
            gate_diag(40, dgt2)
            link(v.tensor_scalar(modc[:, 32:40], modc[:, 32:40], 1.0, None, ALU.add))
            link(v.tensor_tensor(A1, modc[:, 32:40], V("g1"), ALU.mult))
            link(v.tensor_tensor(B1, modc[:, 32:40], V("b1"), ALU.mult))
            link(v.tensor_tensor(B1, B1, modc[:, 24:32], ALU.add))

            def residual(gate, affine_count):
                dve.wait_ge(S.affine, affine_count)
                for t in range(T):
                    for half in range(2):
                        f = slice(half * 512, (half + 1) * 512)
                        y = b_(4 + 2 * t + half)
                        if gate is not None:
                            link(v.tensor_tensor(Sb2[:, t, f], y, gtB[:, gate, f], ALU.mult))
                            y = Sb2[:, t, f]
                        last = v.scalar_tensor_tensor(X[:, t, f], X[:, t, f], ALPHA, y, ALU.mult, ALU.add)
                link(last)

            Sb2 = arena(14000, T, DM)
            dve.wait_ge(S.used, AT["w_out"] + 2)
            dve.wait_ge(S.gtB, 2)
            residual(0, 1)
            layer_norm(2, 3)
            to_hT(2)
            dve.wait_ge(S.used, AT["dn_qkv"])
            residual(1, 2)
            layer_norm(3, 4)
            dve.wait_ge(S.affine, 3)
            layer_norm(4, 5)
            to_hT(3, V("ge"), V("be"))
            dve_second(dve, v, link, residual, layer_norm, to_hT)



def lay_out(i):
    f = np.float32
    d = {"x": i["x"][0], "pos": np.ascontiguousarray(i["positions"][0].reshape(T, P).T)}
    stream = np.zeros((AT["end"], P, CH), f)

    def by_k(w):
        o = np.zeros((P, KD, 512), f)
        o[:, :, :w.shape[1]] = w.reshape(KD, P, -1).transpose(1, 0, 2)
        return o.reshape(P, CH)

    ada = i["w_ada"][0]
    for n in range(4):
        stream[AT["ada_h1"] + n] = by_k(ada[:, n * 512:(n + 1) * 512])
    for n in range(8):
        stream[AT["ada_rest"] + n] = by_k(ada[:, 2048 + n * 512:2048 + (n + 1) * 512])
    w = i["w_in"][0]
    for n, (a, b) in enumerate(((0, 416), (416, 928), (928, 1440), (1440, 1952))):
        stream[AT["w_in"] + n] = by_k(w[:, a:b])
    for n in range(2):
        stream[AT["w_out"] + n] = by_k(i["w_out"][0][:, n * 512:(n + 1) * 512])
        stream[AT["w_out2"] + n] = by_k(i["w_out_2"][0][:, n * 512:(n + 1) * 512])
    for c in range(8):
        stream[AT["ffn"] + (0 if c == 0 else 2 * c - 1)] = by_k(i["w_ff1"][0][:, c * 512:(c + 1) * 512])
        stream[AT["ffn"] + (15 if c == 7 else 2 * c + 2)] = \
            i["w_ff2"][0][c * 512:(c + 1) * 512].reshape(4, P, DM).transpose(1, 0, 2).reshape(P, CH)
    w = i["w_in_2"][0]
    for n in range(3):
        stream[AT["dn_qkv"] + n] = by_k(w[:, n * 512:(n + 1) * 512])
        stream[AT["sb_qkv"] + n] = by_k(w[:, 2056 + n * 512:2056 + (n + 1) * 512])
    stream[AT["dn_z"]] = by_k(w[:, 1536:2048])
    for n in range(4):
        stream[AT["gates"] + n] = by_k(w[:, 3592 + n * 512:3592 + (n + 1) * 512])
    for n, k in enumerate(("w_branch_dn_2", "w_branch_sb_2")):
        stream[AT["branch"] + n] = i[k][0].reshape(4, P, DM).transpose(1, 0, 2).reshape(P, CH)
    wg, wu, wd = (i[k][0].reshape(NE, a, b) for k, a, b in
                  (("expert_w_gate_2", DM, EF), ("expert_w_up_2", DM, EF), ("expert_w_down_2", EF, DM)))
    for e in range(NE):
        s = stream[gate_chunk(e)].reshape(P, KD, 2, EF)
        s[:, :, 0] = wg[e].reshape(KD, P, EF).transpose(1, 0, 2)
        s[:, :, 1] = wu[e].reshape(KD, P, EF).transpose(1, 0, 2)
        s = stream[down_chunk(e)].reshape(P, 2, 2, DM)
        s[:, e % 2] = wd[e].reshape(2, P, DM).transpose(1, 0, 2)
    d["stream"] = stream
    colsrc = dict(g0="ln_in_g", b0="ln_in_b", g1="ln1_g", b1="ln1_b", ge="ln_emb_g_2", be="ln_emb_b_2",
                  g3="ln1_g_2", b3="ln1_b_2", b_ada="b_ada", qg="mla_q_norm", kvg="mla_kv_norm",
                  b_gate="b_gate_2", c="c")
    cols = np.zeros((P, COLS["end"][0]), f)
    for name, (o, k) in COLS.items():
        if name == "end":
            continue
        if name == "conv":
            a = i["dn_conv_w_2"][0].reshape(4, 12, P).transpose(2, 1, 0).reshape(P, 48)
        else:
            a = i[colsrc[name]].reshape(k, P).T
        cols[:, o:o + k] = a
    d["cols"] = cols
    d["consts"] = const_array()
    d["rows"] = np.stack([np.stack([i[a].reshape(DM), i[b].reshape(DM)]) for a, b in
                          (("ln_in_g", "ln_in_b"), ("ln1_g", "ln1_b"), ("ln2_g", "ln2_b"),
                           ("ln_emb_g_2", "ln_emb_b_2"), ("ln1_g_2", "ln1_b_2"), ("ln2_g_2", "ln2_b_2"))])
    d["gn"] = np.stack([i["ret_gn_g"][0], i["ret_gn_b"][0]])
    d["w_uq"] = i["w_uq"][0].reshape(2, P, 768).transpose(1, 0, 2)
    ukv = i["w_ukv"][0].reshape(P, MH, 128)
    d["w_ba"] = i["w_in_2"][0][:, 2048:2056].reshape(KD, P, 8).transpose(1, 0, 2).reshape(P, 64)
    d["dn_rows"] = np.concatenate([i["dn_a_log_2"][0], i["dn_dt_bias_2"][0]])
    d["dn_g"] = i["dn_norm_g_2"][0]
    d["meta"] = i["meta_tokens_2"]
    d["router_w"] = np.concatenate([i["router_group_w_2"][0]] + [i["router_expert_w_2"][0][g] for g in range(4)], 1).reshape(KD, P, 36).transpose(1, 0, 2).reshape(P, 288)
    d["router_b"] = np.concatenate([i["router_group_b_2"][0], i["router_expert_b_2"][0].reshape(32)])
    d["w_ukv"] = np.concatenate([ukv[:, :, :64].reshape(P, 512), ukv[:, :, 64:].reshape(P, 512)], 1)
    return d


def kernel(**inputs):
    import concourse.bacc as bacc
    from concourse.bass_utils import run_bass_kernel_spmd

    nc = bacc.Bacc("TRN2", target_bir_lowering=False, num_devices=1)
    arrays, IN = {}, {}
    for name, a in lay_out({k: np.asarray(v) for k, v in inputs.items()}).items():
        a = np.ascontiguousarray(a)
        arrays["in_" + name] = a
        IN[name] = nc.dram_tensor("in_" + name, a.shape, mybir.dt.from_np(a.dtype), kind="ExternalInput").ap()
    out = nc.dram_tensor("out_dram", (NT, DM), F32, kind="ExternalOutput").ap()

    build(nc, IN, out)
    r = run_bass_kernel_spmd(nc, [arrays], core_ids=[0])
    return r.results[0]["out_dram"].reshape(1, NT, DM)
```

```python
from collections import namedtuple
from contextlib import ExitStack

import numpy as np
import concourse.bass as bass
from concourse import mybir

ALU = mybir.AluOpType
ACT = mybir.ActivationFunctionType
AX = mybir.AxisListType.X
F32 = mybir.dt.float32
I32 = mybir.dt.int32

P = 128
DM = 1024
KD = DM // P
T = 2
NT = T * P
EPS = 1e-5
ALPHA = 2.0 ** 0.25
NEG = -1.0e30

QR, KVR, ROPE = 256, 128, 32
MH, NOPE, MV = 8, 64, 64
QK = NOPE + ROPE
RH, RDK, RDV = 4, 64, 128
FF = 4096
FT = FF // P

CH = 4096
RING = 5

META = 16
L2 = META + NT
DH, DD = 4, 128
SH, SD = 8, 64
NE, EF = 32, 256
CAP = 64
RMS_EPS = 1e-6


def chunk_plan():
    at, n = {}, 0
    for name, k in (("ada_h1", 4), ("w_in", 4), ("ada_rest", 8), ("w_out", 2), ("ffn", 16),
                    ("dn_qkv", 3), ("sb_qkv", 3), ("dn_z", 1), ("gates", 4), ("branch", 2), ("w_out2", 2),
                    ("experts", NE * 3 // 2)):
        at[name] = n
        n += k
    at["end"] = n
    return at


AT = chunk_plan()


def gate_chunk(e):
    return AT["experts"] + 3 * (e // 2) + e % 2


def down_chunk(e):
    return AT["experts"] + 3 * (e // 2) + 2


def ada_chunk(c):
    return AT["ada_h1"] + c if c < 4 else AT["ada_rest"] + c - 4


COLS = {}


def _cols():
    n = 0
    for name, k in (("g0", 8), ("b0", 8), ("g1", 8), ("b1", 8), ("ge", 8), ("be", 8), ("g3", 8), ("b3", 8),
                    ("b_ada", 48), ("qg", 2), ("kvg", 1), ("conv", 48), ("b_gate", 16), ("c", 8)):
        COLS[name] = (n, k)
        n += k
    COLS["end"] = (n, 0)


_cols()

CONST = {}


def _consts():
    n = 0
    for name, k in (("ident", P), ("ones", P), ("causal", P), ("decay", RH * P), ("xi", 2 * P), ("zeta", RH),
                    ("inv", RDK // 2), ("ucum", P), ("strict", P), ("m16", P), ("off16", P), ("causT", P),
                    ("sbmul", P), ("sbadd", P), ("tri", P), ("tie", 8), ("iota", CAP), ("eye32", 32)):
        CONST[name] = (n, k)
        n += k
    CONST["end"] = (n, 0)


_consts()

LN_ROWS = ("ln0", "ln1", "ln2", "emb", "ln3", "ln4")


def const_array():
    c = np.zeros((P, CONST["end"][0]), np.float32)
    p = np.arange(P)[:, None]
    f = np.arange(P)[None, :]

    def put(name, a):
        o, k = CONST[name]
        c[:, o:o + k] = a

    put("ident", p == f)
    put("ones", 1.0)
    put("causal", np.where(f <= p, 0.0, NEG))
    lg = np.log(1.0 - 2.0 ** (-5.0 - np.arange(RH)))
    sc = RDK ** -0.5
    put("decay", np.concatenate([np.where(f >= p, np.exp(lg[h] * np.maximum(f - p, 0)), 0.0) * sc
                                 for h in (0, 2, 1, 3)], 1))
    put("xi", np.concatenate([np.exp(lg[2 * a + p // 64] * (f + 1.0)) for a in range(2)], 1))
    put("zeta", np.exp(lg[None, :] * (P - 1 - p)) * sc)
    put("inv", 10000.0 ** (-np.arange(RDK // 2)[None, :] / (RDK // 2)) * np.ones((P, 1)))
    same = (p // 64) == (f // 64)
    same16 = (p // 16) == (f // 16)
    put("ucum", (p <= f) & same)
    put("strict", (f < p) & same)
    put("m16", np.where((f < p) & same16, -1.0, 0.0))
    put("off16", (f < p) & same & ~same16)
    put("causT", (f >= p) & same)
    put("sbmul", p < f)
    put("sbadd", np.where(p < f, 0.0, NEG))
    put("tri", p >= f)
    put("tie", np.arange(8, 0, -1)[None, :])
    put("eye32", p % 32 == np.arange(32)[None, :])
    put("iota", np.arange(CAP)[None, :])
    return c


def build(nc, IN, out):
    ctx = ExitStack()
    with ctx:
        def sb(name, shape, dt=F32):
            return ctx.enter_context(nc.sbuf_tensor(name, shape, dt))

        names = """
            landed5 landed0 landed1 landed2 landed3 landed4 used in_x in_cst in_col in_row0 in_row1
            in_pos in_uq in_ukv in_gn silu_c xn xn_tr affine hT mod1 mod2 pj_mm pj_ev_a pj_ev_v
            rms_sq qn qn_tr qnT uq_mm rot rot_tr rotT_a rotT_v knope kn_ev sc0 sc1 sm0 sm1 ex0 ex1
            nm0 nm1 p_tr p_ev pv_mm mix_ev trig_r trig rqk_tr rqkT rs_mm sT kz kv_mm rS qx ro_mm
            ro_n rg_s gated g_tr g_ev dg gt_mm gtB ff_mm ff_rl ff_sq y2_mm out_done dve act pool
            ln_s ln_v in_meta meta_v meta_s meta_n meta_tr meta_h in_ba in_dn g2_mm g2_ev conv cvs
            ba_mm ba_ev sq nsq nr nrmd side_ev br_mm mg mgd z1 zc ze zl zk zm za zw zo zov lg_mm cmb
            cT cTv cB_mm cB_ev eg eu hid d_mm rt_e rt_x in_rt be_e ug R_mm E01 ex01 knt vnt kv_ev
            gram ab n1t rd_mm rd_v rd_a u_mm uv wv s_mm sv vn_mm vn_v o_mm o_v os orv on on_tr
            mod_ev flag sel xg xgv sct yv
            """.split()
        S = namedtuple("Semaphores", names)(*[ctx.enter_context(nc.semaphore("s_" + n)) for n in names])
        landed = [S.landed0, S.landed1, S.landed2, S.landed3, S.landed4, S.landed5]

        psum = ctx.enter_context(nc.psum_tensor("psum", [P, 8, 512], F32))

        ring = sb("ring", [P, RING, CH])
        cst = sb("cst", [P, CONST["end"][0]])
        col = sb("col", [P, COLS["end"][0]])
        rowB = sb("rowB", [P, 2, 2, DM])
        gnB = sb("gnB", [P, 2, RH * RDV])
        X = sb("X", [P, T, DM])
        hT = sb("hT", [P, KD, L2])
        small = sb("small", [P, 336])
        modc = sb("modc", [P, 48])
        SCR = 19456
        scr = sb("scr", [P, SCR])

        def C(name, a=0, b=None):
            o, k = CONST[name]
            return cst[:, o + a:o + (k if b is None else b)]

        def V(name, a=0, b=None):
            o, k = COLS[name]
            return col[:, o + a:o + (k if b is None else b)]

        def arena(off, *shape):
            n = int(np.prod(shape))
            assert off + n <= SCR, (off, n)
            a = scr[:, off:off + n]
            if len(shape) == 2:
                return a.rearrange("p (a b) -> p a b", b=shape[1])
            if len(shape) == 3:
                return a.rearrange("p (a b c) -> p a b c", b=shape[1], c=shape[2])
            return a

        stat = small[:, 0:24].rearrange("p (t n s) -> p t n s", t=2, s=6)
        mv = small[:, 24:28].rearrange("p (t s) -> p t s", s=2)
        rstd = small[:, 28:30]
        sd = small[:, 30:32]
        csil = small[:, 32:40]
        epsc = small[:, 40:41]
        ssq = small[:, 42:46]
        rq = small[:, 46:50]
        posf = small[:, 52:54]
        diag = small[:, 208:336].rearrange("p (m j) -> p m j", m=4)
        A1 = small[:, 56:64]
        B1 = small[:, 64:72]
        nmax = small[:, 80:96]
        rsum = small[:, 96:112]
        rinv = small[:, 112:128]
        gst = small[:, 128:128 + 48].rearrange("p (n s) -> p n s", s=6)
        gmv = small[:, 176:192].rearrange("p (n s) -> p n s", s=2)
        grs = small[:, 192:200]
        gsd = small[:, 200:208]
        posi = sb("posi", [P, T], I32)

        pj = arena(0, T, 416)
        rqk = arena(832, T, 512)
        rv = arena(1856, T, 512)
        rg = arena(2880, T, 512)
        qnat = arena(3904, T * 9, QK)
        qnat4 = scr[:, 3904:3904 + T * 9 * QK].rearrange("p (t h d) -> p t h d", t=T, d=QK)
        qT = arena(5632, MH, NT)
        kT = arena(7680, MH, NT)
        vN = arena(9728, T, 512)
        mixT = arena(10752, KD, NT)
        Sb = arena(12800, MH, NT)
        S0 = arena(14848, MH, P)
        PT = scr[:, 15872:15872 + 3072].rearrange("p (k h q) -> p k h q", k=3, h=MH)
        qcn = arena(12800, T, 384)
        qnT = arena(13568, 2, NT)
        kvnT = arena(14080, NT)
        wuq = arena(15872, 2, 768)
        wukv = arena(17408, 1024)
        trig = arena(18944, 4, 64)
        cosT = trig[:, 0, :].rearrange("p (t f) -> p t f", t=T)
        sinT = trig[:, 1, :].rearrange("p (t f) -> p t f", t=T)
        rtmp = scr[:, 14848:15872].rearrange("p (n t w) -> p n t w", n=2, t=T)
        rqT = arena(5632, 4, NT)
        rsT = arena(6656, 8, P)
        rqx = arena(7680, 2, P)
        rkz = arena(7936, RH, RDK)
        rSt = arena(8192, 2, P)
        ro = arena(832, T, 512)
        dgt = arena(12800, KD, P)
        dgt2 = arena(16000, KD, P)
        gtB = arena(0, 2, DM)
        fTr = arena(2048, 8, NT)
        frl = arena(4096, 4, NT)
        metaX = scr[0:META, 12800:12800 + DM]

        raw = arena(0, 12, 3 + L2)
        cv = arena(3300, 12, L2)
        sbT = arena(6564, 8, L2)
        sbv = arena(8740, 3, 512)
        M = [arena(10276 + 1088 * n, 1088) for n in range(7)]
        vb = arena(0, 3, 512)
        kdec = arena(1536, 3, 512)
        kbe = arena(17892, 3, 512)
        sqr = arena(0, 8, L2)
        nrm = arena(10276, 8, L2)
        sm2 = sb("sm2", [P, 400])
        ba = sm2[:, 0:24].rearrange("p (t n) -> p t n", t=3)
        wba = sm2[:, 24:88].rearrange("p (k n) -> p k n", k=KD)
        beta = sm2[:, 88:100].rearrange("p (t n) -> p t n", t=3)
        gdn = sm2[:, 100:112].rearrange("p (t n) -> p t n", t=3)
        dN = sm2[:, 112:124].rearrange("p (t n) -> p t n", t=3)
        edN = sm2[:, 124:136].rearrange("p (t n) -> p t n", t=3)
        bed = sm2[:, 136:148].rearrange("p (t n) -> p t n", t=3)
        kdN = sm2[:, 148:160].rearrange("p (t n) -> p t n", t=3)
        alog = sm2[:, 160:164]
        dtb = sm2[:, 164:168]
        ealog = sm2[:, 168:172]
        t1, t2, t3, t4 = (sm2[:, 172 + 12 * n:184 + 12 * n].rearrange("p (t n) -> p t n", t=3) for n in range(4))
        cdc = sm2[:, 220:236].rearrange("p (n c) -> p n c", c=2)
        oss = sm2[:, 236:244]
        orn = sm2[:, 244:252]
        dnG = sm2[:, 252:380]
        baT = arena(17892, L2)[0:8]
        epsq, epsk = sm2[:, 380:381], sm2[:, 381:382]

        b_ = lambda n: psum[:, n, :]

        def ln_count(i, t):
            return t + 1 if i == 1 else 2 * i + t
        block = ctx.enter_context(nc.Block())

        GROUPS = [(AT["dn_qkv"] + m // 4, m % 4, "T") for m in range(12)]
        GROUPS += [(AT["sb_qkv"] + m // 4, m % 4, "T") for m in range(8)]
        GROUPS += [(AT["sb_qkv"] + 2, 0, t) for t in range(3)]

        def ends_chunk(g):
            return g + 1 == len(GROUPS) or GROUPS[g + 1][0] != GROUPS[g][0]

        def group_wait(eng, g):
            if ends_chunk(g):
                eng.wait_ge(S.used, GROUPS[g][0] + 1)
            else:
                eng.wait_ge(S.g2_mm, sum(not ends_chunk(n) for n in range(g + 1)))

        def tok(t):
            return slice(0, META) if t == 2 else slice(META + t * P, META + (t + 1) * P)

        def prob(m, p):
            return m[:, p * P:(p + 1) * P] if p < 8 else m[0:META, 1024 + (p - 8) * META:1024 + (p - 7) * META]

        def bank_prob(b, p, mb, mo=0):
            if p < 8:
                return psum[:, b + p // 4, (p % 4) * P:(p % 4 + 1) * P]
            return psum[0:META, mb, mo + (p - 8) * META:mo + (p - 7) * META]

        x8 = lambda m: m[:, 0:1024].rearrange("p (n w) -> p n w", w=P)
        m4 = lambda m: m[0:META, 1024:1088].rearrange("p (n w) -> p n w", w=META)
        two = lambda b: psum[:, b:b + 2, :].rearrange("p b (n w) -> p (b n) w", w=P)
        mt4 = lambda b, o=0: psum[0:META, b, o:o + 64].rearrange("p (n w) -> p n w", w=META)
        mask8 = lambda c: C(c).unsqueeze(1).broadcast_to([P, 8, P])
        mask4 = lambda c: C(c)[0:META, 0:META].unsqueeze(1).broadcast_to([META, 4, META])
        M0, M1, M2, M3, M4, M5, M6 = M
        St = [M5[:, 0:512], M5[:, 512:1024]]
        zN = gnB
        oT = arena(10276, 4, NT)
        lk = [arena(n, 640) for n in (12452, 13092, 15012)]
        ez = [arena(n, 640) for n in (13732, 14372, 16804)]
        Z_BANK = (0, 2, 5)

        def z_at(h):
            return psum[:, Z_BANK[h % 3]:Z_BANK[h % 3] + 2, :].rearrange("p a b -> p (a b)")[:, 0:640]

        osT = arena(10276 + 5 * 1088, 4, NT)
        gat = rowB[:, :, :, :].rearrange("p a b d -> p (a b d)").rearrange("p (g n) -> p g n", n=NT)
        mrg = arena(0, 8, NT)
        mtmp = arena(12452, 2, NT)

        SIDE_BANK = [3, 0, 1, 2, 3, 0, 1, 2, 6, 3, 7, 6, 7, 6, 7, 6, 7, 6, 7, 2]
        N_SIDE = 4 + 2 * KD
        side_before = sum(not ends_chunk(g) for g in range(len(GROUPS)))

        def side_wait(eng, i):
            if i % 4 == 3:
                eng.wait_ge(S.used, AT["dn_z"] + i // 4 + 1)
            else:
                eng.wait_ge(S.g2_mm, side_before + 3 * (i // 4) + i % 4 + 1)

        def pe_side(pe, mm, i):
            n = AT["dn_z"] + i // 4
            if i % 4 == 0:
                landed_wait(pe, n)
            earlier = [j for j in range(i) if SIDE_BANK[j] == SIDE_BANK[i]]
            if earlier:
                pe.wait_ge(S.side_ev, earlier[-1] + 1)
            w = ring_at(n).rearrange("p (k n) -> p k n", k=KD)
            o = psum[:, SIDE_BANK[i], 0:NT]
            for k in range(KD):
                if i < 4:
                    last = mm(o, hT[:, k, tok(i // 2)], w[:, k, (i % 2) * NT:(i % 2 + 1) * NT],
                              start=(k == 0), stop=(k == KD - 1))
                else:
                    last = mm(o, w[:, k, (i % 4) * P:(i % 4 + 1) * P], hT[:, k, META:L2],
                              start=(k == 0), stop=(k == KD - 1))
            last.then_inc(S.used if i % 4 == 3 else S.g2_mm, 1)

        def act_side(act, i):
            side_wait(act, i)
            o = psum[:, SIDE_BANK[i], 0:NT]
            if i < 4:
                ins = nc.scalar.activation(zN[:, i // 2, (i % 2) * NT:(i % 2 + 1) * NT], o, ACT.Silu)
            else:
                ins = nc.scalar.activation(gat[:, i - 4, :], o, ACT.Sigmoid, bias=V("b_gate", i - 4, i - 3))
            ins.then_inc(S.side_ev, 1)

        def pe_second(pe, mm, transposes):
            tr = nc.tensor.transpose
            pe.wait_ge(S.hT, 6)
            pe.wait_ge(S.in_ba, 16)
            for k in range(KD):
                last = mm(psum[0:8, 4, 0:L2], wba[:, k, :], hT[:, k, :], start=(k == 0), stop=(k == KD - 1))
            last.then_inc(S.ba_mm, 1)
            for g, (n, m, form) in enumerate(GROUPS):
                if g == 0 or ends_chunk(g - 1):
                    landed_wait(pe, n)
                if g >= 4:
                    pe.wait_ge(S.g2_ev, g - 3)
                w = ring_at(n).rearrange("p (k n) -> p k n", k=KD)
                for k in range(KD):
                    if form == "T":
                        last = mm(psum[:, g % 4, 0:L2], w[:, k, m * P:(m + 1) * P], hT[:, k, :],
                                  start=(k == 0), stop=(k == KD - 1))
                    else:
                        last = mm(psum[0:(META if form == 2 else P), g % 4, :], hT[:, k, tok(form)], w[:, k, :],
                                  start=(k == 0), stop=(k == KD - 1))
                last.then_inc(S.used if ends_chunk(g) else S.g2_mm, 1)
                if g == 0:
                    pe.wait_ge(S.ba_ev, 1)
                    for t in range(3):
                        last = tr(psum[0:(META if t == 2 else P), 5, 8 * t:8 * t + 8], baT[:, tok(t)],
                                  C("ident")[0:8, 0:8])
                    last.then_inc(S.ba_mm, 1)

            for i in range(4):
                pe.wait_ge(S.g2_ev, len(GROUPS) - 3 + i)
                pe_side(pe, mm, i)
            pe.wait_ge(S.sq, 1)
            pe.wait_ge(S.ba_ev, 2)
            for i in range(8):
                if i >= 4:
                    pe.wait_ge(S.nr, i - 3)
                mm(psum[:, 4 + i % 4, 0:L2], C("ones"), sqr[:, i, :], start=True, stop=True).then_inc(S.nsq, 1)
            pe_side(pe, mm, 4)
            pe.wait_ge(S.ug, 1)
            pe.wait_ge(S.nr, 8)
            for b in range(2):
                mm(b_(4 + b), C("ones"), M2[:, 512 * b:512 * b + 512], start=True, stop=True)
            mm(psum[:, 6, 0:64], C("ones")[0:META, :], M2[0:META, 1024:1088], start=True, stop=True)\
                .then_inc(S.R_mm, 1)
            for i in (5, 6, 7):
                pe_side(pe, mm, i)
            pe.wait_ge(S.nrmd, 1)
            pe.wait_ge(S.cvs, 12)
            pe.wait_ge(S.side_ev, 8)
            for t in range(3):
                for h in range(DH):
                    last = tr(psum[0:(META if t == 2 else P), t, h * P:(h + 1) * P], cv[:, 4 + h, tok(t)], C("ident"))
            last.then_inc(S.knt, 1)
            for t, b in enumerate((3, 7, 4)):
                if t == 2:
                    pe.wait_ge(S.ex01, 1)
                for h in range(DH):
                    last = tr(psum[0:(META if t == 2 else P), b, h * P:(h + 1) * P], cv[:, 8 + h, tok(t)], C("ident"))
            last.then_inc(S.vnt, 1)
            pe_side(pe, mm, 8)
            pe.wait_ge(S.kv_ev, 1)
            for p in range(12):
                t, h = p // 4, p % 4
                kT_ = cv[:, 4 + h, tok(t)]
                mm(bank_prob(0, p, 2), kT_, kT_, start=True, stop=True)
                if p < 8:
                    last = mm(bank_prob(4, p, 6), kT_, cv[:, h, tok(t)], start=True, stop=True)
            mm(bank_prob(0, 11, 2), kT_, kT_, start=True, stop=True).then_inc(S.gram, 1)
            pe_side(pe, mm, 9)
            pe_side(pe, mm, 10)
            pe.wait_ge(S.ab, 1)
            for p in range(12):
                last = tr(bank_prob(0, p, 2), prob(M2, p), C("ident") if p < 8 else C("ident")[0:META, 0:META])
            last.then_inc(S.n1t, 1)
            pe_side(pe, mm, 11)

            rounds = [
                (12, [(0, 2, 0, M4, M2), (3, 5, 0, M2, M4)]),
                (12, [(0, 2, 0, M1, M6), (3, 5, 0, M5, M1), (6, 5, 64, M1, M5)]),
                (12, [(0, 2, 0, M2, M6), (3, 5, 0, M4, M2)]),
                (12, [(0, 2, 0, M1, M6)]),
                (8, [(0, 2, 0, M3, M6), (3, 5, 0, M6, None), (6, 5, 64, M6, M3)]),
                (8, [(3, 5, 0, M2, M1)]),
                (8, [(0, 2, 0, M3, M4)]),
                (8, [(0, 2, 0, M5, M4)]),
            ]
            side_after = {0: 12, 2: 13, 3: 14, 5: 15, 6: 16, 7: 17}
            side_gone = {0: 10, 1: 13, 4: 15}
            for r, (count, products) in enumerate(rounds):
                if r in side_gone:
                    pe.wait_ge(S.side_ev, side_gone[r])
                pe.wait_ge(S.rd_v, DVE_ROUNDS[r])
                pe.wait_ge(S.rd_a, ACT_ROUNDS[r])
                for b, mb, mo, lhsT, rhs in products:
                    for p in range(count):
                        o = bank_prob(b, p, mb, mo)
                        if rhs is None:
                            last = tr(o, prob(lhsT, p), C("ident"))
                        else:
                            last = mm(o, prob(lhsT, p), prob(rhs, p), start=True, stop=True)
                last.then_inc(S.rd_mm, 1)
                if r in side_after:
                    pe_side(pe, mm, side_after[r])
            pe.wait_ge(S.rd_v, 8)
            for p in range(12):
                t, h = p // 4, p % 4
                rows_ = slice(0, META) if t == 2 else slice(0, P)
                o = psum[0:META, 5, h * P:(h + 1) * P] if t == 2 else bank_prob(0, p, 2)
                last = mm(o, prob(M6, p), vb[rows_, t, h * P:(h + 1) * P], start=True, stop=True)
                if p < 8:
                    mm(bank_prob(3, p, 5), kbe[:, t, h * P:(h + 1) * P], prob(M6, p), start=True, stop=True)
            last.then_inc(S.u_mm, 1)
            pe_side(pe, mm, 18)
            pe.wait_ge(S.side_ev, 18)
            pe.wait_ge(S.uv, 1)
            for h in range(DH):
                last = mm(psum[:, 6, h * P:(h + 1) * P], kdec[0:META, 2, h * P:(h + 1) * P],
                          M2[0:META, h * P:(h + 1) * P], start=True, stop=True)
            last.then_inc(S.s_mm, 1)
            pe_side(pe, mm, 19)
            pe.wait_ge(S.side_ev, 19)
            pe.wait_ge(S.wv, 1)
            for i in range(4):
                t, c = i // 2, i % 2
                r = slice(64 * c, 64 * c + 64)
                pe.wait_ge(S.sv, i + 1)
                for h in range(DH):
                    p = 4 * t + h
                    last = mm(psum[r, i % 2, h * P:(h + 1) * P], M3[:, p * P + 64 * c:p * P + 64 * c + 64],
                              St[i % 2][:, h * P:(h + 1) * P], start=True, stop=True)
                last.then_inc(S.vn_mm, 1)
                pe.wait_ge(S.vn_v, i + 1)
                vnew = M4[:, 512 * t:512 * t + 512]
                if i < 3:
                    for h in range(DH):
                        last = mm(psum[:, 7 - i % 2, h * P:(h + 1) * P], kdec[r, t, h * P:(h + 1) * P],
                                  vnew[r, h * P:(h + 1) * P], start=True, stop=True)
                    last.then_inc(S.s_mm, 1)
                for h in range(DH):
                    p = 4 * t + h
                    o = psum[r, 3 + t, h * P:(h + 1) * P]
                    mm(o, cv[:, h, META + i * 64:META + i * 64 + 64], St[i % 2][:, h * P:(h + 1) * P],
                       start=True, stop=False)
                    last = mm(o, M0[r, p * P + 64 * c:p * P + 64 * c + 64], vnew[r, h * P:(h + 1) * P],
                              start=False, stop=True)
                last.then_inc(S.o_mm, 1)
            def z_scores(h):
                if h >= 3:
                    pe.wait_ge(S.zw, h - 2)
                r = slice(64 * (h % 2), 64 * (h % 2) + 64)
                z0, z1 = Z_BANK[h % 3], Z_BANK[h % 3] + 1
                q = sbT[r, h // 2, META:L2]
                k = sbT[r, 4 + h // 2, :]
                mm(psum[:, z0, 0:NT], k[:, tok(0)], q, start=True, stop=False, skip_group_check=True)
                mm(psum[:, z0, NT:2 * NT], k[:, 0:P], q, start=False, stop=False, skip_group_check=True)
                mm(psum[:, z1, 0:P], k[:, tok(1)], q[:, P:NT], start=True, stop=False,
                   skip_group_check=True).then_inc(S.z1, 1)

            def z_sums(h):
                b = h % 3
                pe.wait_ge(S.zm, h + 1)
                l0, l1 = lk[b][:, 0:NT], lk[b][:, 512:640]
                k0, me, k1 = z_at(h)[:, 0:NT], z_at(h)[:, NT:512], z_at(h)[:, 512:640]
                mm(k0, C("tri"), l0, start=False, stop=False, skip_group_check=True)
                mm(k0[:, P:NT], C("ones"), l1, start=False, stop=True, skip_group_check=True)
                mm(me[0:META], C("tri")[0:META, 0:META], lk[b][0:META, NT:512], start=False, stop=False,
                   skip_group_check=True)
                mm(me[0:META], C("ones")[:, 0:META], l0, start=False, stop=False, skip_group_check=True)
                mm(me[0:META, P:NT], C("ones")[:, 0:META], l1, start=False, stop=True, skip_group_check=True)
                mm(k1, C("tri"), l1, start=False, stop=True, skip_group_check=True).then_inc(S.za, 1)

            def z_out(h):
                b = h % 3
                pe.wait_ge(S.zw, h + 1)
                r = slice(64 * (h % 2), 64 * (h % 2) + 64)
                if h == 4:
                    pe.wait_ge(S.mg, 4)
                o = psum[r, 4 if h < 4 else 7, (h // 2 % 2) * NT:(h // 2 % 2 + 1) * NT]
                f = slice(64 * h, 64 * h + 64)
                mm(o, sbv[:, 0, f], ez[b][:, 0:NT], start=True, stop=False)
                mm(o, sbv[0:META, 2, f], ez[b][0:META, NT:512], start=False, stop=False)
                mm(o[:, P:NT], sbv[:, 1, f], ez[b][:, 512:640], start=False, stop=True).then_inc(S.zo, 1)

            def branch(i, m, o, src):
                w = ring_at(AT["branch"] + i).rearrange("p (k n) -> p k n", k=4)
                for k in range(4):
                    last = mm(o, w[:, k, m * P:(m + 1) * P], src[:, k, :], start=(k == 0), stop=(k == 3))
                last.then_inc(S.br_mm if m < KD - 1 else S.used, 1)

            def delta_branch(m):
                if m == 0:
                    landed_wait(pe, AT["branch"])
                else:
                    pe.wait_ge(S.mg, m)
                if m == 4:
                    pe.wait_ge(S.zov, 1)
                branch(0, m, psum[:, 7 if m < 4 else 4, 0:NT], oT)

            pe.wait_ge(S.vn_v, 4)
            pe.wait_ge(S.side_ev, N_SIDE)
            z_scores(0)
            z_scores(1)
            pe.wait_ge(S.on, 1)
            for h in range(DH):
                for t in range(T):
                    last = tr(psum[:, 5 + h // 2, (h % 2) * NT + t * P:(h % 2) * NT + (t + 1) * P],
                              M1[:, 512 * t + h * P:512 * t + (h + 1) * P], C("ident"))
            last.then_inc(S.on_tr, 1)
            pe.wait_ge(S.orv, 1)
            for h in range(SH):
                if h + 2 < SH:
                    z_scores(h + 2)
                z_sums(h)
                if h != 4:
                    delta_branch(h if h < 4 else h - 1)
                if h:
                    z_out(h - 1)
            delta_branch(KD - 1)
            z_out(SH - 1)
            pe.wait_ge(S.zov, 2)
            landed_wait(pe, AT["branch"] + 1)
            for m in range(KD):
                if m >= 4:
                    pe.wait_ge(S.mg, KD + m - 3)
                branch(1, m, psum[:, m % 4, 0:NT], osT)
            pe.wait_ge(S.mgd, KD)
            for half in range(2):
                n = AT["w_out2"] + half
                landed_wait(pe, n)
                w = ring_at(n).rearrange("p (k n) -> p k n", k=KD)
                for t in range(T):
                    for k in range(KD):
                        last = mm(b_(4 + 2 * t + half), mrg[:, k, t * P:(t + 1) * P], w[:, k, :],
                                  start=(k == 0), stop=(k == KD - 1))
                last.then_inc(S.used, 1)
            transposes(5)
            pe_experts(pe, mm)

        DVE_ROUNDS = [1, 2, 3, 4, 5, 6, 6, 7]
        ACT_ROUNDS = [0, 1, 2, 3, 3, 4, 5, 5]

        def act_second(act, link, ln_sqrt, act_hT):
            sc = nc.scalar
            act.wait_ge(S.in_dn, 32)
            act.wait_ge(S.ba_ev, 2)
            sc.activation(ealog, alog, ACT.Exp)
            sc.activation(t1, ba[:, :, 0:4], ACT.Exp, scale=-1.0)
            sc.activation(t2, t4, ACT.Exp, scale=-1.0).then_inc(S.be_e, 1)

            def evac(g):
                group_wait(act, g)
                b = psum[:, g % 4, :]
                if g < 12:
                    ins = sc.copy(raw[:, g, 3:3 + L2], b[:, 0:L2])
                elif g < 20:
                    ins = sc.activation(sbT[:, g - 12, :], b[:, 0:L2], ACT.Copy, scale=SD ** -0.5 if g < 16 else 1.0)
                elif g < 22:
                    ins = sc.copy(sbv[:, g - 20, :], b)
                else:
                    ins = sc.copy(sbv[0:META, 2, :], b[0:META])
                ins.then_inc(S.g2_ev, 1)

            for g in range(len(GROUPS)):
                evac(g)
                if g >= 3 and g - 3 < 12:
                    act.wait_ge(S.conv, g - 2)
                    sc.activation(cv[:, g - 3, :], cv[:, g - 3, :], ACT.Silu).then_inc(S.cvs, 1)
            act.wait_ge(S.affine, 3)
            for i in range(3):
                act_side(act, i)
            act.wait_ge(S.cvs, 8)
            act.wait_ge(S.conv, 12)
            sc.activation(sqr[:, :, :], cv[:, 0:8, :], ACT.Square).then_inc(S.sq, 1)
            act_side(act, 3)
            for i in range(8):
                act.wait_ge(S.nsq, i + 1)
                q = i < 4
                sc.activation(nrm[:, i, :], psum[:, 4 + i % 4, 0:L2], ACT.Sqrt, bias=epsq if q else epsk,
                              scale=float(DD) if q else 1.0).then_inc(S.nr, 1)
            for i in (4, 5, 6, 7):
                act_side(act, i)
            act.wait_ge(S.E01, 1)
            sc.activation(M0[:, 0:1024], M0[:, 0:1024], ACT.Exp)
            sc.activation(M0[0:META, 1024:1088], M0[0:META, 1024:1088], ACT.Exp)
            sc.activation(M1[:, 0:1024], M1[:, 0:1024], ACT.Exp, scale=-1.0)
            sc.activation(M1[0:META, 1024:1088], M1[0:META, 1024:1088], ACT.Exp, scale=-1.0)
            sc.activation(M5[:, 0:1024], psum[:, 4:6, :].rearrange("p a b -> p (a b)"), ACT.Exp)
            sc.activation(edN, dN, ACT.Exp)
            sc.activation(kdN, kdN, ACT.Exp).then_inc(S.ex01, 1)
            for i in (8, 9, 10, 11):
                act_side(act, i)

            def evac2(r, pairs):
                act.wait_ge(S.rd_mm, r + 1)
                for dst, b, mo, meta in pairs:
                    last = sc.copy(dst[:, 0:1024], psum[:, b:b + 2, :].rearrange("p a b -> p (a b)"))
                    if meta:
                        last = sc.copy(dst[0:META, 1024:1088], psum[0:META, 5, mo:mo + 64])
                last.then_inc(S.rd_a, 1)

            evac2(0, [(M5, 3, 0, True)])
            act_side(act, 12)
            evac2(1, [(M2, 3, 0, True), (M4, 6, 64, True)])
            evac2(2, [(M1, 3, 0, True)])
            act_side(act, 13)
            act_side(act, 14)
            evac2(4, [(M5, 3, 0, False), (M1, 6, 0, False)])
            evac2(5, [(M3, 3, 0, False)])
            for i in (15, 16, 17):
                act_side(act, i)
            act.wait_ge(S.u_mm, 1)
            sc.copy(M3[:, 0:1024], psum[:, 3:5, :].rearrange("p a b -> p (a b)")).then_inc(S.wv, 1)
            act_side(act, 18)
            act_side(act, 19)
            act.wait_ge(S.o_v, 2)
            for i in range(8):
                last = sc.activation(M2[:, i * P:(i + 1) * P], M1[:, i * P:(i + 1) * P], ACT.Square,
                                     accum_out=oss[:, i:i + 1])
            link(last)
            sc.activation(orn, oss, ACT.Sqrt, bias=epsk, scale=1.0 / DD).then_inc(S.os, 1)
            def keep_logs(h):
                b = h % 3
                act.wait_ge(S.zc, h + 1)
                sc.activation(lk[b][:, :], lk[b][:, :], ACT.Exp).then_inc(S.ze, 1)
                act.wait_ge(S.ze, h + 1)
                sc.activation(lk[b][:, :], lk[b][:, :], ACT.Ln, bias=1.0).then_inc(S.zl, 1)

            keep_logs(0)
            for h in range(SH):
                if h + 1 < SH:
                    keep_logs(h + 1)
                act.wait_ge(S.zk, h + 1)
                if h >= 3:
                    act.wait_ge(S.zo, h - 2)
                sc.activation(ez[h % 3][:, :], z_at(h), ACT.Exp).then_inc(S.zw, 1)
            ln_sqrt(5)
            act_hT(4, V("g3"), V("b3"))
            act_experts(act, link, ln_sqrt)

        def dve_second(dve, v, link, residual, normalise, to_hT):
            for a in (ba, dN, kdN):
                v.memset(a, 0.0)
            v.memset(epsq, DD * RMS_EPS)
            v.memset(epsk, RMS_EPS)
            link(v.memset(raw[:, :, 0:3], 0.0))
            dve.wait_ge(S.ba_mm, 1)
            v.tensor_copy(baT, psum[0:8, 4, 0:L2]).then_inc(S.ba_ev, 1)
            dve.wait_ge(S.ba_mm, 2)
            v.tensor_copy(ba[:, 0:2, :], psum[:, 5, 0:16].rearrange("p (t n) -> p t n", t=2))
            link(v.tensor_copy(ba[0:META, 2, :], psum[0:META, 5, 16:24]))
            dve.wait_ge(S.in_dn, 32)
            link(v.tensor_tensor(t3, ba[:, :, 4:8], dtb.unsqueeze(1).broadcast_to([P, 3, 4]), ALU.add))
            v.scalar_tensor_tensor(t4, t3, -1.0, t3, ALU.mult, ALU.max).then_inc(S.ba_ev, 1)
            dve.wait_ge(S.be_e, 1)
            link(v.tensor_scalar(t1, t1, 1.0, None, ALU.add))
            link(v.reciprocal(beta, t1))
            link(v.tensor_scalar(t4, t2, 2.0, None, ALU.add))
            link(v.reciprocal(t4, t4))
            link(v.tensor_tensor(t4, t4, t2, ALU.mult))
            link(v.tensor_tensor(t1, t4, t4, ALU.mult))
            link(v.tensor_scalar(t2, t1, 1.0 / 15, None, ALU.mult))
            for n in (13, 11, 9, 7, 5, 3):
                link(v.scalar_tensor_tensor(t2, t2, 1.0 / n, t1, ALU.add, ALU.mult))
            link(v.scalar_tensor_tensor(t2, t2, 1.0, t4, ALU.add, ALU.mult))
            link(v.tensor_scalar(t3, t3, 0.0, 0.5, ALU.max, ALU.mult))
            link(v.tensor_tensor(t3, t3, t2, ALU.add))
            link(v.scalar_tensor_tensor(gdn, t3, -2.0, ealog.unsqueeze(1).broadcast_to([P, 3, 4]), ALU.mult, ALU.mult))
            for i in range(12):
                dve.wait_ge(S.g2_ev, i + 1)
                link(v.tensor_scalar(cv[:, i, :], raw[:, i, 0:L2], V("conv", 4 * i, 4 * i + 1), None, ALU.mult))
                for j in range(1, 4):
                    ins = v.scalar_tensor_tensor(cv[:, i, :], raw[:, i, j:j + L2], V("conv", 4 * i + j, 4 * i + j + 1),
                                                 cv[:, i, :], ALU.mult, ALU.add)
                    if j < 3:
                        link(ins)
                ins.then_inc(S.conv, 1)
            for p in range(12):
                t, h = p // 4, p % 4
                r = slice(0, META) if t == 2 else slice(0, P)
                last = v.tensor_scalar(prob(M2, p), C("ucum")[r, 0:(META if t == 2 else P)], gdn[r, t, h:h + 1], None,
                                       ALU.mult)
            last.then_inc(S.ug, 1)
            dve.wait_ge(S.nr, 8)
            link(v.reciprocal(nrm[:, :, :], nrm[:, :, :]))
            v.tensor_tensor(cv[:, 0:8, :], cv[:, 0:8, :], nrm[:, :, :], ALU.mult).then_inc(S.nrmd, 1)
            dve.wait_ge(S.nrmd, 1)
            dve.wait_ge(S.R_mm, 1)
            for p in range(12):
                t, h = p // 4, p % 4
                r = slice(0, META) if t == 2 else slice(0, P)
                last = v.tensor_tensor_reduce(prob(M3, p), bank_prob(4, p, 6)[r], C("ident")[r, 0:(META if t == 2 else P)],
                                              1.0, 0.0, ALU.mult, ALU.add, dN[r, t, h:h + 1])
            link(last)
            for t in range(T):
                d = dN[:, t, :].unsqueeze(2).broadcast_to([P, 4, P])
                v.tensor_tensor(M4[:, 512 * t:512 * t + 512].rearrange("p (n w) -> p n w", w=P),
                                b_(4 + t).rearrange("p (n w) -> p n w", w=P), d, ALU.subtract)
            link(v.tensor_tensor(m4(M4), psum[0:META, 6, 0:64].rearrange("p (n w) -> p n w", w=META),
                                 dN[0:META, 2, :].unsqueeze(2).broadcast_to([META, 4, META]), ALU.subtract))
            for r, a, b in ((slice(0, P), 0, 1024), (slice(0, META), 1024, 1088)):
                v.tensor_scalar(M0[r, a:b], M4[r, a:b], 0.0, None, ALU.min)
                v.tensor_scalar(M1[r, a:b], M4[r, a:b], 0.0, None, ALU.max)
            flat = psum[:, 4:6, :].rearrange("p a b -> p (a b)")
            for c in range(2):
                r = slice(64 * c, 64 * c + 64)
                v.tensor_tensor(kdN[r, 0:2, :], flat[r, 64 * c + 63:1024:P].rearrange("p (t h) -> p t h", t=2),
                                dN[r, 0:2, :], ALU.subtract)
            v.tensor_tensor(kdN[0:META, 2, :], psum[0:META, 6, META - 1:64:META], dN[0:META, 2, :],
                            ALU.subtract).then_inc(S.E01, 1)
            dve.wait_ge(S.ex01, 1)
            v.tensor_tensor(x8(M0), x8(M0), mask8("causT"), ALU.mult)
            v.tensor_copy(cdc[:, :, :].rearrange("p n c -> p (n c)"), M5[:, 63:1024:64])
            link(v.tensor_tensor(bed, beta, edN, ALU.mult))
            dve.wait_ge(S.knt, 1)
            for t in range(3):
                r = slice(0, META) if t == 2 else slice(0, P)
                n = META if t == 2 else P
                src = psum[r, t, :].rearrange("p (h d) -> p h d", d=P)
                for dst, f in ((kbe, bed), (kdec, kdN)):
                    v.tensor_tensor(dst[r, t, :].rearrange("p (h d) -> p h d", d=P), src,
                                    f[r, t, :].unsqueeze(2).broadcast_to([n, 4, P]), ALU.mult)
            dve.wait_ge(S.vnt, 1)
            for t, b in enumerate((3, 7, 4)):
                r = slice(0, META) if t == 2 else slice(0, P)
                n = META if t == 2 else P
                last = v.tensor_tensor(vb[r, t, :].rearrange("p (h d) -> p h d", d=P),
                                       psum[r, b, :].rearrange("p (h d) -> p h d", d=P),
                                       beta[r, t, :].unsqueeze(2).broadcast_to([n, 4, P]), ALU.mult)
            last.then_inc(S.kv_ev, 1)
            dve.wait_ge(S.gram, 1)
            for p in range(12):
                t, h = p // 4, p % 4
                r = slice(0, META) if t == 2 else slice(0, P)
                last = v.scalar_tensor_tensor(prob(M1, p), bank_prob(0, p, 2), beta[r, t, h:h + 1], prob(M1, p),
                                              ALU.mult, ALU.mult)
            link(last)
            for t in range(T):
                c = slice(512 * t, 512 * t + 512)
                v.tensor_tensor(M0[:, c], M0[:, c], b_(4 + t), ALU.mult)
            v.tensor_tensor(x8(M3), x8(M1), mask8("off16"), ALU.mult)
            v.tensor_tensor(x8(M2), x8(M1), mask8("m16"), ALU.mult)
            v.tensor_tensor(m4(M2), m4(M1), mask4("m16"), ALU.mult).then_inc(S.ab, 1)
            for h in range(DH):
                last = v.tensor_tensor(cv[:, h, META:L2].rearrange("p (t w) -> p t w", t=T),
                                       cv[:, h, META:L2].rearrange("p (t w) -> p t w", t=T),
                                       M5[:, 0:1024].rearrange("p (t n w) -> p t n w", t=T, w=P)[:, :, h, :], ALU.mult)
            link(last)
            dve.wait_ge(S.n1t, 1)
            v.tensor_copy(M4[:, 0:1024], psum[:, 0:2, :].rearrange("p a b -> p (a b)"))
            v.tensor_copy(M4[0:META, 1024:1088], psum[0:META, 2, 0:64])
            v.tensor_tensor(x8(M6), two(0), mask8("ident"), ALU.add)
            v.tensor_tensor(m4(M6), mt4(2), mask4("ident"), ALU.add).then_inc(S.rd_v, 1)
            dve.wait_ge(S.rd_mm, 1)
            v.tensor_copy(M1[:, 0:1024], psum[:, 0:2, :].rearrange("p a b -> p (a b)"))
            v.tensor_copy(M1[0:META, 1024:1088], psum[0:META, 2, 0:64]).then_inc(S.rd_v, 1)
            for r in (1, 2, 3):
                dve.wait_ge(S.rd_mm, r + 1)
                v.tensor_tensor(x8(M6), two(0), x8(M6), ALU.add)
                v.tensor_tensor(m4(M6), mt4(2), m4(M6), ALU.add).then_inc(S.rd_v, 1)
            dve.wait_ge(S.rd_mm, 5)
            v.tensor_copy(M2[:, 0:1024], psum[:, 0:2, :].rearrange("p a b -> p (a b)"))
            v.scalar_tensor_tensor(x8(M4), two(0), -1.0, mask8("ident"), ALU.mult, ALU.add).then_inc(S.rd_v, 1)
            dve.wait_ge(S.rd_mm, 7)
            v.tensor_tensor(x8(M4), two(0), x8(M4), ALU.add).then_inc(S.rd_v, 1)
            dve.wait_ge(S.rd_mm, 8)
            v.tensor_copy(x8(M6), two(0)).then_inc(S.rd_v, 1)
            dve.wait_ge(S.u_mm, 1)
            v.tensor_copy(M1[:, 0:1024], psum[:, 0:2, :].rearrange("p a b -> p (a b)"))
            v.tensor_copy(M2[0:META, 0:512], psum[0:META, 5, :]).then_inc(S.uv, 1)
            dve.wait_ge(S.s_mm, 1)
            v.tensor_copy(St[0], b_(6)).then_inc(S.sv, 1)
            for i in range(4):
                t, c = i // 2, i % 2
                r = slice(64 * c, 64 * c + 64)
                f = slice(512 * t, 512 * t + 512)
                dve.wait_ge(S.vn_mm, i + 1)
                v.tensor_tensor(M4[r, f], M1[r, f], psum[r, i % 2, :], ALU.subtract).then_inc(S.vn_v, 1)
                if i < 3:
                    if i >= 1:
                        dve.wait_ge(S.o_mm, i)
                    dve.wait_ge(S.sv, i + 1)
                    dve.wait_ge(S.s_mm, i + 2)
                    for h in range(DH):
                        d = slice(h * P, (h + 1) * P)
                        last = v.scalar_tensor_tensor(St[(i + 1) % 2][:, d], St[i % 2][:, d],
                                                      cdc[:, 4 * t + h, c:c + 1], psum[:, 7 - i % 2, d],
                                                      ALU.mult, ALU.add)
                    last.then_inc(S.sv, 1)
                if c == 1:
                    dve.wait_ge(S.o_mm, i + 1)
                    v.tensor_copy(M1[:, f], b_(3 + t)).then_inc(S.o_v, 1)
            dve.wait_ge(S.os, 1)
            dve.wait_ge(S.o_v, 2)
            link(v.reciprocal(orn, orn))
            link(v.tensor_tensor(x8(M1), x8(M1), orn.unsqueeze(2).broadcast_to([P, 8, P]), ALU.mult))
            link(v.tensor_tensor(x8(M1), x8(M1), dnG.unsqueeze(1).broadcast_to([P, 8, P]), ALU.mult))
            dve.wait_ge(S.side_ev, 4)
            v.tensor_tensor(M1[:, 0:1024], M1[:, 0:1024], zN[:, :, :].rearrange("p t w -> p (t w)"),
                            ALU.mult).then_inc(S.on, 1)
            dve.wait_ge(S.on_tr, 1)
            v.tensor_copy(oT[:, :, :], psum[:, 5:7, :].rearrange("p a (b c) -> p (a b) c", c=NT)).then_inc(S.orv, 1)

            diag = lambda a: a.rearrange("p (n w) -> p n w", w=P)[:, 0:5:4, :]
            mul2 = C("sbmul").unsqueeze(1).broadcast_to([P, 2, P])
            add2 = C("sbadd").unsqueeze(1).broadcast_to([P, 2, P])

            def clamp(h):
                dve.wait_ge(S.z1, h + 1)
                if h >= 3:
                    dve.wait_ge(S.za, h - 2)
                v.tensor_scalar(lk[h % 3][:, :], z_at(h), 80.0, None, ALU.min).then_inc(S.zc, 1)

            def keep(h):
                b = h % 3
                dve.wait_ge(S.zl, h + 1)
                link(v.tensor_tensor(lk[b][:, :], lk[b][:, :], z_at(h), ALU.max))
                link(v.tensor_scalar(lk[b][:, :], lk[b][:, :], -1.0, None, ALU.mult))
                v.tensor_tensor(diag(lk[b]), diag(lk[b]), mul2, ALU.mult).then_inc(S.zm, 1)

            def branch_wait(i, m):
                if m < KD - 1:
                    dve.wait_ge(S.br_mm, i * (KD - 1) + m + 1)
                else:
                    dve.wait_ge(S.used, AT["branch"] + i + 1)

            def delta_branch_out(m):
                branch_wait(0, m)
                v.tensor_tensor(mrg[:, m, :], psum[:, 7 if m < 4 else 4, 0:NT], gat[:, m, :], ALU.mult)\
                    .then_inc(S.mg, 1)

            dve.wait_ge(S.side_ev, N_SIDE)
            clamp(0)
            clamp(1)
            keep(0)
            for h in range(SH):
                if h + 2 < SH:
                    clamp(h + 2)
                if h + 1 < SH:
                    keep(h + 1)
                dve.wait_ge(S.za, h + 1)
                v.tensor_tensor(diag(z_at(h)), diag(z_at(h)), add2, ALU.add).then_inc(S.zk, 1)
                if h != 4:
                    delta_branch_out(h if h < 4 else h - 1)
                else:
                    dve.wait_ge(S.zo, 4)
                    v.tensor_copy(osT[:, 0:2, :], b_(4).rearrange("p (a b) -> p a b", a=2)).then_inc(S.zov, 1)
            delta_branch_out(KD - 1)
            dve.wait_ge(S.zo, SH)
            v.tensor_copy(osT[:, 2:4, :], b_(7).rearrange("p (a b) -> p a b", a=2)).then_inc(S.zov, 1)
            for m in range(KD):
                branch_wait(1, m)
                v.tensor_tensor(mtmp[:, m % 2, :], psum[:, m % 4, 0:NT], gat[:, 8 + m, :], ALU.mult)\
                    .then_inc(S.mg, 1)
                dve.wait_ge(S.mg, KD + m + 1)
                v.tensor_tensor(mrg[:, m, :], mrg[:, m, :], mtmp[:, m % 2, :], ALU.add).then_inc(S.mgd, 1)
            dve.wait_ge(S.used, AT["w_out2"] + 2)
            residual(5, None, 3)
            for t in range(T):
                normalise(5, t)
            to_hT(4, V("g3"), V("b3"))
            dve_experts(dve, v, link, residual, normalise)

        def pool_tail(pool, link, affine, rows):
            pool.wait_ge(S.on, 1)
            pool.dma_start(Rw, IN["router_w"].rearrange("p (k n) -> p k n", k=KD)).then_inc(S.in_rt, 16)
            pool.dma_start(rb, IN["router_b"].partition_broadcast(P)).then_inc(S.in_rt, 16)
            pool.wait_ge(S.mgd, KD)
            rows(4, 0, S.in_row0)
            rows(5, 1, S.in_row1)
            affine(4, 4)
            pool_experts(pool, link, affine)

        lay = gnB[:, :, :].rearrange("p a b -> p (a b)")
        Rw = lay[:, 0:288].rearrange("p (k n) -> p k n", k=KD)
        rb = lay[:, 288:324]
        NG, EG = 4, NE // 4

        def rt(off, *shape):
            return arena(off, T, *shape)

        lg = rt(0, 36)
        gmx, ohg, gex, gsum = rt(80, 1), rt(84, NG), rt(92, NG), rt(100, 1)
        stmp = arena(104, T * NG, EG)
        sel, oh1, oh2 = rt(168, EG), rt(184, EG), rt(200, EG)
        m1, m2, dl, ed = rt(216, 1), rt(218, 1), rt(220, 1), rt(222, 1)
        a1, a2, tq = rt(224, 1), rt(226, 1), rt(228, 1)
        comb = arena(240, T, NE)
        cT = arena(320, NT)[0:NE]
        mem = rt(600, NE)
        slot = rt(664, NE)
        cmx = arena(728, 1)
        flag = sb("flag", [P, 1], I32)
        sel2 = [arena(1000 + 256 * n, T, 2 * CAP) for n in range(2)]
        selw = [arena(1512 + 256 * n, T, 2 * CAP) for n in range(2)]
        xg = [arena(2536 + 1024 * n, KD, 2 * CAP) for n in range(2)]
        yg = [arena(4584 + 1024 * n, DM) for n in range(2)]
        pg = [arena(6632 + 256 * n, 256) for n in range(2)]
        hp = [arena(7144 + 256 * n, 256) for n in range(2)]
        turned = [arena(7656 + 512 * n, 512) for n in range(2)]
        NP = NE // 2
        extra_slot = arena(12288, CH)
        cB = arena(1000, NE, NT)
        eg_s = arena(9192, 2, 512)
        eh_s = arena(10216, 2, 512)
        hid = arena(11240, 2, 512)

        def pe_experts(pe, mm):
            pe.wait_ge(S.hT, 8)
            pe.wait_ge(S.in_rt, 32)
            for t in range(T):
                for k in range(KD):
                    last = mm(psum[:, 4, 36 * t:36 * t + 36], hT[:, k, tok(t)], Rw[:, k, :],
                              start=(k == 0), stop=(k == KD - 1))
            last.then_inc(S.lg_mm, 1)
            pe.wait_ge(S.cmb, 1)
            mm(psum[:, 5, 0:NE], C("sbmul"), mem[:, 0, :], start=True, stop=True)
            mm(psum[:, 5, NE:2 * NE], C("ones"), mem[:, 0, :], start=True, stop=False)
            mm(psum[:, 5, NE:2 * NE], C("sbmul"), mem[:, 1, :], start=False, stop=True)
            mm(psum[:, 5, 2 * NE:3 * NE], C("ones"), mem[:, 0, :], start=True, stop=False)
            mm(psum[:, 5, 2 * NE:3 * NE], C("ones"), mem[:, 1, :], start=False, stop=True).then_inc(S.lg_mm, 1)
            pe.wait_ge(S.flag, 1)
            crowded = pe.value_load(flag[0:1, 0:1], min_val=0, max_val=1)
            with pe.If(crowded == 0):
                pe_gathered(pe, mm)
            with pe.Else():
                pe_dense(pe, mm)

        def pe_gathered(pe, mm):
            def gather(p):
                pe.wait_ge(S.sel, 2 * p + 1)
                if p >= 2:
                    pe.wait_ge(S.yv, 2 * (p - 1))
                for k in range(KD):
                    for t in range(T):
                        last = mm(psum[:, k // 4, (k % 4) * P:(k % 4 + 1) * P], X[:, t, k * P:(k + 1) * P],
                                  sel2[p % 2][:, t, :], start=(t == 0), stop=(t == T - 1))
                last.then_inc(S.xg, 1)

            def gate_up(p):
                for e in range(2):
                    landed_wait(pe, gate_chunk(2 * p + e))
                pe.wait_ge(S.xgv, 2 * (p + 1))
                if p:
                    pe.wait_ge(S.eu, p)
                for k in range(KD):
                    for e in range(2):
                        w = ring_at(gate_chunk(2 * p + e)).rearrange("p (k n) -> p k n", k=KD)
                        last = mm(psum[e * CAP:(e + 1) * CAP, 2, :], xg[p % 2][:, k, e * CAP:(e + 1) * CAP],
                                  w[:, k, :], start=(k == 0), stop=(k == KD - 1))
                        if k == KD - 1:
                            last.then_inc(S.used, 1)

            def turn(p):
                pe.wait_ge(S.sel, 2 * p + 2)
                pe.wait_ge(S.eu, p + 1)
                if p:
                    pe.wait_ge(S.cTv, p)
                for i in range(2):
                    nc.tensor.transpose(psum[:, 3, i * P:(i + 1) * P], hp[p % 2][:, i * P:(i + 1) * P], C("ident"))
                for t in range(T):
                    last = nc.tensor.transpose(psum[:, 3, 256 + t * P:256 + (t + 1) * P], selw[p % 2][:, t, :],
                                               C("ident"))
                last.then_inc(S.cT, 1)

            def scatter(p):
                pe.wait_ge(S.yv, 2 * (p + 1))
                for t in range(T):
                    for half in range(2):
                        last = mm(b_(4 + 2 * t + half), turned[p % 2][:, 256 + t * P:256 + (t + 1) * P],
                                  yg[p % 2][:, half * 512:(half + 1) * 512], start=(p == 0), stop=(p == NP - 1))
                last.then_inc(S.sct, 1)

            def down(p):
                n = down_chunk(2 * p)
                landed_wait(pe, n)
                pe.wait_ge(S.cTv, p + 1)
                if p < NP - 1:
                    pe.wait_ge(S.xgv, 2 * (p + 2))
                w = ring_at(n).rearrange("p (e f n) -> p e f n", e=2, f=2)
                for half in range(2):
                    for f in range(2):
                        for e in range(2):
                            c = f * P + e * CAP
                            last = mm(psum[e * CAP:(e + 1) * CAP, half, :], turned[p % 2][:, c:c + CAP],
                                      w[:, e, f, half * 512:(half + 1) * 512], start=(f == 0), stop=(f == 1))
                last.then_inc(S.used, 1)

            pe.wait_ge(S.affine, 4)
            gather(0)
            for p in range(NP):
                gate_up(p)
                if p < NP - 1:
                    gather(p + 1)
                turn(p)
                if p:
                    scatter(p - 1)
                down(p)
            scatter(NP - 1)

        def pe_dense(pe, mm):
            pe.wait_ge(S.cmb, 2)
            for t in range(T):
                last = nc.tensor.transpose(psum[0:NE, 5, t * P:(t + 1) * P], comb[:, t, :], C("ident"))
            last.then_inc(S.cT, 1)
            pe.wait_ge(S.cTv, 1)
            for e in range(NE):
                if e >= 4:
                    pe.wait_ge(S.cB_ev, e - 3)
                mm(psum[:, e % 4, 0:NT], C("ident")[0:NE, e:e + 1].broadcast_to([NE, P]), cT, start=True, stop=True)\
                    .then_inc(S.cB_mm, 1)
            pe.wait_ge(S.cB_ev, NE)

            def down(e):
                n = down_chunk(e)
                landed_wait(pe, n)
                pe.wait_ge(S.hid, e + 1)
                w = ring_at(n).rearrange("p (e f n) -> p e f n", e=2, f=2)
                for f in range(2):
                    for t in range(T):
                        for half in range(2):
                            last = mm(b_(4 + 2 * t + half), hid[:, e % 2, f * NT + t * P:f * NT + (t + 1) * P],
                                      w[:, e % 2, f, half * 512:(half + 1) * 512],
                                      start=(e == 0 and f == 0), stop=(e == NE - 1 and f == 1))
                last.then_inc(S.used if e % 2 else S.d_mm, 1)

            for e in range(NE):
                n = gate_chunk(e)
                landed_wait(pe, n)
                if e >= 2:
                    pe.wait_ge(S.eu, e - 1)
                w = ring_at(n).rearrange("p (k w n) -> p k w n", w=2, k=KD)
                for i in range(2):
                    for f in range(2):
                        for k in range(KD):
                            last = mm(psum[:, 2 * (e % 2) + i, f * NT:(f + 1) * NT],
                                      w[:, k, i, f * P:(f + 1) * P], hT[:, k, META:L2],
                                      start=(k == 0), stop=(k == KD - 1))
                last.then_inc(S.used, 1)
                if e % 2:
                    down(e - 1)
                    down(e)

        def act_experts(act, link, ln_sqrt):
            act.wait_ge(S.rt_x, 1)
            nc.scalar.activation(gex[:, :, :], gex[:, :, :], ACT.Exp)
            nc.scalar.activation(ed[:, :, :], dl[:, :, :], ACT.Exp).then_inc(S.rt_e, 1)
            act.wait_ge(S.flag, 1)
            crowded = act.value_load(flag[0:1, 0:1], min_val=0, max_val=1)
            with act.If(crowded == 0):
                act_gathered(act)
            with act.Else():
                act_dense(act)
            ln_sqrt(6)

        def act_gathered(act):
            def gathered(p):
                act.wait_ge(S.xg, p + 1)
                nc.scalar.copy(xg[p % 2][:, 0:4, :].rearrange("p k n -> p (k n)"), b_(0)).then_inc(S.xgv, 1)

            gathered(0)
            for p in range(NP):
                act.wait_ge(S.used, gate_chunk(2 * p + 1) + 1)
                if p >= 2:
                    act.wait_ge(S.eu, p - 1)
                nc.scalar.activation(pg[p % 2], psum[:, 2, 0:256], ACT.Silu).then_inc(S.eg, 1)
                if p < NP - 1:
                    gathered(p + 1)
                act.wait_ge(S.used, down_chunk(2 * p) + 1)
                if p >= 2:
                    act.wait_ge(S.sct, p - 1)
                nc.scalar.copy(yg[p % 2][:, 0:512], b_(0)).then_inc(S.yv, 1)

        def act_dense(act):
            for e in range(NE):
                act.wait_ge(S.cB_mm, e + 1)
                nc.scalar.copy(cB[:, e, :], psum[:, e % 4, 0:NT]).then_inc(S.cB_ev, 1)
            for e in range(NE):
                act.wait_ge(S.used, gate_chunk(e) + 1)
                if e >= 2:
                    act.wait_ge(S.eu, e - 1)
                nc.scalar.activation(eg_s[:, e % 2, :], b_(2 * (e % 2)), ACT.Silu).then_inc(S.eg, 1)

        def dve_experts(dve, v, link, residual, normalise):
            dve.wait_ge(S.lg_mm, 1)
            dve.wait_ge(S.in_rt, 32)
            link(v.tensor_tensor(lg[:, :, :], psum[:, 4, 0:72].rearrange("p (t n) -> p t n", t=T),
                                 rb.unsqueeze(1).broadcast_to([P, T, 36]), ALU.add))
            gl, el = lg[:, :, 0:NG], lg[:, :, NG:36]

            def first_max(x, n, mx, oh):
                link(v.tensor_reduce(mx, x, AX, ALU.max))
                link(v.tensor_tensor(oh, x, mx.broadcast_to([P, T, n]), ALU.is_equal))
                link(v.tensor_tensor(oh, oh, C("tie", 0, n).unsqueeze(1).broadcast_to([P, T, n]), ALU.mult))
                link(v.tensor_reduce(tq, oh, AX, ALU.max))
                link(v.tensor_tensor(oh, oh, tq.broadcast_to([P, T, n]), ALU.is_equal))

            first_max(gl, NG, gmx, ohg)
            link(v.tensor_tensor(gex, gl, gmx.broadcast_to([P, T, NG]), ALU.subtract))
            for t in range(T):
                last = v.tensor_tensor(stmp[:, t * NG:(t + 1) * NG, :], el[:, t, :].rearrange("p (g e) -> p g e", g=NG),
                                       ohg[:, t, :].unsqueeze(2).broadcast_to([P, NG, EG]), ALU.mult)
            link(last)
            for t in range(T):
                last = v.tensor_reduce(sel[:, t, :], stmp[:, t * NG:(t + 1) * NG, :].rearrange("p g e -> p e g"), AX,
                                       ALU.add)
            link(last)
            first_max(sel, EG, m1, oh1)
            link(v.scalar_tensor_tensor(sel, oh1, NEG, sel, ALU.mult, ALU.add))
            first_max(sel, EG, m2, oh2)
            v.tensor_tensor(dl, m2, m1, ALU.subtract).then_inc(S.rt_x, 1)
            link(v.tensor_tensor(sel, oh1, oh2, ALU.add))
            for t in range(T):
                last = v.tensor_tensor(mem[:, t, :].rearrange("p (g e) -> p g e", g=NG),
                                       sel[:, t:t + 1, :].broadcast_to([P, NG, EG]),
                                       ohg[:, t, :].unsqueeze(2).broadcast_to([P, NG, EG]), ALU.mult)
            last.then_inc(S.cmb, 1)
            dve.wait_ge(S.rt_e, 1)
            link(v.tensor_reduce(gsum, gex, AX, ALU.add))
            link(v.tensor_scalar(a1, ed, 1.0, None, ALU.add))
            link(v.tensor_tensor(a1, a1, gsum, ALU.mult))
            link(v.reciprocal(a1, a1))
            link(v.tensor_tensor(a2, a1, ed, ALU.mult))
            link(v.tensor_tensor(oh1, oh1, a1.broadcast_to([P, T, EG]), ALU.mult))
            link(v.tensor_tensor(oh2, oh2, a2.broadcast_to([P, T, EG]), ALU.mult))
            link(v.tensor_tensor(oh1, oh1, oh2, ALU.add))
            for t in range(T):
                last = v.tensor_tensor(comb[:, t, :].rearrange("p (g e) -> p g e", g=NG),
                                       oh1[:, t:t + 1, :].broadcast_to([P, NG, EG]),
                                       ohg[:, t, :].unsqueeze(2).broadcast_to([P, NG, EG]), ALU.mult)
            last.then_inc(S.cmb, 1)
            dve.wait_ge(S.lg_mm, 2)
            dve.wait_ge(S.cmb, 2)
            link(v.scalar_tensor_tensor(slot, psum[:, 5, 0:2 * NE].rearrange("p (t n) -> p t n", t=T), 1.0, mem,
                                        ALU.add, ALU.mult))
            link(v.tensor_scalar(slot, slot, -1.0, None, ALU.add))
            link(v.tensor_reduce(cmx, psum[:, 5, 2 * NE:3 * NE], AX, ALU.max))
            v.tensor_scalar(flag[:, :], cmx, float(CAP), None, ALU.is_gt).then_inc(S.flag, 1)
            dve.wait_ge(S.flag, 1)
            crowded = dve.value_load(flag[0:1, 0:1], min_val=0, max_val=1)
            with dve.If(crowded == 0):
                dve_gathered(dve, v)
            with dve.Else():
                dve_dense(dve, v)
            residual(6, None, 4)
            dve.wait_ge(S.in_row1, 48)
            for t in range(T):
                normalise(6, t, rowB[:, 1])

        def dve_gathered(dve, v):
            def select(p):
                if p >= 2:
                    dve.wait_ge(S.xg, p - 1)
                v.tensor_tensor(sel2[p % 2][:, :, :].rearrange("p t (e n) -> p t e n", e=2),
                                C("iota").unsqueeze(1).unsqueeze(1).broadcast_to([P, T, 2, CAP]),
                                slot[:, :, 2 * p:2 * p + 2].unsqueeze(3).broadcast_to([P, T, 2, CAP]),
                                ALU.is_equal).then_inc(S.sel, 1)
                dve.wait_ge(S.sel, 2 * p + 1)
                if p >= 2:
                    dve.wait_ge(S.cT, p - 1)
                v.tensor_tensor(selw[p % 2][:, :, :].rearrange("p t (e n) -> p t e n", e=2),
                                sel2[p % 2][:, :, :].rearrange("p t (e n) -> p t e n", e=2),
                                comb[:, :, 2 * p:2 * p + 2].unsqueeze(3).broadcast_to([P, T, 2, CAP]),
                                ALU.mult).then_inc(S.sel, 1)

            def gathered(p):
                dve.wait_ge(S.xg, p + 1)
                v.tensor_copy(xg[p % 2][:, 4:8, :].rearrange("p k n -> p (k n)"), b_(1)).then_inc(S.xgv, 1)

            select(0)
            select(1)
            gathered(0)
            for p in range(NP):
                dve.wait_ge(S.eg, p + 1)
                if p >= 2:
                    dve.wait_ge(S.cT, p - 1)
                v.tensor_tensor(hp[p % 2], psum[:, 2, 256:512], pg[p % 2], ALU.mult).then_inc(S.eu, 1)
                if p < NP - 1:
                    gathered(p + 1)
                dve.wait_ge(S.cT, p + 1)
                if p >= 2:
                    dve.wait_ge(S.sct, p - 1)
                v.tensor_copy(turned[p % 2], b_(3)).then_inc(S.cTv, 1)
                if p + 2 < NP:
                    select(p + 2)
                dve.wait_ge(S.used, down_chunk(2 * p) + 1)
                v.tensor_copy(yg[p % 2][:, 512:1024], b_(1)).then_inc(S.yv, 1)
            dve.wait_ge(S.sct, NP)

        def dve_dense(dve, v):
            dve.wait_ge(S.cT, 1)
            v.tensor_copy(cT, psum[0:NE, 5, 0:NT]).then_inc(S.cTv, 1)
            for e in range(NE):
                dve.wait_ge(S.eg, e + 1)
                if e >= 2:
                    dve.wait_ge(S.hid, e - 1)
                v.tensor_tensor(eh_s[:, e % 2, :], b_(2 * (e % 2) + 1), eg_s[:, e % 2, :], ALU.mult).then_inc(S.eu, 1)
            dve.wait_ge(S.used, AT["end"])

        def pool_experts(pool, link, affine):
            pool.wait_ge(S.flag, 1)
            crowded = pool.value_load(flag[0:1, 0:1], min_val=0, max_val=1)
            with pool.If(crowded == 1):
                pool_dense(pool)

        def pool_dense(pool):
            for e in range(NE):
                pool.wait_ge(S.eu, e + 1)
                pool.wait_ge(S.cB_ev, NE)
                if e >= 2:
                    if e % 2:
                        pool.wait_ge(S.used, down_chunk(e - 2) + 1)
                    else:
                        pool.wait_ge(S.d_mm, (e - 2) // 2 + 1)
                nc.gpsimd.tensor_tensor(hid[:, e % 2, :].rearrange("p (f t) -> p f t", f=2),
                                        eh_s[:, e % 2, :].rearrange("p (f t) -> p f t", f=2),
                                        cB[:, e:e + 1, :].broadcast_to([P, 2, NT]), ALU.mult).then_inc(S.hid, 1)


        def ring_slot(n):
            m = n - AT["experts"]
            if m < 0:
                return n % RING
            return RING if m % (RING + 1) == RING else (AT["experts"] + m % (RING + 1)) % RING

        slots = [ring_slot(n) for n in range(AT["end"])]

        def ring_at(n):
            return ring[:, slots[n], :] if slots[n] < RING else extra_slot

        def landed_wait(eng, n):
            eng.wait_ge(landed[slots[n]], 16 * slots[:n + 1].count(slots[n]))

        n_chunks = AT["end"]

        @block.sync
        def _(sp):
            sp.dma_start(X[:, :, :], IN["x"].rearrange("(t p) d -> p t d", p=P)).then_inc(S.in_x, 16)
            sp.dma_start(col[:, :], IN["cols"]).then_inc(S.in_col, 16)
            sp.dma_start(metaX, IN["meta"]).then_inc(S.in_meta, 16)
            for n in range(n_chunks):
                earlier = [m for m in range(n) if slots[m] == slots[n]]
                if earlier:
                    sp.wait_ge(S.used, earlier[-1] + 1)
                sp.dma_start(ring_at(n), IN["stream"][n]).then_inc(landed[slots[n]], 16)
            for t in range(T):
                sp.wait_ge(S.xn, 10 + t + 1)
                sp.dma_start(out[t * P:(t + 1) * P, :], X[:, t, :]).then_inc(S.out_done, 16)
            sp.wait_ge(S.out_done, 16 * T)

        @block.gpsimd
        def _(pool):
            chain = [0]

            def link(ins):
                chain[0] += 1
                ins.then_inc(S.pool, 1)
                pool.wait_ge(S.pool, chain[0])

            def rows(i, buf, sem):
                pool.dma_start(rowB[:, buf, :, :], IN["rows"][i].partition_broadcast(P)).then_inc(sem, 16)

            pool.dma_start(cst[:, :], IN["consts"]).then_inc(S.in_cst, 16)
            pool.dma_start(posi[:, :], IN["pos"]).then_inc(S.in_pos, 16)

            def affine(i, count):
                buf = i % 2
                pool.wait_ge((S.in_row0, S.in_row1)[buf], 16 * (i // 2 + 1))
                pool.wait_ge(S.xn_tr, count)
                g = rowB[:, buf, 0:1, :].broadcast_to([P, T, DM])
                b = rowB[:, buf, 1:2, :].broadcast_to([P, T, DM])
                link(nc.gpsimd.tensor_tensor(X[:, :, :], X[:, :, :], g, ALU.mult))
                nc.gpsimd.tensor_tensor(X[:, :, :], X[:, :, :], b, ALU.add).then_inc(S.affine, 1)

            pool.wait_ge(S.used, 5)
            rows(0, 0, S.in_row0)
            pool.dma_start(wuq[:, :, :], IN["w_uq"]).then_inc(S.in_uq, 16)
            pool.dma_start(wukv[:, :], IN["w_ukv"]).then_inc(S.in_ukv, 16)
            pool.dma_start(gnB[:, :, :], IN["gn"].partition_broadcast(P)).then_inc(S.in_gn, 16)
            pool.dma_start(wba[:, :, :], IN["w_ba"]).then_inc(S.in_ba, 16)
            pool.dma_start(sm2[:, 160:168], IN["dn_rows"].partition_broadcast(P)).then_inc(S.in_dn, 16)
            pool.dma_start(dnG, IN["dn_g"].partition_broadcast(P)).then_inc(S.in_dn, 16)
            rows(1, 1, S.in_row1)
            affine(0, 1)
            pool.wait_ge(S.affine, 1)
            rows(2, 0, S.in_row0)
            pool.wait_ge(S.in_gn, 16)
            pool.wait_ge(S.ro_n, 1)
            g = gnB[:, 0:1, :].broadcast_to([P, T, 512])
            b = gnB[:, 1:2, :].broadcast_to([P, T, 512])
            link(nc.gpsimd.tensor_tensor(ro[:, :, :], ro[:, :, :], g, ALU.mult))
            link(nc.gpsimd.tensor_tensor(ro[:, :, :], ro[:, :, :], b, ALU.add))
            pool.wait_ge(S.rg_s, 2)
            nc.gpsimd.tensor_tensor(ro[:, :, :], ro[:, :, :], rg[:, :, :], ALU.mult).then_inc(S.gated, 1)
            pool.wait_ge(S.gated, 1)
            affine(1, 2)
            pool.wait_ge(S.affine, 2)
            rows(3, 1, S.in_row1)
            for f in range(FT):
                pool.wait_ge(S.ff_rl, f + 1)
                if f >= 8:
                    pool.wait_ge(S.y2_mm, f - 7)
                nc.gpsimd.tensor_tensor(fTr[:, f % 8, :], frl[:, f % 4, :], frl[:, f % 4, :], ALU.mult)\
                    .then_inc(S.ff_sq, 1)
            affine(3, 3)
            pool_tail(pool, link, affine, rows)

        @block.tensor
        def _(pe):
            mm = nc.tensor.matmul

            def transposes(i):
                for t in range(T):
                    pe.wait_ge(S.xn, 2 * (i - 1) + t + 1)
                    for k in range(KD):
                        last = nc.tensor.transpose(
                            psum[:, k // 2, (k % 2) * NT + t * P:(k % 2) * NT + (t + 1) * P],
                            X[:, t, k * P:(k + 1) * P], C("ident"))
                last.then_inc(S.xn_tr, 1)

            def ada(c):
                n = ada_chunk(c)
                landed_wait(pe, n)
                if c:
                    pe.wait_ge(S.mod_ev, c)
                w = ring_at(n).rearrange("p (k m q j) -> p k q m j", k=KD, m=4, q=4)
                for k in range(KD):
                    for q in range(4):
                        last = mm(psum[32 * q:32 * q + 32, 7, 0:P].rearrange("p (m j) -> p m j", m=4),
                                  csil[:, k:k + 1].broadcast_to([P, 32]), w[:, k, q],
                                  start=(k == 0), stop=(k == KD - 1))
                last.then_inc(S.used, 1)

            pe.wait_ge(S.in_cst, 16)
            transposes(1)
            pe.wait_ge(S.meta_n, 1)
            for k in range(KD):
                last = nc.tensor.transpose(psum[:, 5, k * META:(k + 1) * META], metaX[:, k * P:(k + 1) * P],
                                           C("ident")[0:META, 0:META])
            last.then_inc(S.meta_tr, 1)
            pe.wait_ge(S.silu_c, 1)
            for c in range(4):
                ada(c)

            g = 0
            pe.wait_ge(S.hT, 2)
            pe.wait_ge(S.meta_h, 1)
            for c in range(4):
                n = AT["w_in"] + c
                landed_wait(pe, n)
                w = ring_at(n).rearrange("p (k n) -> p k n", k=KD)
                wd = 416 if c == 0 else 512
                for t in range(T):
                    if g >= 6:
                        pe.wait_ge(S.pj_ev_a if g % 2 else S.pj_ev_v, (g - 6) // 2 + 1)
                    for k in range(KD):
                        last = mm(psum[:, g % 6, 0:wd], hT[:, k, META + t * P:META + (t + 1) * P], w[:, k, 0:wd],
                                  start=(k == 0), stop=(k == KD - 1))
                    if t == 0:
                        last.then_inc(S.pj_mm, 1)
                    g += 1
                last.then_inc(S.used, 1)

            ada(4)
            pe.wait_ge(S.rot, 1)
            pe.wait_ge(S.pj_ev_a, 4)
            pe.wait_ge(S.pj_ev_v, 4)
            for a in range(4):
                for t in range(T):
                    last = nc.tensor.transpose(psum[:, a // 2, (a % 2) * NT + t * P:(a % 2) * NT + (t + 1) * P],
                                               rqk[:, t, a * P:(a + 1) * P], C("ident"))
            last.then_inc(S.rqk_tr, 1)
            ada(5)
            pe.wait_ge(S.rqkT, 2)
            for t in range(T):
                for h in range(RH):
                    r = slice(64 * (h % 2), 64 * (h % 2) + 64)
                    c = (2 * t + h // 2) * P
                    last = mm(psum[:, 2 + h % 2, c:c + P], rqT[r, 2 + h // 2, t * P:(t + 1) * P],
                              rqT[r, h // 2, t * P:(t + 1) * P], start=True, stop=True)
            last.then_inc(S.rs_mm, 1)
            pe.wait_ge(S.kz, 1)
            for h in range(RH):
                r = slice(64 * (h % 2), 64 * (h % 2) + 64)
                last = mm(psum[r, 4, (h // 2) * P:(h // 2 + 1) * P], rkz[:, h, :],
                          rv[:, 0, h * P:(h + 1) * P], start=True, stop=True)
            last.then_inc(S.kv_mm, 1)
            ada(6)
            pe.wait_ge(S.sT, 2)
            pe.wait_ge(S.rS, 1)
            pe.wait_ge(S.qx, 1)
            for par in range(2):
                r = slice(64 * par, 64 * par + 64)
                for t in range(T):
                    for a in range(2):
                        h = 2 * a + par
                        o = psum[:, 5 + par, (2 * t + a) * P:(2 * t + a + 1) * P]
                        last = mm(o, rsT[:, 4 * par + 2 * t + a, :], rv[:, t, h * P:(h + 1) * P],
                                  start=True, stop=(t == 0))
                        if t == 1:
                            last = mm(o, rqx[r, a, :], rSt[r, a, :], start=False, stop=True)
                last.then_inc(S.ro_mm, 1)
            ada(7)

            pe.wait_ge(S.qn, 1)
            for a in range(3):
                for t in range(T):
                    last = nc.tensor.transpose(psum[:, a // 2, (a % 2) * NT + t * P:(a % 2) * NT + (t + 1) * P],
                                               qcn[:, t, a * P:(a + 1) * P], C("ident"))
            last.then_inc(S.qn_tr, 1)
            pe.wait_ge(S.qnT, 1)
            pe.wait_ge(S.in_uq, 16)
            for i, (t, half) in enumerate(((0, 0), (0, 1), (1, 0), (1, 1))):
                bank = (2, 3, 4, 0)[i]
                for k in range(2):
                    last = mm(psum[:, bank, 0:384], qnT[:, k, t * P:(t + 1) * P],
                              wuq[:, k, half * 384:(half + 1) * 384], start=(k == 0), stop=(k == 1))
                last.then_inc(S.uq_mm, 1)
            pe.wait_ge(S.in_ukv, 16)
            pe.wait_ge(S.ro_n, 1)
            for i in range(4):
                if i >= 2:
                    pe.wait_ge(S.kn_ev, i - 1)
                if i == 1:
                    pe.wait_ge(S.mod_ev, 8)
                bank = (1, 7)[i % 2]
                for hh in range(2):
                    h = 2 * i + hh
                    last = mm(psum[0:64, bank, hh * NT:(hh + 1) * NT], wukv[:, h * 64:(h + 1) * 64], kvnT,
                              start=True, stop=True)
                last.then_inc(S.knope, 1)
            for t in range(T):
                last = mm(b_(5 + t), kvnT[:, t * P:(t + 1) * P], wukv[:, 512:1024], start=True, stop=True)
                last.then_inc(S.knope, 1)
            pe.wait_ge(S.kn_ev, 4)
            ada(8)
            pe.wait_ge(S.rot, 2)
            pe.wait_ge(S.kn_ev, 6)
            for h in range(9):
                for t in range(T):
                    last = nc.tensor.transpose(psum[0:QK, h // 2, (h % 2) * NT + t * P:(h % 2) * NT + (t + 1) * P],
                                               qnat4[:, t, h, :], C("ident"))
            last.then_inc(S.rot_tr, 1)
            ada(9)
            pe.wait_ge(S.rotT_v, 1)
            pe.wait_ge(S.rotT_a, 1)
            for h in range(MH):
                last = mm(psum[:, 5 + h // 4, (h % 4) * P:(h % 4 + 1) * P], qT[0:QK, h, 0:P], kT[0:QK, h, 0:P],
                          start=True, stop=True)
            last.then_inc(S.sc0, 1)
            for h in range(MH):
                last = mm(psum[:, h // 2, (h % 2) * NT:(h % 2 + 1) * NT], qT[0:QK, h, P:NT], kT[0:QK, h, :],
                          start=True, stop=True)
            last.then_inc(S.sc1, 1)
            ada(10)
            pe.wait_ge(S.sm0, 1)
            for h in range(MH):
                last = nc.tensor.transpose(psum[:, 4 + h // 4, (h % 4) * P:(h % 4 + 1) * P], S0[:, h, :], C("ident"))
            last.then_inc(S.p_tr, 1)
            ada(11)
            pe.wait_ge(S.sm1, 1)
            for k in range(2):
                for h in range(MH):
                    last = nc.tensor.transpose(psum[:, 2 * k + h // 4, (h % 4) * P:(h % 4 + 1) * P],
                                               Sb[:, h, k * P:(k + 1) * P], C("ident"))
            last.then_inc(S.p_tr, 1)
            pe.wait_ge(S.p_ev, 3)
            for h in range(MH):
                r = slice(64 * (h % 2), 64 * (h % 2) + 64)
                i = h // 2
                o = psum[r, (6, 4)[i // 2], (i % 2) * NT:(i % 2 + 1) * NT]
                mm(o[:, 0:P], vN[:, 0, h * 64:(h + 1) * 64], PT[:, 0, h, :], start=True, stop=True)
                mm(o[:, P:NT], vN[:, 0, h * 64:(h + 1) * 64], PT[:, 1, h, :], start=True, stop=False)
                last = mm(o[:, P:NT], vN[:, 1, h * 64:(h + 1) * 64], PT[:, 2, h, :], start=False, stop=True)
            last.then_inc(S.pv_mm, 1)
            pe.wait_ge(S.gated, 1)
            for a in range(4):
                for t in range(T):
                    last = nc.tensor.transpose(psum[:, a // 2, (a % 2) * NT + t * P:(a % 2) * NT + (t + 1) * P],
                                               ro[:, t, a * P:(a + 1) * P], C("ident"))
            last.then_inc(S.g_tr, 1)

            def gate_rows(i):
                pe.wait_ge(S.dg, i + 1)
                for half in range(2):
                    last = mm(b_(2 * i + half), C("ones"), (dgt, dgt2)[i][:, 4 * half:4 * half + 4, :],
                              start=True, stop=True)
                last.then_inc(S.gt_mm, 1)

            pe.wait_ge(S.g_ev, 1)
            gate_rows(0)
            gate_rows(1)
            pe.wait_ge(S.mix_ev, 1)
            pe.wait_ge(S.mod2, 1)
            for half in range(2):
                n = AT["w_out"] + half
                landed_wait(pe, n)
                w = ring_at(n).rearrange("p (k n) -> p k n", k=KD)
                for t in range(T):
                    for k in range(KD):
                        last = mm(b_(4 + 2 * t + half), mixT[:, k, t * P:(t + 1) * P], w[:, k, :],
                                  start=(k == 0), stop=(k == KD - 1))
                last.then_inc(S.used, 1)
            pe.wait_ge(S.gtB, 2)
            transposes(2)
            pe.wait_ge(S.hT, 4)

            def ff1(c):
                n = AT["ffn"] + (0 if c == 0 else 2 * c - 1)
                landed_wait(pe, n)
                w = ring_at(n).rearrange("p (k n) -> p k n", k=KD)
                for m in range(4):
                    f = 4 * c + m
                    if f >= 4:
                        pe.wait_ge(S.ff_rl, f - 3)
                    for k in range(KD):
                        last = mm(psum[:, f % 4, 0:NT], w[:, k, m * P:(m + 1) * P], hT[:, k, META:L2],
                                  start=(k == 0), stop=(k == KD - 1))
                    if m < 3:
                        last.then_inc(S.ff_mm, 1)
                last.then_inc(S.used, 1)

            def ff2(c):
                n = AT["ffn"] + (15 if c == 7 else 2 * c + 2)
                landed_wait(pe, n)
                w = ring_at(n).rearrange("p (m n) -> p m n", m=4)
                for m in range(4):
                    f = 4 * c + m
                    pe.wait_ge(S.ff_sq, f + 1)
                    for t in range(T):
                        for half in range(2):
                            last = mm(b_(4 + 2 * t + half), fTr[:, f % 8, t * P:(t + 1) * P],
                                      w[:, m, half * 512:(half + 1) * 512], start=(f == 0), stop=(f == FT - 1))
                    if m < 3:
                        last.then_inc(S.y2_mm, 1)
                last.then_inc(S.used, 1)

            ff1(0)
            for c in range(1, 8):
                ff1(c)
                ff2(c - 1)
            ff2(7)
            transposes(4)
            pe_second(pe, mm, transposes)

        @block.scalar
        def _(act):
            chain = [0]

            def link(ins):
                chain[0] += 1
                ins.then_inc(S.act, 1)
                act.wait_ge(S.act, chain[0])

            def ln_sqrt(i):
                for t in range(T):
                    act.wait_ge(S.ln_v, ln_count(i, t))
                    nc.scalar.activation(sd[:, t:t + 1], mv[:, t, 1:2], ACT.Sqrt, bias=epsc).then_inc(S.ln_s, 1)

            def act_hT(i, A1=A1, B1=B1):
                act.wait_ge(S.xn_tr, i)
                for k in (2, 3, 6, 7):
                    last = nc.scalar.activation(hT[:, k, META:L2], psum[:, k // 2, (k % 2) * NT:(k % 2 + 1) * NT],
                                                ACT.Identity, bias=B1[:, k:k + 1], scale=A1[:, k:k + 1])
                last.then_inc(S.hT, 1)

            act.wait_ge(S.in_col, 16)
            nc.scalar.activation(csil, V("c"), ACT.Silu).then_inc(S.silu_c, 1)
            ln_sqrt(1)
            act.wait_ge(S.meta_v, 1)
            nc.scalar.activation(sd[0:META, 0:1], mv[0:META, 0, 1:2], ACT.Sqrt, bias=epsc[0:META]).then_inc(S.meta_s, 1)
            act.wait_ge(S.trig_r, 1)
            nc.scalar.activation(trig[:, 0:2, :], trig[:, 2:4, :], ACT.Sin).then_inc(S.trig, 1)

            act.wait_ge(S.mod1, 1)
            act_hT(1)
            dst = [pj, rqk, rv, rg]
            for c in range(4):
                act.wait_ge(S.used, AT["w_in"] + c + 1)
                wd = 416 if c == 0 else 512
                if c < 3:
                    nc.scalar.copy(dst[c][:, 1, :], psum[:, (2 * c + 1) % 6, 0:wd]).then_inc(S.pj_ev_a, 1)
                else:
                    nc.scalar.activation(rg[:, 1, :], psum[:, 1, :], ACT.Silu).then_inc(S.pj_ev_a, 1)
            act.wait_ge(S.pj_ev_v, 4)
            nc.scalar.activation(rg[:, 0, :], rg[:, 0, :], ACT.Silu).then_inc(S.rg_s, 2)
            act.wait_ge(S.pj_ev_a, 1)
            for t in range(T):
                nc.scalar.activation(Sb[:, 2 * t, :], pj[:, t, 0:QR], ACT.Square, accum_out=ssq[:, t:t + 1])
                ins = nc.scalar.activation(Sb[:, 2 * t + 1, 0:KVR], pj[:, t, QR:QR + KVR], ACT.Square,
                                           accum_out=ssq[:, 2 + t:3 + t])
                link(ins)
            link(nc.scalar.activation(rq[:, 0:2], ssq[:, 0:2], ACT.Sqrt, bias=epsc, scale=1.0 / QR))
            nc.scalar.activation(rq[:, 2:4], ssq[:, 2:4], ACT.Sqrt, bias=epsc, scale=1.0 / KVR).then_inc(S.rms_sq, 1)
            act.wait_ge(S.rqk_tr, 1)
            nc.scalar.copy(rqT[:, 2:4, :], b_(1)).then_inc(S.rqkT, 1)
            act.wait_ge(S.kv_mm, 1)
            nc.scalar.copy(rSt[:, :, :], psum[:, 4, 0:256]).then_inc(S.rS, 1)
            act.wait_ge(S.ln_v, 3)
            nc.scalar.activation(gsd, gmv[:, :, 1], ACT.Sqrt, bias=epsc).then_inc(S.ln_s, 1)
            for i in range(4):
                act.wait_ge(S.knope, i + 1)
                nc.scalar.copy(kT[0:64, 2 * i:2 * i + 2, :], psum[0:64, (1, 7)[i % 2], :]).then_inc(S.kn_ev, 1)
            for t in range(T):
                act.wait_ge(S.knope, 5 + t)
                nc.scalar.copy(vN[:, t, :], b_(5 + t)).then_inc(S.kn_ev, 1)
            act.wait_ge(S.rot_tr, 1)
            nc.scalar.copy(kT[64:QK, :, :], psum[64:QK, 4:5, 0:NT].broadcast_to([32, MH, NT])).then_inc(S.rotT_a, 1)
            for t, (buf, w) in enumerate(((S0, P), (Sb, NT))):
                act.wait_ge(S.nm0 if t == 0 else S.nm1, 1)
                for h in range(MH):
                    last = nc.scalar.activation(buf[:, h, :], buf[:, h, :], ACT.Exp,
                                                bias=nmax[:, 8 * t + h:8 * t + h + 1],
                                                accum_out=rsum[:, 8 * t + h:8 * t + h + 1])
                last.then_inc(S.ex0 if t == 0 else S.ex1, 1)
            act.wait_ge(S.p_tr, 2)
            nc.scalar.copy(PT[:, 1, :, :], psum[:, 0:2, :].rearrange("p a b -> p (a b)")).then_inc(S.p_ev, 1)
            act.wait_ge(S.pv_mm, 1)
            nc.scalar.copy(mixT[:, 0:2, :], b_(6)).then_inc(S.mix_ev, 1)
            for i in range(2):
                act.wait_ge(S.gt_mm, i + 1)
                nc.scalar.copy(gtB[:, i, :], psum[:, 2 * i:2 * i + 2, :].rearrange("p a b -> p (a b)"))\
                    .then_inc(S.gtB, 1)
            ln_sqrt(2)
            act_hT(2)
            for f in range(FT):
                if f % 4 < 3:
                    act.wait_ge(S.ff_mm, 3 * (f // 4) + f % 4 + 1)
                else:
                    c = f // 4
                    act.wait_ge(S.used, AT["ffn"] + (0 if c == 0 else 2 * c - 1) + 1)
                if f >= 4:
                    act.wait_ge(S.ff_sq, f - 3)
                nc.scalar.activation(frl[:, f % 4, :], psum[:, f % 4, 0:NT], ACT.Relu).then_inc(S.ff_rl, 1)
            ln_sqrt(3)
            ln_sqrt(4)
            act_hT(3, V("ge"), V("be"))
            act_second(act, link, ln_sqrt, act_hT)

        @block.vector
        def _(dve):
            chain = [0]

            def link(ins):
                chain[0] += 1
                ins.then_inc(S.dve, 1)
                dve.wait_ge(S.dve, chain[0])

            v = nc.vector

            def moments(i, t):
                for n in range(2):
                    last = v.bn_stats(stat[:, t, n, :], X[:, t, n * 512:(n + 1) * 512])
                link(last)
                v.bn_aggr(mv[:, t, :], stat[:, t, :, :].rearrange("p n s -> p (n s)")).then_inc(S.ln_v, 1)

            def normalise(i, t, rows=None):
                dve.wait_ge(S.ln_s, ln_count(i, t))
                link(v.reciprocal(rstd[:, t:t + 1], sd[:, t:t + 1]))
                if rows is None:
                    v.tensor_scalar(X[:, t, :], X[:, t, :], mv[:, t, 0:1], rstd[:, t:t + 1],
                                    ALU.subtract, ALU.mult).then_inc(S.xn, 1)
                else:
                    link(v.scalar_tensor_tensor(X[:, t, :], X[:, t, :], mv[:, t, 0:1], rows[:, 0, :],
                                                ALU.subtract, ALU.mult))
                    v.scalar_tensor_tensor(X[:, t, :], X[:, t, :], rstd[:, t:t + 1], rows[:, 1, :],
                                           ALU.mult, ALU.add).then_inc(S.xn, 1)

            def to_hT(i, A1=A1, B1=B1):
                dve.wait_ge(S.xn_tr, i)
                for k in (0, 1, 4, 5):
                    last = v.tensor_scalar(hT[:, k, META:L2], psum[:, k // 2, (k % 2) * NT:(k % 2 + 1) * NT],
                                           A1[:, k:k + 1], B1[:, k:k + 1], ALU.mult, ALU.add)
                last.then_inc(S.hT, 1)

            link(v.memset(epsc, EPS))
            dve.wait_ge(S.in_x, 16)
            for t in range(T):
                moments(1, t)
            for t in range(T):
                normalise(1, t)
            dve.wait_ge(S.in_meta, 16)
            dve.wait_ge(S.xn, 2)
            for n in range(2):
                last = v.bn_stats(stat[0:META, 0, n, :], metaX[:, n * 512:(n + 1) * 512])
            link(last)
            v.bn_aggr(mv[0:META, 0, :], stat[0:META, 0, :, :].rearrange("p n s -> p (n s)")).then_inc(S.meta_v, 1)
            dve.wait_ge(S.meta_s, 1)
            link(v.reciprocal(rstd[0:META, 0:1], sd[0:META, 0:1]))
            v.tensor_scalar(metaX, metaX, mv[0:META, 0, 0:1], rstd[0:META, 0:1],
                            ALU.subtract, ALU.mult).then_inc(S.meta_n, 1)
            dve.wait_ge(S.in_pos, 16)
            dve.wait_ge(S.in_cst, 16)
            link(v.tensor_copy(posf, posi[:, :]))
            ang, kk, red = scr[:, 0:64], scr[:, 64:192].rearrange("p (a b) -> p a b", a=2), trig[:, 2:4, :]
            for t in range(T):
                last = v.tensor_scalar(ang[:, t * 32:(t + 1) * 32], C("inv"), posf[:, t:t + 1], None, ALU.mult)
            link(last)
            R = 12582912.0
            for a, turn in ((0, 0.25), (1, 0.0)):
                link(v.tensor_scalar(kk[:, a, :], ang, float(1.0 / (2 * np.pi)), turn, ALU.mult, ALU.add))
                link(v.tensor_scalar(kk[:, a, :], kk[:, a, :], R, None, ALU.add))
                link(v.tensor_scalar(kk[:, a, :], kk[:, a, :], R, None, ALU.subtract))
                c1 = 6.28125
                c2 = float((np.float32(2 * np.pi - c1).view(np.uint32) & np.uint32(0xFFFFF000)).view(np.float32))
                c3 = float(2 * np.pi - c1 - c2)
                link(v.scalar_tensor_tensor(red[:, a, :], kk[:, a, :], -c1, ang, ALU.mult, ALU.add))
                link(v.scalar_tensor_tensor(red[:, a, :], kk[:, a, :], -c2, red[:, a, :], ALU.mult, ALU.add))
                link(v.scalar_tensor_tensor(red[:, a, :], kk[:, a, :], -c3, red[:, a, :], ALU.mult, ALU.add))
                if a == 0:
                    link(v.tensor_scalar(red[:, a, :], red[:, a, :], float(np.pi / 2), None, ALU.add))
            pi = 3.1415925
            v.tensor_scalar(red, red, pi, -pi, ALU.min, ALU.max).then_inc(S.trig_r, 1)
            dve.wait_ge(S.in_col, 16)
            dve.wait_ge(S.meta_tr, 1)
            for k in range(KD):
                last = v.tensor_scalar(hT[:, k, 0:META], psum[:, 5, k * META:(k + 1) * META], V("ge", k, k + 1),
                                       V("be", k, k + 1), ALU.mult, ALU.add)
            last.then_inc(S.meta_h, 1)

            def take(c):
                dve.wait_ge(S.used, ada_chunk(c) + 1)
                link(v.tensor_tensor(diag, psum[:, 7, 0:P].rearrange("p (m j) -> p m j", m=4),
                                     C("eye32").unsqueeze(1).broadcast_to([P, 4, 32]), ALU.mult))
                last = v.tensor_reduce(modc[:, 4 * c:4 * c + 4], diag, AX, ALU.add)
                last.then_inc(S.mod_ev, 1)

            for c in range(4):
                take(c)
            dve.wait_ge(S.mod_ev, 4)
            link(v.tensor_tensor(modc[:, 0:16], modc[:, 0:16], V("b_ada", 0, 16), ALU.add))
            link(v.tensor_scalar(modc[:, 8:16], modc[:, 8:16], 1.0, None, ALU.add))
            link(v.tensor_tensor(A1, modc[:, 8:16], V("g0"), ALU.mult))
            link(v.tensor_tensor(B1, modc[:, 8:16], V("b0"), ALU.mult))
            v.tensor_tensor(B1, B1, modc[:, 0:8], ALU.add).then_inc(S.mod1, 1)
            dve.wait_ge(S.mod1, 1)
            to_hT(1)
            dst = [pj, rqk, rv, rg]
            for c in range(4):
                dve.wait_ge(S.pj_mm, c + 1)
                wd = 416 if c == 0 else 512
                v.tensor_copy(dst[c][:, 0, :], psum[:, (2 * c) % 6, 0:wd]).then_inc(S.pj_ev_v, 1)

            def rotary(x, heads, half, step, tmp_a, tmp_b):
                x1, x2 = x[:, :, :, 0:half], x[:, :, :, half:2 * half]
                for t in range(T):
                    cb = cosT[:, t:t + 1, 0:32:step].broadcast_to([P, heads, half])
                    sb_ = sinT[:, t:t + 1, 0:32:step].broadcast_to([P, heads, half])
                    a = tmp_a[:, 0:heads * half].rearrange("p (h d) -> p h d", d=half)
                    b = tmp_a[:, heads * half:2 * heads * half].rearrange("p (h d) -> p h d", d=half)
                    c = tmp_b[:, 0:heads * half].rearrange("p (h d) -> p h d", d=half)
                    d = tmp_b[:, heads * half:2 * heads * half].rearrange("p (h d) -> p h d", d=half)
                    v.tensor_tensor(a, x1[:, t], cb, ALU.mult)
                    v.tensor_tensor(b, x2[:, t], sb_, ALU.mult)
                    v.tensor_tensor(c, x2[:, t], cb, ALU.mult)
                    link(v.tensor_tensor(d, x1[:, t], sb_, ALU.mult))
                    v.tensor_tensor(x1[:, t], a, b, ALU.subtract)
                    last = v.tensor_tensor(x2[:, t], c, d, ALU.add)
                    if t == 0:
                        link(last)
                return last

            dve.wait_ge(S.trig, 1)
            dve.wait_ge(S.pj_ev_a, 2)
            dve.wait_ge(S.pj_ev_v, 2)
            tA, tB = rtmp[:, 0].rearrange("p t w -> p (t w)"), rtmp[:, 1].rearrange("p t w -> p (t w)")
            rotary(rqk[:, :, :].rearrange("p t (h d) -> p t h d", d=64), 8, 32, 1, tA, tB).then_inc(S.rot, 1)
            take(4)
            dve.wait_ge(S.rot, 1)
            v.tensor_tensor(rkz[:, :, :], rqk[:, 0, 256:512].rearrange("p (h d) -> p h d", d=64),
                            C("zeta").unsqueeze(2).broadcast_to([P, RH, RDK]), ALU.mult).then_inc(S.kz, 1)
            dve.wait_ge(S.rqk_tr, 1)
            v.tensor_copy(rqT[:, 0:2, :], b_(0).rearrange("p (a b) -> p a b", a=2)).then_inc(S.rqkT, 1)
            take(5)
            dve.wait_ge(S.rqkT, 2)
            v.tensor_tensor(rqx[:, :, :], rqT[:, 0:2, P:NT], C("xi").rearrange("p (a b) -> p a b", a=2),
                            ALU.mult).then_inc(S.qx, 1)
            dve.wait_ge(S.rs_mm, 1)
            for t in range(T):
                v.tensor_tensor(rsT[:, 4 * t:4 * t + 4, :].rearrange("p (t a) b -> p t (a b)", t=T),
                                b_(2 + t).rearrange("p (t w) -> p t w", t=T),
                                C("decay", 256 * t, 256 * t + 256).unsqueeze(1).broadcast_to([P, T, 256]),
                                ALU.mult).then_inc(S.sT, 1)
            take(6)
            dve.wait_ge(S.rms_sq, 1)
            link(v.reciprocal(rq, rq))
            for t in range(T):
                v.tensor_scalar(qcn[:, t, 0:QR], pj[:, t, 0:QR], rq[:, t:t + 1], None, ALU.mult)
                last = v.tensor_scalar(qcn[:, t, QR:384], pj[:, t, QR:384], rq[:, 2 + t:3 + t], None, ALU.mult)
            last.then_inc(S.qn, 1)
            for par in range(2):
                dve.wait_ge(S.ro_mm, par + 1)
                for n in range(4):
                    last = v.bn_stats(gst[:, 4 * par + n, :], psum[:, 5 + par, n * P:(n + 1) * P])
            link(last)
            for i in range(8):
                last = v.bn_aggr(gmv[:, i, :], gst[:, i, :])
            last.then_inc(S.ln_v, 1)
            dve.wait_ge(S.ln_s, 3)
            link(v.reciprocal(grs, gsd))
            for i in range(8):
                par, t, a = i // 4, i // 2 % 2, i % 2
                h = 2 * a + par
                last = v.tensor_scalar(ro[:, t, h * P:(h + 1) * P], psum[:, 5 + par, (i % 4) * P:(i % 4 + 1) * P],
                                       gmv[:, i, 0:1], grs[:, i:i + 1], ALU.subtract, ALU.mult)
            last.then_inc(S.ro_n, 1)
            take(7)
            dve.wait_ge(S.qn_tr, 1)
            for k in range(2):
                v.tensor_scalar(qnT[:, k, :], psum[:, 0, k * NT:(k + 1) * NT], V("qg", k, k + 1), None, ALU.mult)
            v.tensor_scalar(kvnT, psum[:, 1, 0:NT], V("kvg"), None, ALU.mult).then_inc(S.qnT, 1)
            link(v.memset(qnat4[:, :, 8, 0:64], 0.0))
            link(v.tensor_copy(qnat4[:, :, 8, 64:QK], pj[:, :, 384:416]))
            for i, (t, half) in enumerate(((0, 0), (0, 1), (1, 0), (1, 1))):
                bank = (2, 3, 4, 0)[i]
                dve.wait_ge(S.uq_mm, i + 1)
                last = v.tensor_copy(qnat4[:, t, 4 * half:4 * half + 4, :],
                                     psum[:, bank, 0:384].rearrange("p (h d) -> p h d", d=QK))
            link(last)
            rotary(qnat4[:, :, :, 64:QK], 9, 16, 2, tA, tB).then_inc(S.rot, 1)
            take(8)
            dve.wait_ge(S.rot_tr, 1)
            for i in range(4):
                last = v.tensor_copy(qT[0:QK, 2 * i:2 * i + 2, :],
                                     psum[0:QK, i, :].rearrange("p (a b) -> p a b", a=2))
            last.then_inc(S.rotT_v, 1)
            take(9)
            scale = QK ** -0.5
            mask = C("causal").unsqueeze(1).broadcast_to([P, 4, P])
            dve.wait_ge(S.sc0, 1)
            for a in range(2):
                last = v.scalar_tensor_tensor(S0[:, 4 * a:4 * a + 4, :], b_(5 + a).rearrange("p (h k) -> p h k", k=P),
                                              scale, mask, ALU.mult, ALU.add)
            link(last)
            link(v.tensor_reduce(nmax[:, 0:8], S0[:, :, :], AX, ALU.max))
            v.tensor_scalar(nmax[:, 0:8], nmax[:, 0:8], -1.0, None, ALU.mult).then_inc(S.nm0, 1)
            dve.wait_ge(S.sc1, 1)
            mask2 = C("causal").unsqueeze(1).broadcast_to([P, 2, P])
            for a in range(4):
                src = b_(a).rearrange("p (h k) -> p h k", k=NT)
                v.tensor_scalar(Sb[:, 2 * a:2 * a + 2, 0:P], src[:, :, 0:P], scale, None, ALU.mult)
                last = v.scalar_tensor_tensor(Sb[:, 2 * a:2 * a + 2, P:NT], src[:, :, P:NT], scale, mask2,
                                              ALU.mult, ALU.add)
            link(last)
            link(v.tensor_reduce(nmax[:, 8:16], Sb[:, :, :], AX, ALU.max))
            v.tensor_scalar(nmax[:, 8:16], nmax[:, 8:16], -1.0, None, ALU.mult).then_inc(S.nm1, 1)
            take(10)
            for t, (buf, w) in enumerate(((S0, P), (Sb, NT))):
                dve.wait_ge(S.ex0 if t == 0 else S.ex1, 1)
                link(v.reciprocal(rinv[:, 8 * t:8 * t + 8], rsum[:, 8 * t:8 * t + 8]))
                v.tensor_tensor(buf[:, :, :], buf[:, :, :],
                                rinv[:, 8 * t:8 * t + 8].unsqueeze(2).broadcast_to([P, MH, w]),
                                ALU.mult).then_inc(S.sm0 if t == 0 else S.sm1, 1)
            dve.wait_ge(S.p_tr, 1)
            v.tensor_copy(PT[:, 0, :, :], psum[:, 4:6, :].rearrange("p a (b c) -> p (a b) c", c=P)).then_inc(S.p_ev, 1)
            dve.wait_ge(S.p_tr, 2)
            v.tensor_copy(PT[:, 2, :, :], psum[:, 2:4, :].rearrange("p a (b c) -> p (a b) c", c=P)).then_inc(S.p_ev, 1)
            take(11)
            dve.wait_ge(S.pv_mm, 1)
            v.tensor_copy(mixT[:, 2:4, :], b_(4).rearrange("p (a b) -> p a b", a=2))
            dve.wait_ge(S.g_tr, 1)
            v.tensor_copy(mixT[:, 4:8, :], psum[:, 0:2, :].rearrange("p a (b c) -> p (a b) c", c=NT)).then_inc(S.g_ev, 1)
            dve.wait_ge(S.mod_ev, 12)
            v.tensor_tensor(modc[:, 16:48], modc[:, 16:48], V("b_ada", 16, 48), ALU.add).then_inc(S.mod2, 1)
            dve.wait_ge(S.mod2, 1)

            def gate_diag(first, dgt):
                for k in range(KD):
                    last = v.tensor_scalar(dgt[:, k, :], C("ident"), modc[:, first + k:first + k + 1], None, ALU.mult)
                last.then_inc(S.dg, 1)

            gate_diag(16, dgt)
            gate_diag(40, dgt2)
            link(v.tensor_scalar(modc[:, 32:40], modc[:, 32:40], 1.0, None, ALU.add))
            link(v.tensor_tensor(A1, modc[:, 32:40], V("g1"), ALU.mult))
            link(v.tensor_tensor(B1, modc[:, 32:40], V("b1"), ALU.mult))
            link(v.tensor_tensor(B1, B1, modc[:, 24:32], ALU.add))

            def residual(i, gate, affine_count):
                dve.wait_ge(S.affine, affine_count)
                for t in range(T):
                    for half in range(2):
                        f = slice(half * 512, (half + 1) * 512)
                        y = b_(4 + 2 * t + half)
                        if gate is not None:
                            link(v.tensor_tensor(Sb2[:, t, f], y, gtB[:, gate, f], ALU.mult))
                            y = Sb2[:, t, f]
                        last = v.scalar_tensor_tensor(X[:, t, f], X[:, t, f], ALPHA, y, ALU.mult, ALU.add)
                    link(last)
                    moments(i, t)

            Sb2 = arena(14000, T, DM)
            dve.wait_ge(S.used, AT["w_out"] + 2)
            dve.wait_ge(S.gtB, 2)
            residual(2, 0, 1)
            for t in range(T):
                normalise(2, t)
            to_hT(2)
            dve.wait_ge(S.used, AT["dn_qkv"])
            residual(3, 1, 2)
            dve.wait_ge(S.in_row0, 32)
            for t in range(T):
                normalise(3, t, rowB[:, 0])
                dve.wait_ge(S.xn, 4 + t + 1)
                moments(4, t)
            for t in range(T):
                normalise(4, t)
            to_hT(3, V("ge"), V("be"))
            dve_second(dve, v, link, residual, normalise, to_hT)



def lay_out(i):
    f = np.float32
    d = {"x": i["x"][0], "pos": np.ascontiguousarray(i["positions"][0].reshape(T, P).T)}
    stream = np.zeros((AT["end"], P, CH), f)

    def by_k(w):
        o = np.zeros((P, KD, 512), f)
        o[:, :, :w.shape[1]] = w.reshape(KD, P, -1).transpose(1, 0, 2)
        return o.reshape(P, CH)

    ada = i["w_ada"][0]
    for n in range(4):
        stream[AT["ada_h1"] + n] = by_k(ada[:, n * 512:(n + 1) * 512])
    for n in range(8):
        stream[AT["ada_rest"] + n] = by_k(ada[:, 2048 + n * 512:2048 + (n + 1) * 512])
    w = i["w_in"][0]
    for n, (a, b) in enumerate(((0, 416), (416, 928), (928, 1440), (1440, 1952))):
        stream[AT["w_in"] + n] = by_k(w[:, a:b])
    for n in range(2):
        stream[AT["w_out"] + n] = by_k(i["w_out"][0][:, n * 512:(n + 1) * 512])
        stream[AT["w_out2"] + n] = by_k(i["w_out_2"][0][:, n * 512:(n + 1) * 512])
    for c in range(8):
        stream[AT["ffn"] + (0 if c == 0 else 2 * c - 1)] = by_k(i["w_ff1"][0][:, c * 512:(c + 1) * 512])
        stream[AT["ffn"] + (15 if c == 7 else 2 * c + 2)] = \
            i["w_ff2"][0][c * 512:(c + 1) * 512].reshape(4, P, DM).transpose(1, 0, 2).reshape(P, CH)
    w = i["w_in_2"][0]
    for n in range(3):
        stream[AT["dn_qkv"] + n] = by_k(w[:, n * 512:(n + 1) * 512])
        stream[AT["sb_qkv"] + n] = by_k(w[:, 2056 + n * 512:2056 + (n + 1) * 512])
    stream[AT["dn_z"]] = by_k(w[:, 1536:2048])
    for n in range(4):
        stream[AT["gates"] + n] = by_k(w[:, 3592 + n * 512:3592 + (n + 1) * 512])
    for n, k in enumerate(("w_branch_dn_2", "w_branch_sb_2")):
        stream[AT["branch"] + n] = i[k][0].reshape(4, P, DM).transpose(1, 0, 2).reshape(P, CH)
    wg, wu, wd = (i[k][0].reshape(NE, a, b) for k, a, b in
                  (("expert_w_gate_2", DM, EF), ("expert_w_up_2", DM, EF), ("expert_w_down_2", EF, DM)))
    for e in range(NE):
        s = stream[gate_chunk(e)].reshape(P, KD, 2, EF)
        s[:, :, 0] = wg[e].reshape(KD, P, EF).transpose(1, 0, 2)
        s[:, :, 1] = wu[e].reshape(KD, P, EF).transpose(1, 0, 2)
        s = stream[down_chunk(e)].reshape(P, 2, 2, DM)
        s[:, e % 2] = wd[e].reshape(2, P, DM).transpose(1, 0, 2)
    d["stream"] = stream
    colsrc = dict(g0="ln_in_g", b0="ln_in_b", g1="ln1_g", b1="ln1_b", ge="ln_emb_g_2", be="ln_emb_b_2",
                  g3="ln1_g_2", b3="ln1_b_2", b_ada="b_ada", qg="mla_q_norm", kvg="mla_kv_norm",
                  b_gate="b_gate_2", c="c")
    cols = np.zeros((P, COLS["end"][0]), f)
    for name, (o, k) in COLS.items():
        if name == "end":
            continue
        if name == "conv":
            a = i["dn_conv_w_2"][0].reshape(4, 12, P).transpose(2, 1, 0).reshape(P, 48)
        else:
            a = i[colsrc[name]].reshape(k, P).T
        cols[:, o:o + k] = a
    d["cols"] = cols
    d["consts"] = const_array()
    d["rows"] = np.stack([np.stack([i[a].reshape(DM), i[b].reshape(DM)]) for a, b in
                          (("ln_in_g", "ln_in_b"), ("ln1_g", "ln1_b"), ("ln2_g", "ln2_b"),
                           ("ln_emb_g_2", "ln_emb_b_2"), ("ln1_g_2", "ln1_b_2"), ("ln2_g_2", "ln2_b_2"))])
    d["gn"] = np.stack([i["ret_gn_g"][0], i["ret_gn_b"][0]])
    d["w_uq"] = i["w_uq"][0].reshape(2, P, 768).transpose(1, 0, 2)
    ukv = i["w_ukv"][0].reshape(P, MH, 128)
    d["w_ba"] = i["w_in_2"][0][:, 2048:2056].reshape(KD, P, 8).transpose(1, 0, 2).reshape(P, 64)
    d["dn_rows"] = np.concatenate([i["dn_a_log_2"][0], i["dn_dt_bias_2"][0]])
    d["dn_g"] = i["dn_norm_g_2"][0]
    d["meta"] = i["meta_tokens_2"]
    d["router_w"] = np.concatenate([i["router_group_w_2"][0]] + [i["router_expert_w_2"][0][g] for g in range(4)], 1).reshape(KD, P, 36).transpose(1, 0, 2).reshape(P, 288)
    d["router_b"] = np.concatenate([i["router_group_b_2"][0], i["router_expert_b_2"][0].reshape(32)])
    d["w_ukv"] = np.concatenate([ukv[:, :, :64].reshape(P, 512), ukv[:, :, 64:].reshape(P, 512)], 1)
    return d


def kernel(**inputs):
    import concourse.bacc as bacc
    from concourse.bass_utils import run_bass_kernel_spmd

    nc = bacc.Bacc("TRN2", target_bir_lowering=False, num_devices=1)
    arrays, IN = {}, {}
    for name, a in lay_out({k: np.asarray(v) for k, v in inputs.items()}).items():
        a = np.ascontiguousarray(a)
        arrays["in_" + name] = a
        IN[name] = nc.dram_tensor("in_" + name, a.shape, mybir.dt.from_np(a.dtype), kind="ExternalInput").ap()
    out = nc.dram_tensor("out_dram", (NT, DM), F32, kind="ExternalOutput").ap()

    build(nc, IN, out)
    r = run_bass_kernel_spmd(nc, [arrays], core_ids=[0])
    return r.results[0]["out_dram"].reshape(1, NT, DM)
```
